# Optimizing a Trainium2 kernel written in Bass

```python
import math
import jax
import jax.numpy as jnp
from jax import lax
import numpy as np

D_MODEL = 1024
BATCH = 1
SEQ = 512
DEPTH = 1
DEC_BATCH = 8
DEC_SEQ = 8
PAST_LEN = 2048
PAGE_SIZE = 128

SSM_WIDTH = D_MODEL // 2
SSM_GROUP = 16
SSM_GROUPS = SSM_WIDTH // SSM_GROUP
SSM_STATE = 64
DT_MIN = 0.001
DT_MAX = 0.1
SWA_HEADS = 8
SWA_KV_HEADS = 2
SWA_REP = SWA_HEADS // SWA_KV_HEADS
SWA_HEAD_DIM = 64
SWA_WIDTH = SWA_HEADS * SWA_HEAD_DIM
SWA_KV_WIDTH = SWA_KV_HEADS * SWA_HEAD_DIM
WINDOW = 128
REL_BUCKETS = 32
REL_MAX_DIST = 128
MEM_TOKENS = 256
MEM_HEADS = 4
MEM_HEAD_DIM = 128
MEM_WIDTH = MEM_HEADS * MEM_HEAD_DIM
N_BRANCHES = 3
IN_SPLITS = (SSM_WIDTH, SWA_WIDTH, SWA_KV_WIDTH, SWA_KV_WIDTH, MEM_WIDTH)
IN_COLS = sum(IN_SPLITS) + N_BRANCHES * D_MODEL
N_EXPERT_GROUPS = 4
EXPERTS_PER_GROUP = 8
N_EXPERTS = N_EXPERT_GROUPS * EXPERTS_PER_GROUP
TOP_K_IN_GROUP = 2
D_EXPERT = D_MODEL // 4
EPS = 1e-6
NEG_INF = -1e30

kernel_name = 'hybrid_s5_swa_sink_memx_hmoe_step'

def rmsnorm(x, g):
    xf = x.astype(jnp.float32)
    xf = xf * lax.rsqrt(jnp.mean(xf * xf, axis=-1, keepdims=True) + EPS)
    return xf.astype(x.dtype) * g

def _ssm_combine(e1, e2):
    a1r, a1i, b1r, b1i = e1
    a2r, a2i, b2r, b2i = e2
    return (a2r * a1r - a2i * a1i,
            a2r * a1i + a2i * a1r,
            a2r * b1r - a2i * b1i + b2r,
            a2r * b1i + a2i * b1r + b2i)

def s5_scan(u, h0_re, h0_im, lp):
    f32 = jnp.float32
    bsz, t = u.shape[:2]
    uf = u.astype(f32).reshape(bsz, t, SSM_GROUPS, SSM_GROUP)
    lr = lp['lam_re'].astype(f32)
    li = lp['lam_im'].astype(f32)
    dt = jnp.exp(lp['log_dt'].astype(f32))[:, None]
    mag = jnp.exp(lr * dt)
    a_re = mag * jnp.cos(li * dt)
    a_im = mag * jnp.sin(li * dt)
    den = lr * lr + li * li
    f_re = ((a_re - 1.0) * lr + a_im * li) / den
    f_im = (a_im * lr - (a_re - 1.0) * li) / den
    br = lp['bm_re'].astype(f32)
    bi = lp['bm_im'].astype(f32)
    bb_re = f_re[..., None] * br - f_im[..., None] * bi
    bb_im = f_re[..., None] * bi + f_im[..., None] * br
    bu_re = jnp.einsum('btgh,gph->btgp', uf, bb_re)
    bu_im = jnp.einsum('btgh,gph->btgp', uf, bb_im)
    aa_re = jnp.broadcast_to(a_re, bu_re.shape)
    aa_im = jnp.broadcast_to(a_im, bu_im.shape)
    cum_a_re, cum_a_im, cum_b_re, cum_b_im = lax.associative_scan(
        _ssm_combine, (aa_re, aa_im, bu_re, bu_im), axis=1)
    h0r = h0_re.astype(f32)[:, None]
    h0i = h0_im.astype(f32)[:, None]
    h_re = cum_a_re * h0r - cum_a_im * h0i + cum_b_re
    h_im = cum_a_re * h0i + cum_a_im * h0r + cum_b_im
    y = (jnp.einsum('btgp,ghp->btgh', h_re, lp['cm_re'].astype(f32))
         - jnp.einsum('btgp,ghp->btgh', h_im, lp['cm_im'].astype(f32))
         + lp['d_skip'].astype(f32).reshape(SSM_GROUPS, SSM_GROUP) * uf)
    return y.reshape(bsz, t, SSM_WIDTH).astype(u.dtype), h_re[:, -1], h_im[:, -1]

def t5_bucket(dist):
    n = jnp.maximum(dist, 0)
    max_exact = REL_BUCKETS // 2
    nf = jnp.maximum(n, 1).astype(jnp.float32)
    large = max_exact + (jnp.log(nf / max_exact) / math.log(REL_MAX_DIST / max_exact)
                         * (REL_BUCKETS - max_exact)).astype(jnp.int32)
    large = jnp.minimum(large, REL_BUCKETS - 1)
    return jnp.where(n < max_exact, n, large)

def sink_band_attention(q, k, v, kmask, sinks, rel_table):
    f32 = jnp.float32
    tq = q.shape[-3]
    tk = k.shape[-3]
    qg = q.reshape(q.shape[:-2] + (SWA_KV_HEADS, SWA_REP, SWA_HEAD_DIM))
    s = jnp.einsum('...qgrd,...kgd->...grqk', qg, k).astype(f32) * (SWA_HEAD_DIM ** -0.5)
    dist = jnp.arange(tq)[:, None] + WINDOW - jnp.arange(tk)[None, :]
    bias = rel_table[t5_bucket(dist)].astype(f32)
    bias = jnp.moveaxis(bias, -1, 0).reshape(SWA_KV_HEADS, SWA_REP, tq, tk)
    valid = (dist >= 0) & (dist < WINDOW) & kmask
    s = jnp.where(valid, s + bias, NEG_INF)
    sink = sinks.astype(f32).reshape(SWA_KV_HEADS, SWA_REP, 1, 1)
    m = jnp.maximum(jnp.max(s, axis=-1, keepdims=True), sink)
    e = jnp.exp(s - m)
    p = e / (jnp.sum(e, axis=-1, keepdims=True) + jnp.exp(sink - m))
    o = jnp.einsum('...grqk,...kgd->...qgrd', p.astype(v.dtype), v)
    return o.reshape(o.shape[:-3] + (SWA_WIDTH,))

def swa_prompt(q, k, v, sinks, rel_table):
    b, t = q.shape[:2]
    nblk = t // WINDOW
    qb = q.reshape(b, nblk, WINDOW, SWA_HEADS, SWA_HEAD_DIM)
    pad = jnp.zeros((b, WINDOW, SWA_KV_HEADS, SWA_HEAD_DIM), k.dtype)
    kb = jnp.concatenate([pad, k], axis=1).reshape(b, nblk + 1, WINDOW, SWA_KV_HEADS, SWA_HEAD_DIM)
    vb = jnp.concatenate([pad, v], axis=1).reshape(b, nblk + 1, WINDOW, SWA_KV_HEADS, SWA_HEAD_DIM)
    kk = jnp.concatenate([kb[:, :-1], kb[:, 1:]], axis=2)
    vv = jnp.concatenate([vb[:, :-1], vb[:, 1:]], axis=2)
    kpos = jnp.arange(nblk)[:, None] * WINDOW + jnp.arange(2 * WINDOW)[None, :] - WINDOW
    kmask = (kpos >= 0)[:, None, None, None, :]
    o = sink_band_attention(qb, kk, vv, kmask, sinks, rel_table)
    return o.reshape(b, t, SWA_WIDTH)

def mem_project(mem, lp):
    b, n = mem.shape[:2]
    kv = rmsnorm(mem, lp['mem_norm_g']) @ lp['w_mem_kv']
    k, v = jnp.split(kv, 2, axis=-1)
    return (k.reshape(b, n, MEM_HEADS, MEM_HEAD_DIM), v.reshape(b, n, MEM_HEADS, MEM_HEAD_DIM))

def mem_attention(q, k, v):
    s = jnp.einsum('bqhd,bkhd->bhqk', q, k).astype(jnp.float32) * (MEM_HEAD_DIM ** -0.5)
    p = jax.nn.softmax(s, axis=-1).astype(v.dtype)
    o = jnp.einsum('bhqk,bkhd->bqhd', p, v)
    return o.reshape(o.shape[:2] + (MEM_WIDTH,))

def hier_moe(x, lp):
    f32 = jnp.float32
    shp = x.shape
    xt = x.reshape(-1, D_MODEL)
    g_logits = (xt @ lp['w_rg']).astype(f32) + lp['b_rg'].astype(f32)
    g_prob = jax.nn.softmax(g_logits, axis=-1)
    g_w, g_idx = lax.top_k(g_prob, 1)
    e_logits = ((xt @ lp['w_rexp']).astype(f32) + lp['b_rexp'].astype(f32)).reshape(
        -1, N_EXPERT_GROUPS, EXPERTS_PER_GROUP)
    e_in = jnp.einsum('ng,nge->ne', jax.nn.one_hot(g_idx[:, 0], N_EXPERT_GROUPS, dtype=f32), e_logits)
    e_prob = jax.nn.softmax(e_in, axis=-1)
    e_w, e_idx = lax.top_k(e_prob, TOP_K_IN_GROUP)
    w = e_w / jnp.sum(e_w, axis=-1, keepdims=True) * g_w
    expert_id = g_idx * EXPERTS_PER_GROUP + e_idx
    combine = jnp.einsum('nk,nke->ne', w, jax.nn.one_hot(expert_id, N_EXPERTS, dtype=f32)).astype(x.dtype)
    y = jnp.zeros_like(xt)
    for e in range(N_EXPERTS):
        h = jax.nn.silu(xt @ lp['w_e_gate'][e]) * (xt @ lp['w_e_up'][e])
        y = y + combine[:, e:e + 1] * (h @ lp['w_e_down'][e])
    return y.reshape(shp)

def trunk_layer(x, h0_re, h0_im, swa_k_past, swa_v_past, mem_k, mem_v, lp, rel_table):
    b, t = x.shape[:2]
    xn = rmsnorm(x, lp['norm1_g'])
    split_at = [int(i) for i in np.cumsum(IN_SPLITS)]
    u, q, k, v, qm, gates = jnp.split(xn @ lp['w_in'], split_at, axis=-1)
    y_ssm, h_re, h_im = s5_scan(u, h0_re, h0_im, lp)
    z = jax.nn.gelu(y_ssm)
    z = z * jax.nn.sigmoid(z @ lp['w_glu'] + lp['b_glu'])
    q = q.reshape(b, t, SWA_HEADS, SWA_HEAD_DIM)
    k = k.reshape(b, t, SWA_KV_HEADS, SWA_HEAD_DIM)
    v = v.reshape(b, t, SWA_KV_HEADS, SWA_HEAD_DIM)
    if swa_k_past is None:
        o_swa = swa_prompt(q, k, v, lp['sinks'], rel_table)
        k_buf, v_buf = k[:, -WINDOW:], v[:, -WINDOW:]
    else:
        kk = jnp.concatenate([swa_k_past.astype(k.dtype), k], axis=1)
        vv = jnp.concatenate([swa_v_past.astype(v.dtype), v], axis=1)
        o_swa = sink_band_attention(q, kk, vv, True, lp['sinks'], rel_table)
        k_buf, v_buf = kk[:, -WINDOW:], vv[:, -WINDOW:]
    o_mem = mem_attention(qm.reshape(b, t, MEM_HEADS, MEM_HEAD_DIM), mem_k.astype(qm.dtype), mem_v.astype(qm.dtype))
    g = jax.nn.sigmoid(gates.reshape(b, t, N_BRANCHES, D_MODEL))
    merged = (g[:, :, 0] * (z @ lp['w_br_ssm'])
              + g[:, :, 1] * (o_swa @ lp['w_br_swa'])
              + g[:, :, 2] * (o_mem @ lp['w_br_mem']))
    x = x + merged @ lp['w_out']
    x = x + hier_moe(rmsnorm(x, lp['norm2_g']), lp)
    return x, h_re, h_im, k_buf, v_buf

def setup_inputs(seed: int = 0) -> dict:
    key = jax.random.key(seed)
    ks = jax.random.split(key, 38)
    f32 = jnp.float32

    def nrm(i, shape, scale=1.0):
        return jax.random.normal(ks[i], shape, f32) * scale

    n_idx = jnp.arange(SSM_STATE, dtype=f32)
    return {
        'x_prompt': nrm(0, (BATCH, SEQ, D_MODEL)),
        'x_sample': nrm(1, (DEC_BATCH, DEC_SEQ, D_MODEL)),
        'cache_swa_k': nrm(2, (DEPTH, DEC_BATCH, WINDOW, SWA_KV_HEADS, SWA_HEAD_DIM)),
        'cache_swa_v': nrm(3, (DEPTH, DEC_BATCH, WINDOW, SWA_KV_HEADS, SWA_HEAD_DIM)),
        'state_ssm_re': nrm(4, (DEPTH, DEC_BATCH, SSM_GROUPS, SSM_STATE), 0.3),
        'state_ssm_im': nrm(5, (DEPTH, DEC_BATCH, SSM_GROUPS, SSM_STATE), 0.3),
        'cache_mem_k': nrm(6, (DEPTH, DEC_BATCH, MEM_TOKENS, MEM_HEADS, MEM_HEAD_DIM)),
        'cache_mem_v': nrm(7, (DEPTH, DEC_BATCH, MEM_TOKENS, MEM_HEADS, MEM_HEAD_DIM)),
        'mem_prompt': nrm(8, (BATCH, MEM_TOKENS, D_MODEL)),
        'norm1_g': 1.0 + nrm(9, (DEPTH, D_MODEL), 0.01),
        'w_in': nrm(10, (DEPTH, D_MODEL, IN_COLS), D_MODEL ** -0.5),
        'lam_re': -0.5 + nrm(11, (DEPTH, SSM_GROUPS, SSM_STATE), 0.01),
        'lam_im': math.pi * n_idx + nrm(12, (DEPTH, SSM_GROUPS, SSM_STATE), 0.01),
        'log_dt': jax.random.uniform(ks[13], (DEPTH, SSM_GROUPS), f32, math.log(DT_MIN), math.log(DT_MAX)),
        'bm_re': nrm(14, (DEPTH, SSM_GROUPS, SSM_STATE, SSM_GROUP), (2 * SSM_GROUP) ** -0.5),
        'bm_im': nrm(15, (DEPTH, SSM_GROUPS, SSM_STATE, SSM_GROUP), (2 * SSM_GROUP) ** -0.5),
        'cm_re': nrm(16, (DEPTH, SSM_GROUPS, SSM_GROUP, SSM_STATE), (2 * SSM_STATE) ** -0.5),
        'cm_im': nrm(17, (DEPTH, SSM_GROUPS, SSM_GROUP, SSM_STATE), (2 * SSM_STATE) ** -0.5),
        'd_skip': nrm(18, (DEPTH, SSM_WIDTH)),
        'w_glu': nrm(19, (DEPTH, SSM_WIDTH, SSM_WIDTH), SSM_WIDTH ** -0.5),
        'b_glu': nrm(20, (DEPTH, SSM_WIDTH), 0.01),
        'sinks': nrm(21, (DEPTH, SWA_HEADS), 0.5),
        'rel_table': nrm(22, (REL_BUCKETS, SWA_HEADS), 0.1),
        'mem_norm_g': 1.0 + nrm(23, (DEPTH, D_MODEL), 0.01),
        'w_mem_kv': nrm(24, (DEPTH, D_MODEL, 2 * MEM_WIDTH), D_MODEL ** -0.5),
        'w_br_ssm': nrm(25, (DEPTH, SSM_WIDTH, D_MODEL), SSM_WIDTH ** -0.5),
        'w_br_swa': nrm(26, (DEPTH, SWA_WIDTH, D_MODEL), SWA_WIDTH ** -0.5),
        'w_br_mem': nrm(27, (DEPTH, MEM_WIDTH, D_MODEL), MEM_WIDTH ** -0.5),
        'w_out': nrm(28, (DEPTH, D_MODEL, D_MODEL), 0.5 * D_MODEL ** -0.5),
        'norm2_g': 1.0 + nrm(29, (DEPTH, D_MODEL), 0.01),
        'w_rg': nrm(30, (DEPTH, D_MODEL, N_EXPERT_GROUPS), D_MODEL ** -0.5),
        'b_rg': nrm(31, (DEPTH, N_EXPERT_GROUPS), 0.01),
        'w_rexp': nrm(32, (DEPTH, D_MODEL, N_EXPERTS), D_MODEL ** -0.5),
        'b_rexp': nrm(33, (DEPTH, N_EXPERTS), 0.01),
        'w_e_gate': nrm(34, (DEPTH, N_EXPERTS, D_MODEL, D_EXPERT), D_MODEL ** -0.5),
        'w_e_up': nrm(35, (DEPTH, N_EXPERTS, D_MODEL, D_EXPERT), D_MODEL ** -0.5),
        'w_e_down': nrm(36, (DEPTH, N_EXPERTS, D_EXPERT, D_MODEL), D_EXPERT ** -0.5),
        'final_norm_g': 1.0 + nrm(37, (D_MODEL,), 0.01),
    }

def reference(x_prompt, x_sample, cache_swa_k, cache_swa_v, state_ssm_re, state_ssm_im,
              cache_mem_k, cache_mem_v, mem_prompt,
              norm1_g, w_in, lam_re, lam_im, log_dt, bm_re, bm_im, cm_re, cm_im, d_skip,
              w_glu, b_glu, sinks, rel_table, mem_norm_g, w_mem_kv, w_br_ssm, w_br_swa, w_br_mem,
              w_out, norm2_g, w_rg, b_rg, w_rexp, b_rexp, w_e_gate, w_e_up, w_e_down, final_norm_g):
    layer_params = {
        'norm1_g': norm1_g, 'w_in': w_in, 'lam_re': lam_re, 'lam_im': lam_im, 'log_dt': log_dt,
        'bm_re': bm_re, 'bm_im': bm_im, 'cm_re': cm_re, 'cm_im': cm_im, 'd_skip': d_skip,
        'w_glu': w_glu, 'b_glu': b_glu, 'sinks': sinks, 'mem_norm_g': mem_norm_g, 'w_mem_kv': w_mem_kv,
        'w_br_ssm': w_br_ssm, 'w_br_swa': w_br_swa, 'w_br_mem': w_br_mem, 'w_out': w_out,
        'norm2_g': norm2_g, 'w_rg': w_rg, 'b_rg': b_rg, 'w_rexp': w_rexp, 'b_rexp': b_rexp,
        'w_e_gate': w_e_gate, 'w_e_up': w_e_up, 'w_e_down': w_e_down,
    }
    xp, xs = x_prompt, x_sample
    zero_state = jnp.zeros((x_prompt.shape[0], SSM_GROUPS, SSM_STATE), jnp.float32)
    pk, pv, pre, pim, pmk, pmv = [], [], [], [], [], []
    sk, sv, sre, sim = [], [], [], []
    for l in range(DEPTH):
        lp = {name: arr[l] for name, arr in layer_params.items()}
        mk, mv = mem_project(mem_prompt, lp)
        xp, hr, hi, kb, vb = trunk_layer(xp, zero_state, zero_state, None, None, mk, mv, lp, rel_table)
        xs, hrs, his, kbs, vbs = trunk_layer(xs, state_ssm_re[l], state_ssm_im[l], cache_swa_k[l], cache_swa_v[l],
                                             cache_mem_k[l], cache_mem_v[l], lp, rel_table)
        pk.append(kb); pv.append(vb)
        pre.append(hr.astype(x_prompt.dtype)); pim.append(hi.astype(x_prompt.dtype))
        pmk.append(mk); pmv.append(mv)
        sk.append(kbs.astype(cache_swa_k.dtype)); sv.append(vbs.astype(cache_swa_v.dtype))
        sre.append(hrs.astype(state_ssm_re.dtype)); sim.append(his.astype(state_ssm_im.dtype))
    y_prompt = rmsnorm(xp, final_norm_g)
    y_sample = rmsnorm(xs, final_norm_g)
    new_swa_k_prompt = jnp.stack(pk, axis=0)
    new_swa_v_prompt = jnp.stack(pv, axis=0)
    new_ssm_re_prompt = jnp.stack(pre, axis=0)
    new_ssm_im_prompt = jnp.stack(pim, axis=0)
    new_mem_k_prompt = jnp.stack(pmk, axis=0)
    new_mem_v_prompt = jnp.stack(pmv, axis=0)
    new_swa_k_sample = jnp.stack(sk, axis=0)
    new_swa_v_sample = jnp.stack(sv, axis=0)
    new_ssm_re_sample = jnp.stack(sre, axis=0)
    new_ssm_im_sample = jnp.stack(sim, axis=0)
    return (y_prompt, y_sample,
            new_swa_k_prompt, new_swa_v_prompt, new_ssm_re_prompt, new_ssm_im_prompt,
            new_mem_k_prompt, new_mem_v_prompt,
            new_swa_k_sample, new_swa_v_sample, new_ssm_re_sample, new_ssm_im_sample)


_drawn_inputs = setup_inputs


def setup_inputs(seed=0):
    import zlib

    import numpy as np

    out = dict(_drawn_inputs(seed))
    spreads = {}
    factors = {'norm1_g': 5.586,
     'lam_re': 18.287,
     'b_glu': 50.408,
     'sinks': 64.0,
     'rel_table': 3.174,
     'mem_norm_g': 5.826,
     'final_norm_g': 29.466,
     'cm_im': 2.885,
     'norm2_g': 8.0,
     'b_rg': 8.0,
     'b_rexp': 8.0}
    for name, (base, spread) in spreads.items():
        noise = np.random.default_rng([zlib.crc32(name.encode()), seed]).standard_normal(out[name].shape)
        drawn = base * np.exp(spread * noise) if base else spread * noise
        out[name] = jnp.asarray(drawn.astype(out[name].dtype))
    for name, factor in factors.items():
        out[name] = (out[name] * factor).astype(out[name].dtype)
    return out
```

```python
from contextlib import ExitStack

import concourse.bass as bass
from concourse import mybir

F32 = mybir.dt.float32
U32 = mybir.dt.uint32
I32 = mybir.dt.int32
ALU = mybir.AluOpType
ACT = mybir.ActivationFunctionType
AX = mybir.AxisListType.X

P = 128
D = 1024
KT = D // P
NP_, NB, NQ = 512, 8, 8
T = NP_ + NB * NQ
TT = 5
ROWS = [128, 128, 128, 128, 64]
TH = T // 2
G, CH, ST = 32, 16, 64
L = 8
NC = T // L
PC = NP_ // L
MEM, MH = 256, 4
MEM_SCALE = float(128) ** -0.5
SWA_SCALE = 0.125
NE, DE = 32, 256
PAIRS = 2 * T
OVER = 8
BLK = NE + OVER
NOROW = 4096
WB = 2048
NBLOCKS = 36
RING = 4
EPS = 1e-6
TWO_PI_A, TWO_PI_B, TWO_PI_C = 6.28125, 0.0019354820251464844, -1.7484555314695172e-07
MAGIC = 12582912.0

O_W = 0
O_X = 8192
O_TH = 12800
O_Z = 17408
O_O = 19712
O_H = O_Z
O_Q = 24320
O_UG = 26624
O_KT = 28928
O_KV = 29504
O_RS = 30784
O_ID = 31360
O_ONE = 31488
O_SM = 31616
O_PW = 32640
O_A = 34368
WORDS = 53136

S_LR, S_LI, S_LD, S_G1, S_GM, S_BG, S_DS, S_SK, S_SS = 0, 32, 64, 96, 104, 112, 116, 148, 156
N_SMALL = 158
S_T = 160
S_A8 = 640
S_SC = 768
S_ST = 896

A_VT, A_Y, A_UC, A_TAIL = O_A, O_A + 4096, O_A + 8704, O_A + 12800
A_US = A_TAIL
A_KS = A_TAIL + 2560
A_S = A_TAIL
SLOTS = PC + NB + 1 + NB
A_ZERO = A_TAIL + 5184
A_UP = A_TAIL
A_MK, A_MV = O_A, O_A + 2048
A_MKV, A_KMT, A_SB, A_SKT = O_A + 4096, O_A + 6144, O_A + 7168, O_A + 7440
A_SC, A_PT, A_BI, A_SV, A_SVN, A_QZ = O_A + 8528, O_A + 10576, O_A + 12624, O_A + 14672, O_A + 15696, O_A + 16720
A_THG = O_A + 8704
O_QZS = O_PW
O_T1, O_T2, O_M = O_PW, O_PW + 576, O_PW + 1152
A_WG = O_A

M_X2 = O_X
M_X2T = O_X + 2048
M_G2, M_GF, M_WR, M_BR = O_TH, O_TH + 1024, O_TH + 2048, O_TH + 2336
M_R = O_TH + 2372
M_XG, M_XGT = 22528, 24576
M_THE, M_HID, M_HT, M_YO = 26624, 27136, 27648, 28160
M_IDX = 30208
M_JUNK = O_PW
A_GL = A_TAIL
C_TRI, C_IOTA, C_PF, C_NOROW, N_CONST = 128, 256, 288, 298, 338
_at = [M_R]


def _take(n):
    _at[0] += n
    return _at[0] - n


R_TRI, R_IOTA, R_PF, R_NOROW = _take(128), _take(32), _take(10), _take(BLK)
R_LG, R_GP, R_GM, R_IX = _take(36 * TT), _take(8 * TT), _take(8 * TT), _take(8 * TT)
R_GX, R_GE, R_OG, R_EP, R_EM, R_ED = _take(TT), _take(4 * TT), _take(4 * TT), _take(8 * TT), _take(8 * TT), _take(TT)
R_EK, R_MK, R_M, R_TM, R_TM2 = _take(2 * TT), _take(64 * TT), _take(32 * TT), _take(64 * TT), _take(256)
R_RK, R_NB, R_RA, R_OB, R_FL, R_OV = _take(192), _take(96), _take(10), _take(10), _take(10), _take(10)
R_SL, R_PI, R_W0, R_W1, R_SS = _take(10), _take(10), _take(TT), _take(TT), _take(16)
assert _at[0] <= O_Z


def plan_jobs():
    jobs = ["ssq"] + [f"u{t}" for t in range(TT)] + [f"kv{t}" for t in range(TT)] + ["kT"]
    jobs += [f"q{m}" for m in range(4)] + [f"K{i}" for i in range(8)]
    jobs += [f"VT{i}" for i in range(4)] + [f"U{i}" for i in range(4)] + [f"B{i}" for i in range(4)]
    jobs += [f"g0{d}" for d in range(8)] + [f"Y{i}" for i in range(4)] + [f"qm{m}" for m in range(4)]
    jobs += [f"Z{i}" for i in range(4)] + ["ssqm"] + [f"mm{i}" for i in range(4)] + ["kmT"]
    jobs += [f"G{m}" for m in range(4)]
    n = len(UNITS)
    jobs += ["S0"]
    for i in range(n + 1):
        jobs += [f"S{i + 1}"] if i + 1 < n else []
        jobs += [f"O{i - 1}"] if i >= 1 else []
        jobs += [f"T{i}"] if i < n else []
    for d in range(8):
        jobs += [f"{k}{d}" for k in ("ga", "gb", "pa", "pb", "pc")]
    jobs += [f"w{b}{t}" for b in range(4) for t in range(TT)]
    jobs += [j for t in range(TT) for j in (f"x2T{t}", f"lg{t}")] + ["rk"]
    return {j: i for i, j in enumerate(jobs)}


UNITS = [("w", qt, kv) for qt in range(4) for kv in range(2)]
UNITS += [("m", qt, 0) for qt in range(4)] + [("ws", 0, 0), ("ms", 0, 0), ("ms", 1, 0)]
J = plan_jobs()


def build(nc, small, ssm, h0, xT, x, memT, wstream, wexp, bias, sbias, skT, sv, mkT, mv, cache_k, cache_v,
          const, rows, wr, out_y, out_kvp, out_mem, out_sk, out_sv, out_ssm):
    u_d = nc.dram_tensor("u_rows", [T, 512], F32)
    k_d = nc.dram_tensor("k_pad", [G, CH, 240], F32)
    kvs_d = nc.dram_tensor("kv_sample", [64, 256], F32)
    x2_d = nc.dram_tensor("xn2_rows", [T, D], F32)
    y_d = nc.dram_tensor("expert_rows", [PAIRS, D], F32)
    tab_d = nc.dram_tensor("pair_table", [P * BLK, 1], U32)

    with ExitStack() as ctx:
        def sem(name):
            return ctx.enter_context(nc.semaphore(name))

        sb = ctx.enter_context(nc.sbuf_tensor("sb", [P, WORDS], F32))
        ps = [ctx.enter_context(nc.psum_tensor(f"ps{i}", [P, 1024], F32)) for i in range(4)]

        def at(off, *dims, p0=0, pn=P):
            return bass.AP(sb, p0 * WORDS + off, [[WORDS, pn]] + [[s, n] for s, n in dims])

        def pat(i, off, *dims, p0=0, pn=P):
            return bass.AP(ps[i], p0 * 1024 + off, [[1024, pn]] + [[s, n] for s, n in dims])

        ident = at(O_ID, (1, 128))

        ps_ready = sem("ps_ready")
        ps_free = [sem(f"ps_free{i}") for i in range(4)]
        vec_step, act_step, pool_step = sem("vec_step"), sem("act_step"), sem("pool_step")
        w_ready = [sem(f"w_ready{i}") for i in range(RING)]
        w_used = sem("w_used")
        ld = {n: sem("ld_" + n) for n in ("small", "ssm", "xT", "const", "h0", "memT", "bias", "samp", "svn", "uc", "T",
                                          "x", "rows", "wr", "tab", "tb")}
        x_sq, ones_set, xn_ready = sem("x_sq"), sem("ones_set"), sem("xn_ready")
        u_sb, kv_sb, kT_sb, q_sb = sem("u_sb"), sem("kv_sb"), sem("kT_sb"), sem("q_sb")
        u_out, kvs_out, kz_out = sem("u_out"), sem("kvs_out"), sem("kz_out")
        exp_ssm, trig, ang_ready, par_ready = sem("exp_ssm"), sem("trig"), sem("ang_ready"), sem("par_ready")
        zero_set, y_built, vt_built = sem("zero_set"), sem("y_built"), sem("vt_built")
        ks_sb, vt_sb, ug_sb, b_sb = sem("ks_sb"), sem("vt_sb"), sem("ug_sb"), sem("b_sb")
        scan, scanned = sem("scan"), sem("scanned")
        yc_sb, gelu_in, gelu_th, zc_ready, z_sb = sem("yc_sb"), sem("gelu_in"), sem("gelu_th"), sem("zc_ready"), sem("z_sb")
        qm_sb, memn, memsq, mkv_sb, kmT_sb, thg_sb, zz_ready = (sem(n) for n in (
            "qm_sb", "memn", "memsq", "mkv_sb", "kmT_sb", "thg_sb", "zz_ready"))
        qz_ready, qzs_ready = sem("qz_ready"), sem("qzs_ready")
        stat_ready, exp_ready, p_ready, pt_ready, o_sb = (sem(n) for n in (
            "stat_ready", "exp_ready", "p_ready", "pt_ready", "o_sb"))
        ldmk, ldmv = [sem("ldmk0"), sem("ldmk1")], [sem("ldmv0"), sem("ldmv1")]
        ga_sb, gb_sb, m_ready, h_ready = sem("ga_sb"), sem("gb_sb"), sem("m_ready"), sem("h_ready")
        ss2, x2_ready, x2T_sb, lg_sb, gate_d, gate_e, m_onehot, rk_sb, slot_ready, tab_set, idx_ready = (
            sem(n) for n in ("ss2", "x2_ready", "x2T_sb", "lg_sb", "gate_d", "gate_e", "m_onehot", "rk_sb",
                             "slot_ready", "tab_set", "idx_ready"))
        xg_clear = sem("xg_clear")
        scat = sem("scat")
        mk_used, mv_used, t_ready, svn_ready, up_sb, ms_ready, root_ready = sem("mk_used"), sem("mv_used"), sem("t_ready"), sem("svn_ready"), sem("up_sb"), sem("ms_ready"), sem("root_ready")
        k_out = [sem(f"k_out{i}") for i in range(4)]
        x2_out = [sem(f"x2_out{i}") for i in range(2)]
        y_ld = [sem(f"y_ld{i}") for i in range(TT)]
        wg_ready = [sem(f"wg_ready{i}") for i in range(4)]
        wd_ready = [sem(f"wd_ready{i}") for i in range(4)]
        xg_ready = [sem(f"xg_ready{i}") for i in range(2)]
        y_sent = [sem(f"y_sent{i}") for i in range(2)]
        xt_ps, xgT_ready, gu_ps, th_ready, hid_ready, hT_ps, hT_ready, y_ps, y_copied = (
            sem(n) for n in ("xt_ps", "xgT_ready", "gu_ps", "th_ready", "hid_ready", "hT_ps", "hT_ready", "y_ps", "y_copied"))
        ssf, y_done = sem("ssf"), sem("y_done")
        out_st = sem("out_st")
        block = ctx.enter_context(nc.Block())

        def pair(job):
            return J[job] % 4

        def filled(eng, job):
            eng.wait_ge(ps_ready, J[job] + 1)

        def free_count(job):
            return J[job] // 4 + 1

        def wait_pos(eng, sem_, r, k, d):
            if not isinstance(r, int) or 4 * r + k + d > 0:
                eng.wait_ge(sem_, r * 4 + (k + d))

        def overflow(eng):
            eng.wait_ge(idx_ready, 1)
            return eng.value_load(at(M_IDX + 256 + OVER, (1, 1), pn=1).bitcast(I32), min_val=0, max_val=OVER)

        class Chain:

            def __init__(self, eng, step):
                self.eng, self.step, self.count, self.last = eng, step, {}, None

            def do(self, ins, to=None, value=None):
                to = self.step if to is None else to
                ins.then_inc(to, 1)
                self.count[id(to)] = self.count.get(id(to), 0) + 1
                self.last = (to, self.count[id(to)] if value is None else value)

            def free(self, ins, job):
                self.do(ins, ps_free[pair(job)], free_count(job))

            def settle(self):
                self.eng.wait_ge(*self.last)

        @block.sync
        def _(sp):
            for s in range(RING):
                sp.dma_start(at(O_W + s * WB, (1, WB)), wstream[s]).then_inc(w_ready[s], 16)
            with sp.Fori(1, NBLOCKS // RING) as r:
                for s in range(RING):
                    sp.wait_ge(w_used, r * RING + (s + 1 - RING))
                    sp.dma_start(at(O_W + s * WB, (1, WB)), wstream[r * RING + s]).then_inc(w_ready[s], 16)

            def gate_up(e, s):
                sp.dma_start(at(A_WG + s * 4096, (1, 4096)), wexp[e, :, 0:4096]).then_inc(wg_ready[s], 16)

            def down(e, s):
                sp.dma_start(at(O_W + s * WB, (1, WB)), wexp[e, :, 4096:6144]).then_inc(wd_ready[s], 16)

            filled(sp, f"O{len(UNITS) - 1}")
            sp.wait_ge(out_st, 16 * 7)
            sp.wait_ge(o_sb, len(UNITS))
            for s in range(4):
                gate_up(s, s)
            sp.wait_ge(w_used, NBLOCKS)
            for s in range(4):
                down(s, s)
            with sp.Fori(1, NE // 4) as r:
                for s in range(4):
                    sp.wait_ge(gu_ps, r * 4 + (s - 3))
                    gate_up(r * 4 + s, s)
                    sp.wait_ge(y_ps, r * 4 + (s - 3))
                    down(r * 4 + s, s)
            with sp.If(overflow(sp) > 0):
                for j in range(OVER):
                    e = sp.value_load(at(M_IDX + 256 + j, (1, 1), pn=1).bitcast(I32), min_val=0, max_val=NE - 1)
                    i = NE + j
                    sp.wait_ge(gu_ps, i - 3)
                    gate_up(e, i % 4)
                    sp.wait_ge(y_ps, i - 3)
                    down(e, i % 4)

        @block.tensor
        def _(pe):
            blocks_taken = [0]

            def take(job):
                if J[job] >= 4:
                    pe.wait_ge(ps_free[pair(job)], J[job] // 4)

            def weights():
                b = blocks_taken[0]
                blocks_taken[0] += 1
                pe.wait_ge(w_ready[b % RING], 16 * (b // RING + 1))
                return O_W + (b % RING) * WB

            owed = []

            def signed(ins):
                if owed:
                    ins.then_inc(*owed.pop(0))
                return ins

            def mm(*a, **kw):
                return signed(nc.tensor.matmul(*a, **kw))

            def turn_tile(*a):
                return signed(nc.tensor.transpose(*a))

            def columns(job, w, wstep, src, kts):
                take(job)
                p = pair(job)
                for half in range(2):
                    for kt in range(kts):
                        last = mm(pat(p, half * 512, (1, TH)), at(w + kt * wstep, (1, 128)),
                                  at(src + kt * T + half * TH, (1, TH)), start=(kt == 0), stop=(kt == kts - 1))
                return last

            def rows_of(job, off, w, wn, n, src, t, kts=KT, wstep=None, srcw=T):
                wstep = wn if wstep is None else wstep
                R = ROWS[t]
                for kt in range(kts):
                    last = mm(pat(pair(job), off, (1, n), pn=R), at(src + kt * srcw + t * 128, (1, R)),
                              at(w + kt * wstep, (1, n)), start=(kt == 0), stop=(kt == kts - 1))
                return last

            pe.wait_ge(ones_set, 1)
            pe.wait_ge(x_sq, 1)
            take("ssq")
            for half in range(2):
                for kt in range(KT):
                    last = mm(pat(pair("ssq"), half * 512, (1, TH)), at(O_ONE, (1, 128)),
                              at(A_Y + kt * T + half * TH, (1, TH)), start=(kt == 0), stop=(kt == KT - 1))
            last.then_inc(ps_ready, 1)
            pe.wait_ge(xn_ready, 1)
            wu = [weights(), weights()]
            for t in range(TT):
                take(f"u{t}")
                for i in range(2):
                    last = rows_of(f"u{t}", i * 256, wu[i], 256, 256, O_X, t)
                last.then_inc(ps_ready, 1)
            owed.append((w_used, 2))
            w = weights()
            for t in range(TT):
                take(f"kv{t}")
                rows_of(f"kv{t}", 0, w, 256, 256, O_X, t).then_inc(ps_ready, 1)
            owed.append((w_used, 1))
            pe.wait_ge(ld["const"], 16)
            pe.wait_ge(kv_sb, TT)
            take("kT")
            for t in range(TT):
                last = turn_tile(pat(pair("kT"), t * 128, (1, ROWS[t])),
                                           at(O_KV + t * 256, (1, 128), pn=ROWS[t]), at(O_ID, (1, ROWS[t]), pn=ROWS[t]))
            last.then_inc(ps_ready, 1)
            for m in range(4):
                if m % 2 == 0:
                    w = weights()
                columns(f"q{m}", w + (m % 2) * 128, 256, O_X, KT).then_inc(ps_ready, 1)
                if m % 2:
                    owed.append((w_used, 1))
            pe.wait_ge(y_built, 1)
            for i in range(8):
                take(f"K{i}")
                for n in range(4):
                    g = 4 * i + n
                    last = mm(pat(pair(f"K{i}"), n * 128, (1, 128), pn=CH), at(O_TH + 2048 + g * CH, (1, CH)),
                              at(A_Y + g * 144, (1, 128)), start=True, stop=True)
                last.then_inc(ps_ready, 1)
            pe.wait_ge(vt_built, 1)
            for i in range(4):
                take(f"VT{i}")
                for n in range(8):
                    last = turn_tile(pat(pair(f"VT{i}"), n * 128, (1, 128)),
                                               at(O_O + (8 * i + n) * 128, (1, 128)), ident)
                last.then_inc(ps_ready, 1)
            for i in range(4):
                pe.wait_ge(up_sb, i + 1)
                take(f"U{i}")
                for n in range(8):
                    g = 8 * i + n
                    last = turn_tile(pat(pair(f"U{i}"), (n // 4) * 512 + (n % 4) * NC, (1, NC)),
                                               at(A_UP + (i % 2) * 1024 + n * 128, (1, 128), pn=NC), at(O_ID, (1, NC), pn=NC))
                last.then_inc(ps_ready, 1)
            for i in range(4):
                pe.wait_ge(vt_sb, i + 1)
                pe.wait_ge(ug_sb, i + 1)
                take(f"B{i}")
                for n in range(8):
                    g = 8 * i + n
                    last = mm(pat(pair(f"B{i}"), (n // 4) * 512 + (n % 4) * NC, (1, NC)), at(A_VT + g * 128, (1, 128)),
                              at(O_UG + g * NC, (1, NC)), start=True, stop=True)
                last.then_inc(ps_ready, 1)
            for d in range(8):
                if d % 2 == 0:
                    w = weights()
                columns(f"g0{d}", w + (d % 2) * 128, 256, O_X, KT).then_inc(ps_ready, 1)
                if d % 2:
                    owed.append((w_used, 1))
            pe.wait_ge(ld["T"], 16 * L)
            pe.wait_ge(scanned, 1)
            for i in range(4):
                take(f"Y{i}")
                for n in range(8):
                    g = 8 * i + n
                    dst = pat(pair(f"Y{i}"), n * 128, (1, 128), pn=NC)
                    mm(dst, at(O_UG + g * NC, (1, NC)), at(A_VT + g * 128, (1, 128)), start=True, stop=False)
                    last = mm(dst, at(A_S + g, (G, NC)), at(A_Y + g * 144 + CH, (1, 128)), start=False, stop=True)
                last.then_inc(ps_ready, 1)
            for m in range(4):
                if m % 2 == 0:
                    w = weights()
                columns(f"qm{m}", w + (m % 2) * 128, 256, O_X, KT).then_inc(ps_ready, 1)
                if m % 2:
                    owed.append((w_used, 1))
            for i in range(4):
                pe.wait_ge(zc_ready, i + 1)
                take(f"Z{i}")
                for j in range(L):
                    last = turn_tile(pat(pair(f"Z{i}"), (j // 4) * 512 + (j % 4) * NC, (1, NC)),
                                               at(A_UC + i * 1024 + j * 128, (1, 128), pn=NC), at(O_ID, (1, NC), pn=NC))
                last.then_inc(ps_ready, 1)
            pe.wait_ge(memsq, 1)
            take("ssqm")
            for kt in range(KT):
                last = mm(pat(pair("ssqm"), 0, (1, MEM)), at(O_ONE, (1, 128)), at(A_MV + kt * MEM, (1, MEM)),
                          start=(kt == 0), stop=(kt == KT - 1))
            last.then_inc(ps_ready, 1)
            pe.wait_ge(memn, 1)
            for i in range(4):
                w = weights()
                take(f"mm{i}")
                for t in range(2):
                    last = rows_of(f"mm{i}", t * 512, w, 256, 256, A_MK, t, srcw=MEM)
                last.then_inc(ps_ready, 1)
                owed.append((w_used, 1))
            pe.wait_ge(mkv_sb, 2)
            take("kmT")
            for h in range(MH):
                for t in range(2):
                    last = turn_tile(pat(pair("kmT"), h * 256 + t * 128, (1, 128)),
                                               at(A_MKV + t * 1024 + h * 128, (1, 128)), ident)
            last.then_inc(ps_ready, 1)
            pe.wait_ge(z_sb, 4)
            w = weights()
            for m in range(4):
                columns(f"G{m}", w + m * 128, 512, O_Z, 4).then_inc(ps_ready, 1)
            owed.append((w_used, 1))

            def scores(n):
                kind, a, b = UNITS[n]
                take(f"S{n}")
                p = pair(f"S{n}")
                if kind == "w":
                    k0, kn = (a - 1, 256) if a else (0, 128)
                    for m in range(4):
                        last = mm(pat(p, m * 256, (1, kn)), at(O_Q + m * T + a * 128, (1, 128), p0=64 * b, pn=64),
                                  at(O_KT + k0 * 128, (1, kn), p0=64 * b, pn=64), start=True, stop=True)
                elif kind == "m":
                    for h in range(MH):
                        last = mm(pat(p, h * 256, (1, MEM)), at(O_UG + h * T + a * 128, (1, 128)),
                                  at(A_KMT + h * MEM, (1, MEM)), start=True, stop=True)
                elif kind == "ws":
                    pe.wait_ge(ld["samp"], 48)
                    pe.wait_ge(qzs_ready, 1)
                    for kv in range(2):
                        for hf in range(2):
                            for b4 in range(4):
                                last = mm(pat(p, (kv * 2 + hf) * 256, (1, 136)),
                                          at(O_QZS + hf * 512 + b4 * 128, (1, 128), p0=64 * kv, pn=64),
                                          at(A_SKT + (4 * hf + b4) * 136, (1, 136), p0=64 * kv, pn=64),
                                          start=(b4 == 0), stop=(b4 == 3))
                else:
                    pe.wait_ge(qz_ready, a + 1)
                    for b4 in range(4):
                        bb = 4 * a + b4
                        pe.wait_ge(ldmk[bb % 2], 16 * (bb // 2 + 1))
                        for h in range(MH):
                            last = mm(pat(p, 0, (1, MEM)), at(A_QZ + (b4 * 4 + h) * 128, (1, 128)),
                                      at(A_MK + (bb % 2) * 1024 + h * MEM, (1, MEM)),
                                      start=(b4 == 0 and h == 0), stop=(b4 == 3 and h == 3))
                        if b4 < 3:
                            last.then_inc(mk_used, 1)
                last.then_inc(ps_ready, 1)
                if kind == "ms":
                    owed.append((mk_used, 1))

            def turn(n):
                kind, a, b = UNITS[n]
                pe.wait_ge(p_ready, n + 1)
                take(f"T{n}")
                p = pair(f"T{n}")
                sc = A_SC + (n % 2) * 1024
                if kind in "wm":
                    for kb in range(1 if kind == "w" and a == 0 else 2):
                        for m in range(4):
                            last = turn_tile(pat(p, kb * 512 + m * 128, (1, 128)),
                                                       at(sc + m * 256 + kb * 128, (1, 128)), ident)
                elif kind == "ws":
                    for t4 in range(4):
                        turn_tile(pat(p, t4 * 128, (1, 128)), at(sc + t4 * 256, (1, 128)), ident)
                        last = turn_tile(pat(p, 512 + t4 * 128, (1, 128), pn=8),
                                                   at(sc + t4 * 256 + 128, (1, 8)), ident)
                else:
                    for kb in range(2):
                        last = turn_tile(pat(p, kb * 128, (1, 128)), at(sc + kb * 128, (1, 128)), ident)
                last.then_inc(ps_ready, 1)

            def outputs(n):
                kind, a, b = UNITS[n]
                pe.wait_ge(pt_ready, n + 1)
                take(f"O{n}")
                p = pair(f"O{n}")
                pt = A_PT + (n % 2) * 1024
                if kind == "w":
                    kbs = 2 if a else 1
                    for kb in range(kbs):
                        last = mm(pat(p, 0, (1, 512), pn=64),
                                  at(O_KV + (a - (kbs - 1) + kb) * 256 + 128 + 64 * b, (1, 64)),
                                  at(pt + kb * 512, (1, 512)), start=(kb == 0), stop=(kb == kbs - 1))
                elif kind == "m":
                    for h in range(MH):
                        for kb in range(2):
                            last = mm(pat(p, h * 128, (1, 128)), at(A_MKV + kb * 1024 + 512 + h * 128, (1, 128)),
                                      at(pt + kb * 512 + h * 128, (1, 128)), start=(kb == 0), stop=(kb == 1))
                elif kind == "ws":
                    pe.wait_ge(ld["svn"], 16)
                    pe.wait_ge(svn_ready, 16)
                    for kv in range(2):
                        for bb in range(NB):
                            dst = pat(p, kv * 256 + bb * 32, (1, 32), pn=64)
                            col = (kv * 2 + bb // 4) * 128 + (bb % 4) * 32
                            mm(dst, at(A_SV + bb * 128 + kv * 64, (1, 64)), at(pt + col, (1, 32)), start=True, stop=False)
                            last = mm(dst, at(A_SVN + bb * 128 + kv * 64, (1, 64), pn=8),
                                      at(pt + 512 + col, (1, 32), pn=8), start=False, stop=True)
                else:
                    for b4 in range(4):
                        bb = 4 * a + b4
                        pe.wait_ge(ldmv[bb % 2], 16 * (bb // 2 + 1))
                        for h in range(MH):
                            for kb in range(2):
                                last = mm(pat(p, (b4 * 4 + h) * 8, (1, 8)),
                                          at(A_MV + (bb % 2) * 1024 + kb * 512 + h * 128, (1, 128)),
                                          at(pt + kb * 128 + (b4 * 4 + h) * 8, (1, 8)), start=(kb == 0), stop=(kb == 1))
                        if b4 < 3:
                            last.then_inc(mv_used, 1)
                last.then_inc(ps_ready, 1)
                if kind == "ms":
                    owed.append((mv_used, 1))

            pe.wait_ge(kT_sb, 1)
            pe.wait_ge(q_sb, 4)
            pe.wait_ge(qm_sb, 4)
            pe.wait_ge(kmT_sb, 1)
            pe.wait_ge(mkv_sb, 4)
            n_units = len(UNITS)
            scores(0)
            for n in range(n_units + 1):
                if n + 1 < n_units:
                    scores(n + 1)
                if n >= 1:
                    outputs(n - 1)
                if n < n_units:
                    turn(n)

            pe.wait_ge(zz_ready, 1)
            pe.wait_ge(o_sb, n_units)
            for d in range(8):
                w = weights()
                columns(f"ga{d}", w, 256, O_X, KT).then_inc(ps_ready, 1)
                columns(f"gb{d}", w + 128, 256, O_X, KT).then_inc(ps_ready, 1)
                owed.append((w_used, 1))
                w = weights()
                columns(f"pa{d}", w + 512, 128, O_O, 4).then_inc(ps_ready, 1)
                columns(f"pb{d}", w + 1024, 128, O_O + 2304, 4).then_inc(ps_ready, 1)
                columns(f"pc{d}", w, 128, O_Z, 4).then_inc(ps_ready, 1)
                owed.append((w_used, 1))
            pe.wait_ge(m_ready, 8)
            for b in range(4):
                w = weights()
                for t in range(TT):
                    take(f"w{b}{t}")
                    rows_of(f"w{b}{t}", 0, w, 256, 256, O_Q, t).then_inc(ps_ready, 1)
                owed.append((w_used, 1))
            for t in range(TT):
                R = ROWS[t]
                pe.wait_ge(x2_ready, t + 1)
                take(f"x2T{t}")
                for kt in range(KT):
                    last = turn_tile(pat(pair(f"x2T{t}"), kt * 128, (1, R)),
                                               at(M_X2 + (t % 2) * 1024 + kt * 128, (1, 128), pn=R),
                                               at(O_ID, (1, R), pn=R))
                last.then_inc(ps_ready, 1)
                if t == 0:
                    pe.wait_ge(ld["wr"], 16)
                pe.wait_ge(x2T_sb, t + 1)
                take(f"lg{t}")
                for kt in range(KT):
                    last = mm(pat(pair(f"lg{t}"), 0, (1, 36), pn=R), at(M_X2T + (t % 2) * 1024 + kt * 128, (1, R)),
                              at(M_WR + kt * 36, (1, 36)), start=(kt == 0), stop=(kt == KT - 1))
                last.then_inc(ps_ready, 1)
            pe.wait_ge(m_onehot, 1)
            take("rk")
            p = pair("rk")
            for t in range(TT + 1):
                R = ROWS[t] if t < TT else 128
                srcs = list(range(t)) + ([t] if t < TT else [])
                for n, s in enumerate(srcs):
                    K = ROWS[s]
                    lhs = at(R_TRI, (1, R), pn=K) if s == t else at(O_ONE, (1, R), pn=K)
                    last = mm(pat(p, t * 32, (1, 32), pn=R), lhs, at(R_M + s * 32, (1, 32), pn=K),
                              start=(n == 0), stop=(n == len(srcs) - 1))
            last.then_inc(ps_ready, 1)

            def turn_rows(r, k):
                pe.wait_ge(xg_ready[k % 2], 32 * r + 16 * (k // 2 + 1))
                wait_pos(pe, xgT_ready, r, k, 0)
                for kt in range(KT):
                    last = turn_tile(pat(0, kt * 128, (1, 128)), at(M_XG + (k % 2) * 1024 + kt * 128, (1, 128)),
                                               ident)
                last.then_inc(xt_ps, 1)

            def gate_up(r, k, kts):
                if kts[0] == 0:
                    pe.wait_ge(wg_ready[k], 16 * r + 16)
                    wait_pos(pe, xgT_ready, r, k, 1)
                    wait_pos(pe, hid_ready, r, k, -1)
                for kt in kts:
                    last = mm(pat(1, (k % 2) * 512, (1, 512)), at(M_XGT + (k % 2) * 1024 + kt * 128, (1, 128)),
                              at(A_WG + k * 4096 + kt * 512, (1, 512)), start=(kt == 0), stop=(kt == KT - 1))
                if kts[-1] == KT - 1:
                    last.then_inc(gu_ps, 1)

            def turn_hidden(r, k):
                wait_pos(pe, hid_ready, r, k, 1)
                wait_pos(pe, hT_ready, r, k, 0)
                for c in range(2):
                    last = turn_tile(pat(2, c * 128, (1, 128)), at(M_HID + (k % 2) * 256 + c * 128, (1, 128)),
                                               ident)
                last.then_inc(hT_ps, 1)

            def down(r, k):
                pe.wait_ge(wd_ready[k % 4], 16 * r + 16)
                wait_pos(pe, hT_ready, r, k, 1)
                wait_pos(pe, y_copied, r, k, 0)
                for half in range(2):
                    for c in range(2):
                        last = mm(pat(3, half * 512, (1, 512)), at(M_HT + (k % 2) * 256 + c * 128, (1, 128)),
                                  at(O_W + (k % 4) * WB + c * 1024 + half * 512, (1, 512)), start=(c == 0), stop=(c == 1))
                last.then_inc(y_ps, 1)

            def body(r, k, first=False, last=False):
                pr, pk = (r, k - 1) if k else (r - 1, 3)
                nr, nk = (r, k + 1) if k < 3 else (r + 1, 0)
                gate_up(r, k, range(0, 4))
                if not first:
                    turn_hidden(pr, pk)
                if not last:
                    turn_rows(nr, nk)
                gate_up(r, k, range(4, 8))
                if not first:
                    down(pr, pk)

            for i in range(4):
                last_job = max(j for j in J.values() if j % 4 == i)
                pe.wait_ge(ps_free[i], last_job // 4 + 1)

            def blocks(r0, r1):
                turn_rows(r0, 0)
                for k in range(4):
                    body(r0, k, first=(k == 0))
                if r1 - r0 > 2:
                    with pe.Fori(r0 + 1, r1 - 1) as r:
                        for k in range(4):
                            body(r, k)
                for k in range(4):
                    body(r1 - 1, k, last=(k == 3))
                turn_hidden(r1 - 1, 3)
                down(r1 - 1, 3)

            blocks(0, NE // 4)
            with pe.If(overflow(pe) > 0):
                blocks(NE // 4, BLK // 4)

        @block.scalar
        def _(act):
            c = Chain(act, act_step)
            fn = nc.scalar.activation

            act.dma_start(at(O_X, (1, KT * T)), xT).then_inc(ld["xT"], 16)
            act.dma_start(at(O_SM, (1, N_SMALL)), small).then_inc(ld["small"], 16)
            act.dma_start(at(O_TH, (1, 2048)), ssm).then_inc(ld["ssm"], 16)
            act.dma_start(at(O_ID, (1, 128)), const[:, 0:128]).then_inc(ld["const"], 16)
            act.wait_ge(ld["small"], 16)
            fn(at(O_SM + S_T, (1, 32)), at(O_SM + S_LD, (1, 32)), ACT.Exp).then_inc(exp_ssm, 1)
            act.wait_ge(ld["xT"], 16)
            fn(at(A_Y, (1, KT * T)), at(O_X, (1, KT * T)), ACT.Square).then_inc(x_sq, 1)
            act.wait_ge(ang_ready, 1)
            fn(at(O_SM + S_T + 32, (1, 32)), at(O_SM + S_T + 64, (1, 32)), ACT.Exp).then_inc(exp_ssm, 1)
            fn(at(O_SM + S_T + 96, (1, 64)), at(O_SM + S_T + 160, (1, 64)), ACT.Sin).then_inc(trig, 1)

            roots = [0]

            def root(ap):
                roots[0] += 1
                act.wait_ge(ms_ready, roots[0])
                fn(ap, ap, ACT.Sqrt).then_inc(root_ready, 1)

            root(at(O_RS, (1, T)))

            def copy_out(job, dst, src, to, **kw):
                filled(act, job)
                c.free(fn(dst, src, ACT.Copy, **kw), job)
                act.wait_ge(*c.last)
                act.sem_inc(to, 1)

            for t in range(TT):
                R = ROWS[t]
                copy_out(f"u{t}", at(A_US + t * 512, (1, 512), pn=R), pat(pair(f"u{t}"), 0, (1, 512), pn=R), u_sb)
            for t in range(TT):
                R = ROWS[t]
                copy_out(f"kv{t}", at(O_KV + t * 256, (1, 256), pn=R), pat(pair(f"kv{t}"), 0, (1, 256), pn=R), kv_sb)
            copy_out("kT", at(O_KT, (1, T)), pat(pair("kT"), 0, (1, T)), kT_sb)
            for m in range(4):
                copy_out(f"q{m}", at(O_Q + m * T, (TH, 2), (1, TH)), pat(pair(f"q{m}"), 0, (512, 2), (1, TH)), q_sb)
            for i in range(4):
                copy_out(f"VT{i}", at(A_VT + i * 1024, (1, 1024)), pat(pair(f"VT{i}"), 0, (1, 1024)), vt_sb)
            for i in range(4):
                copy_out(f"U{i}", at(O_UG + i * 8 * NC, (4 * NC, 2), (1, 4 * NC)),
                         pat(pair(f"U{i}"), 0, (512, 2), (1, 4 * NC)), ug_sb)
            for d in range(8):
                filled(act, f"g0{d}")
                c.free(fn(at(O_TH + d * T, (TH, 2), (1, TH)), pat(pair(f"g0{d}"), 0, (512, 2), (1, TH)), ACT.Tanh, scale=0.5),
                       f"g0{d}")
            for i in range(4):
                p = pair(f"Y{i}")
                copy_out(f"Y{i}", at(A_UC + i * 1024, (CH, 8), (128, L), (1, CH), pn=NC),
                         pat(p, 0, (128, 8), (CH, L), (1, CH), pn=NC), yc_sb)
            for m in range(4):
                copy_out(f"qm{m}", at(O_UG + m * T, (TH, 2), (1, TH)), pat(pair(f"qm{m}"), 0, (512, 2), (1, TH)), qm_sb)
            for i in range(4):
                act.wait_ge(gelu_in, i + 1)
                fn(at(A_GL + (i % 2) * 1024, (1, 1024), pn=NC), at(A_GL + (i % 2) * 1024, (1, 1024), pn=NC), ACT.Tanh,
                   scale=0.7978845608028654).then_inc(gelu_th, 1)
            for i in range(4):
                filled(act, f"Z{i}")
                for half in range(2):
                    ins = fn(at(O_Z + i * T + half * 4, (1, 4), (L, NC)), pat(pair(f"Z{i}"), half * 512, (NC, 4), (1, NC)),
                             ACT.Copy, scale=0.5)
                    if half:
                        c.free(ins, f"Z{i}")
                    else:
                        c.do(ins)
                act.wait_ge(*c.last)
                act.sem_inc(z_sb, 1)
            act.wait_ge(ld["memT"], 16)
            fn(at(A_MV, (1, KT * MEM)), at(A_MK, (1, KT * MEM)), ACT.Square).then_inc(memsq, 1)
            root(at(O_RS, (1, MEM)))
            for i in range(4):
                copy_out(f"mm{i}", at(A_MKV + i * 256, (1024, 2), (1, 256)), pat(pair(f"mm{i}"), 0, (512, 2), (1, 256)), mkv_sb)
            copy_out("kmT", at(A_KMT, (1, 1024)), pat(pair("kmT"), 0, (1, 1024)), kmT_sb)
            act.wait_ge(par_ready, 1)
            for m in range(4):
                filled(act, f"G{m}")
                c.free(fn(at(A_THG + m * T, (TH, 2), (1, TH)), pat(pair(f"G{m}"), 0, (512, 2), (1, TH)), ACT.Tanh, scale=0.5,
                          bias=at(O_SM + S_BG + m, (1, 1))), f"G{m}")
            act.wait_ge(*c.last)
            act.sem_inc(thg_sb, 1)

            def stat(n, k):
                return O_SM + S_ST + (n % 2) * 24 + 4 * k

            def exponentials(n):
                kind, a, b = UNITS[n]
                act.wait_ge(stat_ready, n + 1)
                sc = A_SC + (n % 2) * 1024
                if n >= 2:
                    filled(act, f"T{n - 2}")
                if kind in ("w", "ws"):
                    keys = 136 if kind == "ws" else (256 if a else 128)
                    for m in range(4):
                        fn(at(sc + m * 256, (1, keys)), at(sc + m * 256, (1, keys)), ACT.Exp,
                           bias=at(stat(n, 1) + m, (1, 1)), accum_out=at(stat(n, 3) + m, (1, 1)))
                    fn(at(stat(n, 4), (1, 4)), at(stat(n, 2), (1, 4)), ACT.Exp).then_inc(exp_ready, 1)
                else:
                    for m in range(4 if kind == "m" else 1):
                        ins = fn(at(sc + m * 256, (1, 256)), pat(pair(f"S{n}"), m * 256, (1, 256)), ACT.Exp, scale=MEM_SCALE,
                                 bias=at(stat(n, 1) + m, (1, 1)), accum_out=at(stat(n, 3) + m, (1, 1)))
                    ins.then_inc(exp_ready, 1)

            def turned(n):
                kind, a, b = UNITS[n]
                filled(act, f"T{n}")
                if n >= 2:
                    filled(act, f"O{n - 2}")
                p, pt = pair(f"T{n}"), A_PT + (n % 2) * 1024
                if kind == "ws":
                    c.do(fn(at(pt, (1, 512)), pat(p, 0, (1, 512)), ACT.Copy))
                    ins = fn(at(pt + 512, (1, 512), pn=8), pat(p, 512, (1, 512), pn=8), ACT.Copy)
                else:
                    w = 256 if kind == "ms" else (512 if kind == "w" and a == 0 else 1024)
                    ins = fn(at(pt, (1, w)), pat(p, 0, (1, w)), ACT.Copy)
                c.free(ins, f"T{n}")
                act.wait_ge(*c.last)
                act.sem_inc(pt_ready, 1)

            def output(n):
                kind, a, b = UNITS[n]
                filled(act, f"O{n}")
                p = pair(f"O{n}")
                if kind == "w":
                    ins = fn(at(O_O + a * 128, (T, 4), (1, 128), p0=64 * b, pn=64), pat(p, 0, (128, 4), (1, 128), pn=64), ACT.Copy)
                elif kind == "m":
                    ins = fn(at(O_O + 2304 + a * 128, (T, 4), (1, 128)), pat(p, 0, (128, 4), (1, 128)), ACT.Copy)
                elif kind == "ws":
                    for kv in range(2):
                        ins = fn(at(O_O + 512, (NQ, NB), (T, 4), (1, NQ), p0=64 * kv, pn=64),
                                 pat(p, kv * 256, (32, NB), (8, 4), (1, NQ), pn=64), ACT.Copy)
                        if kv == 0:
                            c.do(ins)
                else:
                    ins = fn(at(O_O + 2304 + 512 + a * 32, (NQ, 4), (T, 4), (1, NQ)), pat(p, 0, (32, 4), (8, 4), (1, NQ)), ACT.Copy)
                c.free(ins, f"O{n}")
                act.wait_ge(*c.last)
                act.sem_inc(o_sb, 1)

            n_units = len(UNITS)
            exponentials(0)
            for n in range(n_units + 1):
                if n + 1 < n_units:
                    exponentials(n + 1)
                if n >= 1:
                    output(n - 1)
                if n < n_units:
                    turned(n)
            for d in range(8):
                for job, dst, ready in ((f"ga{d}", O_T1, ga_sb), (f"gb{d}", O_T2, gb_sb)):
                    filled(act, job)
                    if d >= 1:
                        act.wait_ge(m_ready, d)
                    c.free(fn(at(dst, (TH, 2), (1, TH)), pat(pair(job), 0, (512, 2), (1, TH)), ACT.Tanh, scale=0.5), job)
                    act.wait_ge(*c.last)
                    act.sem_inc(ready, 1)
            def copy_x2T(t):
                R = ROWS[t]
                if t >= 2:
                    filled(act, f"lg{t - 2}")
                copy_out(f"x2T{t}", at(M_X2T + (t % 2) * 1024, (128, KT), (1, R)),
                         pat(pair(f"x2T{t}"), 0, (128, KT), (1, R)), x2T_sb)

            for t in range(TT):
                R = ROWS[t]
                act.wait_ge(h_ready, 15 + t + 1)
                fn(at(M_JUNK, (1, D), pn=R), at(O_H + t * D, (1, D), pn=R), ACT.Square,
                   accum_out=at(R_SS + t, (1, 1), pn=R)).then_inc(ss2, 1)
                root(at(R_SS + t, (1, 1), pn=R))
                if t >= 1:
                    copy_x2T(t - 1)
            copy_x2T(TT - 1)
            act.wait_ge(gate_d, 1)
            fn(at(R_GE, (1, 20)), at(R_GE, (1, 20)), ACT.Exp).then_inc(gate_e, 1)
            fn(at(R_ED, (1, 5)), at(R_ED, (1, 5)), ACT.Exp).then_inc(gate_e, 1)

            def rows_turned(r, k):
                wait_pos(act, xt_ps, r, k, 1)
                wait_pos(act, gu_ps, r, k, -1)
                fn(at(M_XGT + (k % 2) * 1024, (1, 1024)), pat(0, 0, (1, 1024)), ACT.Copy).then_inc(xgT_ready, 1)

            def gate(r, k):
                wait_pos(act, gu_ps, r, k, 1)
                wait_pos(act, hid_ready, r, k, -1)
                fn(at(M_THE + (k % 2) * 256, (1, 256)), pat(1, (k % 2) * 512, (1, 256)), ACT.Tanh, scale=0.5)\
                    .then_inc(th_ready, 1)

            def body(r, k, last=False):
                nr, nk = (r, k + 1) if k < 3 else (r + 1, 0)
                if not last:
                    rows_turned(nr, nk)
                gate(r, k)

            def blocks(r0, r1):
                rows_turned(r0, 0)
                for k in range(4):
                    body(r0, k)
                if r1 - r0 > 2:
                    with act.Fori(r0 + 1, r1 - 1) as r:
                        for k in range(4):
                            body(r, k)
                for k in range(4):
                    body(r1 - 1, k, last=(k == 3))

            blocks(0, NE // 4)
            with act.If(overflow(act) > 0):
                blocks(NE // 4, BLK // 4)
            for t in range(TT):
                R = ROWS[t]
                act.wait_ge(y_done, 2 * t + 1)
                fn(at(M_JUNK, (1, D), pn=R), at(O_H + t * D, (1, D), pn=R), ACT.Square,
                   accum_out=at(R_SS + 8 + t, (1, 1), pn=R)).then_inc(ssf, 1)
                root(at(R_SS + 8 + t, (1, 1), pn=R))

        @block.vector
        def _(dve):
            c = Chain(dve, vec_step)
            v = nc.vector

            def sm(k, n=32, p0=0, pn=P):
                return at(O_SM + S_T + 32 * k, (1, n), p0=p0, pn=pn)

            def op(ins, settle=True):
                c.do(ins)
                if settle:
                    c.settle()

            roots = [0]

            def inverse(ap):
                c.settle()
                dve.sem_inc(ms_ready, 1)
                roots[0] += 1
                dve.wait_ge(root_ready, roots[0])
                op(v.reciprocal(ap, ap))

            v.memset(at(O_ONE, (1, 128)), 1.0).then_inc(ones_set, 1)
            v.memset(at(A_ZERO, (1, 112)), 0.0).then_inc(zero_set, 1)
            dve.wait_ge(ld["small"], 16)
            op(v.tensor_scalar(at(O_SM + S_BG, (1, 4)), at(O_SM + S_BG, (1, 4)), 0.5, None, ALU.mult))
            dve.wait_ge(exp_ssm, 1)
            op(v.tensor_tensor(sm(2), at(O_SM + S_LR, (1, 32)), sm(0), ALU.mult), False)
            op(v.tensor_tensor(sm(7), at(O_SM + S_LI, (1, 32)), sm(0), ALU.mult))
            op(v.tensor_scalar(sm(8), sm(7), 1.0 / 6.283185307179586, MAGIC, ALU.mult, ALU.add))
            op(v.tensor_scalar(sm(8), sm(8), MAGIC, None, ALU.subtract))
            for part in (TWO_PI_A, TWO_PI_B, TWO_PI_C):
                op(v.scalar_tensor_tensor(sm(7), sm(8), -part, sm(7), ALU.mult, ALU.add))
            op(v.tensor_scalar(sm(5), sm(7), 3.1415925, -3.1415925, ALU.min, ALU.max))
            op(v.scalar_tensor_tensor(sm(6), sm(5), -1.0, sm(5), ALU.mult, ALU.max))
            c.do(v.tensor_scalar(sm(6), sm(6), -1.0, 1.5707963267948966, ALU.mult, ALU.add), ang_ready)
            filled(dve, "ssq")
            p = pair("ssq")
            c.free(v.tensor_scalar(at(O_RS, (TH, 2), (1, TH)), pat(p, 0, (512, 2), (1, TH)), 1.0 / D, EPS, ALU.mult, ALU.add),
                   "ssq")
            inverse(at(O_RS, (1, T)))
            for kt in range(KT):
                ins = v.scalar_tensor_tensor(at(O_X + kt * T, (1, T)), at(O_X + kt * T, (1, T)),
                                             at(O_SM + S_G1 + kt, (1, 1)), at(O_RS, (1, T)), ALU.mult, ALU.mult)
                if kt < KT - 1:
                    c.do(ins)
                else:
                    c.do(ins, xn_ready)

            dve.wait_ge(exp_ssm, 2)
            dve.wait_ge(trig, 1)
            pr, pi = O_PW, O_PW + 288

            def pw(base, j, n=1, **kw):
                return at(base + j * 32, (1, 32 * n), **kw)

            op(v.memset(pw(pr, 0), 1.0), False)
            op(v.memset(pw(pi, 0), 0.0), False)
            op(v.tensor_tensor(pw(pr, 1), sm(1), sm(4), ALU.mult), False)
            op(v.tensor_tensor(pw(pi, 1), sm(1), sm(3), ALU.mult))
            for j in range(2, 9):
                h = {2: 1, 3: 2, 4: 2, 5: 4, 6: 4, 7: 4, 8: 4}[j]
                op(v.tensor_tensor(sm(7), pw(pr, h), pw(pr, j - h), ALU.mult), False)
                op(v.tensor_tensor(sm(8), pw(pi, h), pw(pi, j - h), ALU.mult), False)
                op(v.tensor_tensor(sm(9), pw(pr, h), pw(pi, j - h), ALU.mult), False)
                op(v.tensor_tensor(sm(10), pw(pi, h), pw(pr, j - h), ALU.mult))
                op(v.tensor_tensor(pw(pr, j), sm(7), sm(8), ALU.subtract), False)
                op(v.tensor_tensor(pw(pi, j), sm(9), sm(10), ALU.add))
            op(v.tensor_copy(at(O_SM + S_A8, (32, 2), (1, 32)), at(pr + 8 * 32, (0, 2), (1, 32))), False)
            op(v.tensor_scalar(at(O_SM + S_A8 + 64, (1, 32)), pw(pi, 8), -1.0, None, ALU.mult), False)
            op(v.tensor_copy(at(O_SM + S_A8 + 96, (1, 32)), pw(pi, 8)))
            lr, li = at(O_SM + S_LR, (1, 32)), at(O_SM + S_LI, (1, 32))
            op(v.tensor_tensor(sm(7), lr, lr, ALU.mult), False)
            op(v.tensor_tensor(sm(8), li, li, ALU.mult), False)
            op(v.tensor_scalar(sm(9), pw(pr, 1), 1.0, None, ALU.subtract))
            op(v.tensor_tensor(sm(7), sm(7), sm(8), ALU.add), False)
            op(v.tensor_tensor(sm(10), sm(9), lr, ALU.mult), False)
            op(v.tensor_tensor(sm(11), pw(pi, 1), li, ALU.mult), False)
            op(v.tensor_tensor(sm(12), pw(pi, 1), lr, ALU.mult), False)
            op(v.tensor_tensor(sm(13), sm(9), li, ALU.mult))
            op(v.reciprocal(sm(7), sm(7)), False)
            op(v.tensor_tensor(sm(10), sm(10), sm(11), ALU.add), False)
            op(v.tensor_tensor(sm(12), sm(12), sm(13), ALU.subtract))
            op(v.tensor_tensor(sm(11), sm(10), sm(7), ALU.mult), False)
            op(v.tensor_tensor(sm(12), sm(12), sm(7), ALU.mult))
            P1, P2, Q1, Q2 = (O_PW + 576 + 288 * k for k in range(4))
            for dst, re, rs, im, is_ in ((P1, pr, 1.0, pi, -1.0), (P2, pi, -1.0, pr, -1.0), (Q1, pr, 1.0, pi, 1.0),
                                         (Q2, pi, -1.0, pr, 1.0)):
                op(v.tensor_scalar(pw(dst, 0, 9, pn=64), pw(re, 0, 9, pn=64), rs, None, ALU.mult), False)
                op(v.tensor_scalar(pw(dst, 0, 9, p0=64, pn=64), pw(im, 0, 9, p0=64, pn=64), is_, None, ALU.mult), False)
            c.settle()
            dve.wait_ge(ld["ssm"], 16)
            b1, b2, c1, c2 = (O_TH + 512 * k for k in range(4))
            br_, bi_ = O_TH + 3072, O_TH + 3584
            bst = O_TH + 2048

            def g16(off, n=G):
                return at(off, (CH, n), (1, CH))

            def fb(k):
                return at(O_SM + S_T + 32 * k, (1, G), (0, CH))

            tmp = O_Z
            op(v.tensor_tensor(g16(br_), g16(b1), fb(11), ALU.mult), False)
            op(v.tensor_tensor(g16(tmp), g16(b2), fb(12), ALU.mult), False)
            op(v.tensor_tensor(g16(bi_), g16(b2), fb(11), ALU.mult), False)
            op(v.tensor_tensor(g16(tmp + 512), g16(b1), fb(12), ALU.mult))
            op(v.tensor_tensor(at(br_, (1, 512)), at(br_, (1, 512)), at(tmp, (1, 512)), ALU.subtract), False)
            op(v.tensor_tensor(at(bi_, (1, 512)), at(bi_, (1, 512)), at(tmp + 512, (1, 512)), ALU.add))
            op(v.tensor_copy(at(bst, (1, 512), pn=64), at(br_, (1, 512), pn=64)), False)
            op(v.tensor_copy(at(bst, (1, 512), p0=64, pn=64), at(bi_, (1, 512), p0=64, pn=64)))

            for hf in range(2):
                dims = ((144, 16), (CH, 9), (1, CH))
                g0 = 16 * hf
                dst = at(A_Y + g0 * 144, *dims)
                op(v.tensor_tensor(dst, at(c1 + g0 * CH, (CH, 16), (0, 9), (1, CH)), at(P1 + g0, (1, 16), (32, 9), (0, CH)),
                                   ALU.mult), False)
                op(v.tensor_tensor(at(tmp, *dims), at(c2 + g0 * CH, (CH, 16), (0, 9), (1, CH)),
                                   at(P2 + g0, (1, 16), (32, 9), (0, CH)), ALU.mult))
                ins = v.tensor_tensor(at(A_Y + g0 * 144, (1, 2304)), at(A_Y + g0 * 144, (1, 2304)), at(tmp, (1, 2304)), ALU.add)
                if hf:
                    c.do(ins, y_built)
                else:
                    c.do(ins)
                c.settle()
            for hf in range(2):
                dims = ((128, 16), (CH, L), (1, CH))
                g0 = 16 * hf
                op(v.tensor_tensor(at(O_O + g0 * 128, *dims), at(br_ + g0 * CH, (CH, 16), (0, L), (1, CH)),
                                   at(Q1 + 7 * 32 + g0, (1, 16), (-32, L), (0, CH)), ALU.mult), False)
                op(v.tensor_tensor(at(tmp, *dims), at(bi_ + g0 * CH, (CH, 16), (0, L), (1, CH)),
                                   at(Q2 + 7 * 32 + g0, (1, 16), (-32, L), (0, CH)), ALU.mult))
                ins = v.tensor_tensor(at(O_O + g0 * 128, (1, 2048)), at(O_O + g0 * 128, (1, 2048)), at(tmp, (1, 2048)), ALU.add)
                if hf:
                    c.do(ins, vt_built)
                else:
                    c.do(ins)
                c.settle()
            dve.wait_ge(ld["const"], 16)
            op(v.tensor_tensor(at(tmp, (CH, G), (1, CH), pn=CH), at(O_ID, (0, G), (1, CH), pn=CH),
                               at(O_SM + S_DS, (1, G), (0, CH), pn=CH), ALU.mult))
            for i in range(8):
                filled(dve, f"K{i}")
                if i >= 4:
                    dve.wait_ge(k_out[i % 4], 16)
                p, ks = pair(f"K{i}"), A_KS + (i % 4) * 512
                op(v.tensor_copy(at(ks, (1, 512), pn=CH), pat(p, 0, (1, 512), pn=CH)))
                c.free(v.tensor_tensor(at(ks, (128, 4), (1, CH), pn=CH), pat(p, 0, (128, 4), (1, CH), pn=CH),
                                       at(tmp + i * 64, (CH, 4), (1, CH), pn=CH), ALU.add), f"K{i}")
                c.settle()
                dve.sem_inc(ks_sb, 1)

            dve.wait_ge(u_out, 16 * TT)
            dve.wait_ge(ld["uc"], 16)
            for i in range(4):
                if i >= 2:
                    filled(dve, f"U{i - 2}")
                c.do(v.tensor_copy(at(A_UP + (i % 2) * 1024, (128, 8), (CH, L), (1, CH), pn=NC),
                                   at(A_UC + i * 128, (CH, 8), (512, L), (1, CH), pn=NC)), up_sb)

            def slot(n, comp=0, cnt=1, p0=0, pn=P):
                return at(A_S + comp * SLOTS * G + n * G, (1, cnt * G), p0=p0, pn=pn)

            dve.wait_ge(u_out, 16 * TT)
            for n in range(4):
                dve.wait_ge(k_out[n], 32)
            dve.wait_ge(kz_out, 16)
            filled(dve, "U3")
            op(v.memset(slot(0), 0.0), False)
            op(v.memset(slot(0, 1), 0.0))
            dve.sem_inc(par_ready, 1)
            for i in range(4):
                filled(dve, f"B{i}")
                p = pair(f"B{i}")
                for n in range(2):
                    g0 = 8 * i + 4 * n
                    op(v.tensor_copy(at(A_S + G + g0, (G, PC - 1), (1, 4)), pat(p, n * 512, (1, PC - 1), (NC, 4))), False)
                    ins = v.tensor_copy(at(A_S + 72 * G + g0, (G, 1 + NB), (1, 4)), pat(p, n * 512 + PC - 1, (1, 1 + NB), (NC, 4)))
                    if n == 0:
                        c.do(ins)
                    else:
                        c.free(ins, f"B{i}")
            c.settle()
            for a, cnt in ((1, PC - 1), (72, 1 + NB)):
                op(v.tensor_scalar(slot(a, 1, cnt, 0, 64), slot(a, 0, cnt, 64, 64), -1.0, None, ALU.mult), False)
                op(v.tensor_copy(slot(a, 1, cnt, 64, 64), slot(a, 0, cnt, 0, 64)), False)
            dve.wait_ge(ld["h0"], 16)
            op(v.tensor_scalar(slot(64, 1, NB, 0, 64), slot(64, 1, NB, 0, 64), -1.0, None, ALU.mult))
            t1 = O_SM + S_SC
            CS = SLOTS * G

            def advance(src, dst, k):
                v.tensor_tensor(at(t1, (64, 2), (32, 2), (1, G)), at(O_SM + S_A8, (64, 2), (32, 2), (1, G)),
                                at(A_S + src, (0, 2), (CS, 2), (1, G)), ALU.mult).then_inc(scan, 1)
                dve.wait_ge(scan, k * 4 + 1)
                v.tensor_tensor(at(A_S + dst, (CS, 2), (1, G)), at(A_S + dst, (CS, 2), (1, G)), at(t1, (32, 2), (1, G)),
                                ALU.add).then_inc(scan, 1)
                dve.wait_ge(scan, k * 4 + 2)
                for comp, term in ((0, 3), (1, 2)):
                    part = at(A_S + comp * CS + dst, (1, G))
                    v.tensor_tensor(part, part, at(t1 + 32 * term, (1, G)), ALU.add).then_inc(scan, 1)
                dve.wait_ge(scan, k * 4 + 4)

            with dve.Fori(0, (PC - 2) // 2) as r:
                for k in range(2):
                    advance((r * 2 + (k + 1)) * G, (r * 2 + (k + 2)) * G, r * 2 + k)
            advance((PC - 1) * G, 72 * G, PC - 2)
            for n in range(NB):
                src, dst = (64 + n) * G, (73 + n) * G
                w = tmp + 64 * n
                op(v.tensor_tensor(at(w, (1, G)), at(O_SM + S_A8, (1, G)), at(A_S + src, (1, G)), ALU.mult), False)
                op(v.tensor_tensor(at(w + 32, (1, G)), at(O_SM + S_A8 + 96, (1, G)), at(A_S + CS + src, (1, G)), ALU.mult), False)
            c.settle()
            for n in range(2):
                op(v.tensor_tensor(at(A_S + 73 * G, (G, NB), (1, G)), at(A_S + 73 * G, (G, NB), (1, G)),
                                   at(tmp + 32 * n, (64, NB), (1, G)), ALU.add))
            dve.sem_inc(scanned, 1)

            def gelu_begin(i):
                yc, gl = at(A_UC + i * 1024, (1, 1024), pn=NC), at(A_GL + (i % 2) * 1024, (1, 1024), pn=NC)
                dve.wait_ge(yc_sb, i + 1)
                op(v.scalar_tensor_tensor(gl, yc, 0.044715, yc, ALU.mult, ALU.mult))
                c.do(v.scalar_tensor_tensor(gl, gl, 1.0, yc, ALU.add, ALU.mult), gelu_in)

            def gelu_end(i):
                yc, gl = at(A_UC + i * 1024, (1, 1024), pn=NC), at(A_GL + (i % 2) * 1024, (1, 1024), pn=NC)
                dve.wait_ge(gelu_th, i + 1)
                c.do(v.scalar_tensor_tensor(yc, gl, 1.0, yc, ALU.add, ALU.mult), zc_ready)
                c.settle()

            filled(dve, "Y3")
            dve.wait_ge(out_st, 16 * 2)
            gelu_begin(0)
            for i in range(4):
                if i < 3:
                    gelu_begin(i + 1)
                gelu_end(i)
            filled(dve, "ssqm")
            c.free(v.tensor_scalar(at(O_RS, (1, MEM)), pat(pair("ssqm"), 0, (1, MEM)), 1.0 / D, EPS, ALU.mult, ALU.add), "ssqm")
            inverse(at(O_RS, (1, MEM)))
            for kt in range(KT):
                ins = v.scalar_tensor_tensor(at(A_MK + kt * MEM, (1, MEM)), at(A_MK + kt * MEM, (1, MEM)),
                                             at(O_SM + S_GM + kt, (1, 1)), at(O_RS, (1, MEM)), ALU.mult, ALU.mult)
                c.do(ins, memn if kt == KT - 1 else None)
            dve.wait_ge(thg_sb, 1)
            ins = v.scalar_tensor_tensor(at(O_Z, (1, 4 * T)), at(A_THG, (1, 4 * T)), 1.0, at(O_Z, (1, 4 * T)), ALU.add, ALU.mult)
            c.do(ins, zz_ready)
            c.settle()

            def stat(n, k, m=4):
                return at(O_SM + S_ST + (n % 2) * 24 + 4 * k, (1, m))

            def maxima(n):
                kind, a, b = UNITS[n]
                filled(dve, f"S{n}")
                if n >= 2:
                    filled(dve, f"T{n - 2}")
                p, sc = pair(f"S{n}"), A_SC + (n % 2) * 1024
                if kind in ("w", "ws"):
                    if kind == "w":
                        keys, k0 = (256, 0) if a else (128, 128)
                        sc_v, ps_v = at(sc, (256, 4), (1, keys)), pat(p, 0, (256, 4), (1, keys))
                        bias_v = at(A_BI + b * 1024 + k0, (256, 4), (1, keys))
                        sink = at(O_SM + S_SK + 4 * b, (1, 4))
                        if n == 0:
                            dve.wait_ge(ld["bias"], 16)
                        c.free(v.scalar_tensor_tensor(sc_v, ps_v, SWA_SCALE, bias_v, ALU.mult, ALU.add), f"S{n}")
                    else:
                        keys = 136
                        sc_v = at(sc, (256, 4), (1, keys))
                        sink = at(O_SM + S_SS, (1, 2), (0, 2))
                        for kv in range(2):
                            ins = v.scalar_tensor_tensor(at(sc + kv * 512, (256, 2), (1, keys)),
                                                         pat(p, kv * 512, (256, 2), (1, keys)), SWA_SCALE,
                                                         at(A_SB + kv * 136, (0, 2), (1, keys)), ALU.mult, ALU.add)
                            if kv:
                                c.free(ins, f"S{n}")
                            else:
                                c.do(ins)
                    c.settle()
                    op(v.tensor_reduce(stat(n, 0), sc_v, AX, ALU.max))
                    op(v.tensor_tensor(stat(n, 0), stat(n, 0), sink, ALU.max))
                    op(v.tensor_scalar(stat(n, 1), stat(n, 0), -1.0, None, ALU.mult), False)
                    c.do(v.tensor_tensor(stat(n, 2), sink, stat(n, 0), ALU.subtract), stat_ready)
                else:
                    m = 4 if kind == "m" else 1
                    op(v.tensor_reduce(stat(n, 0, m), pat(p, 0, (256, m), (1, 256)), AX, ALU.max))
                    c.do(v.tensor_scalar(stat(n, 1, m), stat(n, 0, m), -MEM_SCALE, None, ALU.mult), stat_ready)

            def divide(n):
                kind, a, b = UNITS[n]
                dve.wait_ge(exp_ready, n + 1)
                sc = A_SC + (n % 2) * 1024
                m = 1 if kind == "ms" else 4
                if kind in ("w", "ws"):
                    keys = 136 if kind == "ws" else (256 if a else 128)
                    op(v.tensor_tensor(stat(n, 3), stat(n, 3), stat(n, 4), ALU.add))
                    op(v.reciprocal(stat(n, 5), stat(n, 3)))
                else:
                    keys = 256
                    c.free(v.reciprocal(stat(n, 5, m), stat(n, 3, m)), f"S{n}")
                    c.settle()
                c.do(v.tensor_tensor(at(sc, (256, m), (1, keys)), at(sc, (256, m), (1, keys)),
                                     at(O_SM + S_ST + (n % 2) * 24 + 20, (1, m), (0, keys)), ALU.mult), p_ready)

            op(v.memset(at(O_QZS, (1, 1024)), 0.0), False)
            dve.wait_ge(q_sb, 4)
            c.settle()
            for hf in range(2):
                c.do(v.tensor_copy(at(O_QZS + hf * 512, (128 + 32, 4), (8, 4), (1, NQ)),
                                   at(O_Q + 512 + hf * 32, (NQ, 4), (T, 4), (1, NQ))), qzs_ready if hf else None)
            dve.wait_ge(z_sb, 4)
            op(v.memset(at(A_QZ, (1, 2048)), 0.0), False)
            dve.wait_ge(qm_sb, 4)
            c.settle()

            def place(half):
                c.do(v.tensor_copy(at(A_QZ, (4 * 136, 4), (136, 4), (1, NQ)), at(O_UG + 512 + half * 32, (NQ, 4), (T, 4), (1, NQ))),
                     qz_ready)

            place(0)
            n_units = len(UNITS)
            maxima(0)
            for n in range(n_units):
                if n + 1 < n_units:
                    maxima(n + 1)
                divide(n)
                if UNITS[n][0] == "ws":
                    filled(dve, f"S{n + 1}")
                    place(1)

            for d in range(8):
                dve.wait_ge(ga_sb, d + 1)
                filled(dve, f"pa{d}")
                m2 = at(O_M, (TH, 2), (1, TH))

                def prod(job, gate, dst):
                    c.free(v.scalar_tensor_tensor(at(dst, (TH, 2), (1, TH)), at(gate, (TH, 2), (1, TH)), 1.0,
                                                  pat(pair(job), 0, (512, 2), (1, TH)), ALU.add, ALU.mult), job)

                prod(f"pa{d}", O_T1, O_M)
                dve.wait_ge(gb_sb, d + 1)
                filled(dve, f"pb{d}")
                prod(f"pb{d}", O_T2, O_T2)
                filled(dve, f"pc{d}")
                prod(f"pc{d}", O_TH + d * T, O_TH + d * T)
                c.settle()
                op(v.tensor_tensor(at(O_M, (1, T)), at(O_M, (1, T)), at(O_T2, (1, T)), ALU.add))
                c.do(v.scalar_tensor_tensor(at(O_Q + d * T, (1, T)), at(O_TH + d * T, (1, T)), 0.5, at(O_M, (1, T)),
                                            ALU.mult, ALU.add), m_ready)
            c.settle()
            dve.wait_ge(ld["x"], 16 * TT)
            for b in range(4):
                for t in range(TT):
                    R, job = ROWS[t], f"w{b}{t}"
                    filled(dve, job)
                    h = at(O_H + t * D + b * 256, (1, 256), pn=R)
                    c.free(v.scalar_tensor_tensor(h, pat(pair(job), 0, (1, 256), pn=R), 0.5, h, ALU.mult, ALU.add), job)
                    c.settle()
                    dve.sem_inc(h_ready, 1)
            dve.wait_ge(ld["rows"], 32)
            op(v.memset(at(R_LG, (1, 36 * TT)), 0.0), False)
            op(v.memset(at(R_GP, (1, 8 * TT)), -3.0e38), False)

            def logits(t):
                R = ROWS[t]
                filled(dve, f"lg{t}")
                c.free(v.tensor_tensor(at(R_LG + 36 * t, (1, 36), pn=R), pat(pair(f"lg{t}"), 0, (1, 36), pn=R),
                                       at(M_BR, (1, 36), pn=R), ALU.add), f"lg{t}")

            dve.wait_ge(ld["wr"], 16)
            for t in range(TT):
                R = ROWS[t]
                ss = at(R_SS + t, (1, 1), pn=R)
                dve.wait_ge(ss2, t + 1)
                op(v.tensor_scalar(ss, ss, 1.0 / D, EPS, ALU.mult, ALU.add))
                inverse(ss)
                if t >= 2:
                    dve.wait_ge(x2_out[t % 2], 16 * (t // 2))
                    filled(dve, f"x2T{t - 2}")
                c.do(v.scalar_tensor_tensor(at(M_X2 + (t % 2) * 1024, (1, D), pn=R), at(O_H + t * D, (1, D), pn=R), ss,
                                            at(M_G2, (1, D), pn=R), ALU.mult, ALU.mult), x2_ready)
                if t >= 1:
                    logits(t - 1)
            logits(TT - 1)
            c.settle()
            n5 = TT
            op(v.tensor_copy(at(R_GP, (8, n5), (1, 4)), at(R_LG, (36, n5), (1, 4))))
            for t in range(n5):
                op(v.max(at(R_GM + 8 * t, (1, 8)), at(R_GP + 8 * t, (1, 8))), False)
            c.settle()
            for t in range(n5):
                op(v.max_index(at(R_IX + 8 * t, (1, 8)).bitcast(U32), at(R_GM + 8 * t, (1, 8)), at(R_GP + 8 * t, (1, 8))), False)
            c.settle()
            op(v.tensor_copy(at(R_GX, (1, n5)), at(R_IX, (8, n5)).bitcast(U32)), False)
            op(v.tensor_tensor(at(R_GE, (4, n5), (1, 4)), at(R_LG, (36, n5), (1, 4)), at(R_GM, (8, n5), (0, 4)), ALU.subtract))
            op(v.tensor_tensor(at(R_OG, (4, n5), (1, 4)), at(R_IOTA, (0, n5), (1, 4)), at(R_GX, (1, n5), (0, 4)), ALU.is_equal))
            op(v.tensor_tensor(at(R_TM, (32, n5), (8, 4), (1, 8)), at(R_LG + 4, (36, n5), (8, 4), (1, 8)),
                               at(R_OG, (4, n5), (1, 4), (0, 8)), ALU.mult))
            op(v.tensor_reduce(at(R_EP, (8, n5), (1, 8)), at(R_TM, (32, n5), (1, 8), (8, 4)), AX, ALU.add))
            for t in range(n5):
                op(v.max(at(R_EM + 8 * t, (1, 8)), at(R_EP + 8 * t, (1, 8))), False)
            c.settle()
            for t in range(n5):
                op(v.max_index(at(R_IX + 8 * t, (1, 8)).bitcast(U32), at(R_EM + 8 * t, (1, 8)), at(R_EP + 8 * t, (1, 8))), False)
            c.do(v.tensor_tensor(at(R_ED, (1, n5)), at(R_EM + 1, (8, n5)), at(R_EM, (8, n5)), ALU.subtract), gate_d)
            c.settle()
            op(v.tensor_copy(at(R_EK, (n5, 2), (1, n5)), at(R_IX, (1, 2), (8, n5)).bitcast(U32)))
            op(v.scalar_tensor_tensor(at(R_EK, (n5, 2), (1, n5)), at(R_GX, (0, 2), (1, n5)), 8.0, at(R_EK, (n5, 2), (1, n5)),
                                      ALU.mult, ALU.add))
            op(v.tensor_tensor(at(R_MK, (32, 2 * n5), (1, 32)), at(R_IOTA, (0, 2 * n5), (1, 32)),
                               at(R_EK, (1, 2 * n5), (0, 32)), ALU.is_equal))
            c.do(v.tensor_tensor(at(R_M, (1, 32 * n5)), at(R_MK, (1, 32 * n5)), at(R_MK + 32 * n5, (1, 32 * n5)), ALU.add), m_onehot)
            dve.wait_ge(gate_e, 2)
            op(v.tensor_reduce(at(R_W0, (1, n5)), at(R_GE, (4, n5), (1, 4)), AX, ALU.add), False)
            op(v.tensor_scalar(at(R_W1, (1, n5)), at(R_ED, (1, n5)), 1.0, None, ALU.add))
            op(v.tensor_tensor(at(R_W0, (1, n5)), at(R_W0, (1, n5)), at(R_W1, (1, n5)), ALU.mult))
            op(v.reciprocal(at(R_W0, (1, n5)), at(R_W0, (1, n5))))
            op(v.tensor_scalar(at(R_W0, (1, n5)), at(R_W0, (1, n5)), 0.5, None, ALU.mult))
            op(v.tensor_tensor(at(R_W1, (1, n5)), at(R_W0, (1, n5)), at(R_ED, (1, n5)), ALU.mult), False)
            filled(dve, "rk")
            for t in range(TT + 1):
                R = ROWS[t] if t < TT else 128
                ins = v.tensor_copy(at(R_RK + 32 * t, (1, 32), pn=R), pat(pair("rk"), 32 * t, (1, 32), pn=R))
                if t < TT:
                    c.do(ins)
                else:
                    c.free(ins, "rk")
            op(v.memset(at(R_RK + 32 * 4, (1, 32), p0=64, pn=64), 0.0))
            cnt, nb, inc, ovo = R_RK + 160, R_NB, R_NB + 32, R_NB + 64
            op(v.tensor_scalar(at(nb, (1, 32)), at(cnt, (1, 32)), 128.0, None, ALU.is_gt))
            for th in (256.0, 384.0, 512.0):
                op(v.scalar_tensor_tensor(at(nb, (1, 32)), at(cnt, (1, 32)), th, at(nb, (1, 32)), ALU.is_gt, ALU.add))
            op(v.tensor_tensor_scan(at(inc, (1, 32)), at(O_ONE, (1, 32)), at(nb, (1, 32)), 0.0, ALU.mult, ALU.add))
            op(v.tensor_tensor(at(ovo, (1, 32)), at(inc, (1, 32)), at(nb, (1, 32)), ALU.subtract))
            op(v.tensor_tensor(at(R_TM, (160, 2), (1, 160)), at(R_MK, (160, 2), (1, 160)), at(R_RK, (0, 2), (1, 160)), ALU.mult))
            op(v.tensor_reduce(at(R_RA, (1, 10)), at(R_TM, (32, 10), (1, 32)), AX, ALU.add))
            op(v.tensor_tensor(at(R_TM, (32, 10), (1, 32)), at(R_MK, (32, 10), (1, 32)), at(ovo, (0, 10), (1, 32)), ALU.mult))
            op(v.tensor_reduce(at(R_OB, (1, 10)), at(R_TM, (32, 10), (1, 32)), AX, ALU.add), False)
            ra, ob, fl, ov, ek = (at(o, (1, 10)) for o in (R_RA, R_OB, R_FL, R_OV, R_EK))
            op(v.tensor_scalar(ov, ra, 128.0, None, ALU.is_ge))
            op(v.tensor_copy(fl, ov))
            for th in (256.0, 384.0, 512.0):
                op(v.scalar_tensor_tensor(fl, ra, th, fl, ALU.is_ge, ALU.add))
            op(v.tensor_tensor(ob, ob, fl, ALU.add))
            op(v.tensor_scalar(ob, ob, float(NE - 1), None, ALU.add))
            op(v.tensor_tensor(ob, ob, ek, ALU.subtract))
            op(v.tensor_tensor(ob, ob, ov, ALU.mult))
            op(v.tensor_tensor(ob, ob, ek, ALU.add))
            op(v.scalar_tensor_tensor(ra, fl, -128.0, ra, ALU.mult, ALU.add))
            op(v.scalar_tensor_tensor(ra, ra, float(BLK), ob, ALU.mult, ALU.add))
            op(v.tensor_copy(at(R_SL, (1, 10)).bitcast(U32), ra), False)
            c.do(v.tensor_copy(at(R_PI, (1, 10)).bitcast(U32), at(R_PF, (1, 10))), slot_ready)
            op(v.tensor_tensor(at(R_TM, (32, 8), (1, 32)), at(ovo, (0, 8), (1, 32)), at(R_IOTA, (1, 8), (0, 32)), ALU.is_le), False)
            op(v.tensor_tensor(at(R_TM2, (32, 8), (1, 32)), at(inc, (0, 8), (1, 32)), at(R_IOTA, (1, 8), (0, 32)), ALU.is_gt))
            op(v.tensor_tensor(at(R_TM, (1, 256)), at(R_TM, (1, 256)), at(R_TM2, (1, 256)), ALU.mult))
            op(v.tensor_tensor(at(R_TM, (32, 8), (1, 32)), at(R_TM, (32, 8), (1, 32)), at(R_IOTA, (0, 8), (1, 32)), ALU.mult))
            op(v.tensor_reduce(at(R_TM2, (1, 8)), at(R_TM, (32, 8), (1, 32)), AX, ALU.add))
            op(v.tensor_copy(at(M_IDX + 256, (1, OVER)).bitcast(I32), at(R_TM2, (1, OVER))), False)
            c.do(v.tensor_copy(at(M_IDX + 256 + OVER, (1, 1)).bitcast(I32), at(inc + 31, (1, 1))), idx_ready)
            dve.wait_ge(ld["tb"], 16)
            tb, tf, tg = M_IDX, M_IDX + 64, M_IDX + 128
            op(v.tensor_copy(at(tf, (1, BLK)), at(tb, (1, BLK)).bitcast(U32)))
            op(v.tensor_scalar(at(tg, (1, BLK)), at(tf, (1, BLK)), float(T), -float(T), ALU.is_ge, ALU.mult))
            op(v.tensor_tensor(at(tf, (1, BLK)), at(tf, (1, BLK)), at(tg, (1, BLK)), ALU.add))
            c.do(v.tensor_copy(at(tg, (1, BLK)).bitcast(U32), at(tf, (1, BLK))), idx_ready)

            def hidden(r, k):
                wait_pos(dve, th_ready, r, k, 1)
                g, u = pat(1, (k % 2) * 512, (1, 256)), pat(1, (k % 2) * 512 + 256, (1, 256))
                th, hid = at(M_THE + (k % 2) * 256, (1, 256)), at(M_HID + (k % 2) * 256, (1, 256))
                v.scalar_tensor_tensor(th, th, 1.0, g, ALU.add, ALU.mult).then_inc(t_ready, 1)
                wait_pos(dve, t_ready, r, k, 1)
                wait_pos(dve, hT_ps, r, k, -1)
                v.tensor_tensor(hid, th, u, ALU.mult).then_inc(hid_ready, 1)

            def hidden_turned(r, k):
                wait_pos(dve, hT_ps, r, k, 1)
                wait_pos(dve, y_ps, r, k, -1)
                v.tensor_copy(at(M_HT + (k % 2) * 256, (1, 256)), pat(2, 0, (1, 256))).then_inc(hT_ready, 1)

            def result(r, k):
                wait_pos(dve, y_ps, r, k, 1)
                prev = 32 * r + 16 * (k // 2)
                if not (isinstance(prev, int) and prev <= 0):
                    dve.wait_ge(y_sent[k % 2], prev)
                v.tensor_copy(at(M_YO + (k % 2) * 1024, (1, 1024)), pat(3, 0, (1, 1024))).then_inc(y_copied, 1)

            def body(r, k, first=False):
                pr, pk = (r, k - 1) if k else (r - 1, 3)
                if not first:
                    hidden_turned(pr, pk)
                hidden(r, k)
                if not first:
                    result(pr, pk)

            def blocks(r0, r1):
                for k in range(4):
                    body(r0, k, first=(k == 0))
                with dve.Fori(r0 + 1, r1) as r:
                    for k in range(4):
                        body(r, k)
                hidden_turned(r1 - 1, 3)
                result(r1 - 1, 3)

            blocks(0, NE // 4)
            with dve.If(overflow(dve) > 0):
                blocks(NE // 4, BLK // 4)

            def combine(t):
                R = ROWS[t]
                h = at(O_H + t * D, (1, D), pn=R)
                dve.wait_ge(y_ld[t], 32)
                op(v.scalar_tensor_tensor(h, at(A_WG + t * 2048, (1, D), pn=R), at(R_W0 + t, (1, 1), pn=R), h, ALU.mult, ALU.add))
                c.do(v.scalar_tensor_tensor(h, at(A_WG + t * 2048 + D, (1, D), pn=R), at(R_W1 + t, (1, 1), pn=R), h,
                                            ALU.mult, ALU.add), y_done)

            def finish(t):
                R = ROWS[t]
                h = at(O_H + t * D, (1, D), pn=R)
                ss = at(R_SS + 8 + t, (1, 1), pn=R)
                dve.wait_ge(ssf, t + 1)
                op(v.tensor_scalar(ss, ss, 1.0 / D, EPS, ALU.mult, ALU.add))
                inverse(ss)
                c.do(v.scalar_tensor_tensor(h, h, ss, at(M_GF, (1, D), pn=R), ALU.mult, ALU.mult), y_done)

            for t in range(TT):
                combine(t)
                finish(t)

        @block.gpsimd
        def _(pool):
            stores = [0]

            def store(dst, src):
                pool.dma_start(dst, src).then_inc(out_st, 16)
                stores[0] += 1

            pool.wait_ge(zero_set, 1)
            pool.dma_start(k_d[:, :, 0:112].rearrange("(a g) h c -> (g h) a c", g=8),
                           at(A_ZERO, (0, 4), (1, 112))).then_inc(kz_out, 16)
            for t in range(TT):
                R = ROWS[t]
                pool.wait_ge(u_sb, t + 1)
                pool.dma_start(u_d[t * 128:t * 128 + R, :], at(A_US + t * 512, (1, 512), pn=R)).then_inc(u_out, 16)
            pool.wait_ge(u_out, 16 * TT)
            pool.dma_start(at(A_UC, (1, 4096), pn=NC), u_d[:, :].rearrange("(c j) f -> c (j f)", j=L)).then_inc(ld["uc"], 16)
            pool.wait_ge(kv_sb, TT)
            pool.dma_start(kvs_d[:, :], at(O_KV + 4 * 256, (1, 256), pn=64)).then_inc(kvs_out, 16)
            for i in range(8):
                pool.wait_ge(ks_sb, i + 1)
                pool.dma_start(k_d[4 * i:4 * i + 4, :, 112:240].rearrange("g h c -> h g c"),
                               at(A_KS + (i % 4) * 512, (128, 4), (1, 128), pn=CH)).then_inc(k_out[i % 4], 16)
            for n in range(4):
                pool.wait_ge(k_out[n], 32)
            pool.dma_start(at(A_S + 64 * G, (SLOTS * G, 2), (1, NB * G)), h0).then_inc(ld["h0"], 16)
            filled(pool, "B3")
            for s in range(L):
                pool.dma_start(at(A_VT, (128, G), (1, 128), p0=CH * s, pn=CH),
                               k_d[:, :, 112 - CH * s:240 - CH * s].rearrange("g h c -> h g c")).then_inc(ld["T"], 16)
            store(out_kvp, at(O_KV + 3 * 256, (1, 256)))
            pool.wait_ge(scanned, 1)
            store(out_ssm, at(A_S + 72 * G, (1, 9 * G)))
            filled(pool, "Y3")
            pool.dma_start(at(A_MK, (1, KT * MEM)), memT).then_inc(ld["memT"], 16)
            pool.wait_ge(kvs_out, 16)
            pool.dma_start(at(A_SKT, (136, NB), (1, 128)), skT[:, :, :]).then_inc(ld["samp"], 16)
            pool.dma_start(at(A_SB, (1, 272)), sbias).then_inc(ld["samp"], 16)
            pool.wait_ge(kT_sb, 1)
            pool.dma_start(at(A_SKT + 128, (136, NB), (1, NQ)), at(O_KT + 512, (NQ, NB), (1, NQ))).then_inc(ld["samp"], 16)
            pool.wait_ge(zc_ready, 4)
            filled(pool, "Z3")
            pool.dma_start(at(A_BI, (1, 2048)), bias).then_inc(ld["bias"], 16)
            pool.dma_start(at(A_SV, (1, 1024)), sv).then_inc(ld["svn"], 16)
            pool.wait_ge(ld["svn"], 16)
            pool.dma_start(at(A_SVN, (128, NB), (1, 128), pn=NQ),
                           kvs_d[:, 128:256].rearrange("(b q) f -> q b f", q=NQ)).then_inc(svn_ready, 16)
            store(out_sk[:, 0:120, :], cache_k[:, 8:128, :])
            store(out_sv[:, 0:120, :], cache_v[:, 8:128, :])
            store(out_sk[:, 120:128, :], kvs_d[:, 0:128].rearrange("(b q) f -> b q f", q=NQ))
            store(out_sv[:, 120:128, :], kvs_d[:, 128:256].rearrange("(b q) f -> b q f", q=NQ))
            pool.wait_ge(mkv_sb, 4)
            store(out_mem.rearrange("(t p) f -> p t f", p=128), at(A_MKV, (1024, 2), (1, 1024)))
            def load_k(b):
                if b >= 2:
                    pool.wait_ge(mk_used, b - 1)
                pool.dma_start(at(A_MK + (b % 2) * 1024, (1, 1024)), mkT[b]).then_inc(ldmk[b % 2], 16)

            def load_v(b):
                if b >= 2:
                    pool.wait_ge(mv_used, b - 1)
                pool.dma_start(at(A_MV + (b % 2) * 1024, (1, 1024)), mv[b]).then_inc(ldmv[b % 2], 16)

            for b in range(2):
                load_k(b)
                load_v(b)
            for b in range(2, NB):
                load_k(b)
            for b in range(2, NB):
                load_v(b)
            filled(pool, "pc7")
            for t in range(TT):
                R = ROWS[t]
                pool.dma_start(at(O_H + t * D, (1, D), pn=R), x[t * 128:t * 128 + R, :]).then_inc(ld["x"], 16)
            pool.wait_ge(m_ready, 8)
            pool.dma_start(at(M_G2, (1, 2048)), bass.AP(rows.tensor, rows.offset, [[0, P], [1, 2048]])).then_inc(ld["rows"], 16)
            pool.dma_start(at(M_WR, (1, 324)), wr).then_inc(ld["wr"], 16)
            pool.dma_start(at(R_TRI, (1, N_CONST - 128)), const[:, 128:N_CONST]).then_inc(ld["rows"], 16)
            pool.wait_ge(ld["rows"], 32)
            c = Chain(pool, pool_step)
            c.do(nc.gpsimd.tensor_copy(at(M_IDX, (1, BLK)).bitcast(U32), at(R_NOROW, (1, BLK))))
            c.settle()
            pool.dma_start(tab_d[:, :].rearrange("(p b) o -> p (b o)", b=BLK), at(M_IDX, (1, BLK)).bitcast(U32))\
                .then_inc(tab_set, 16)
            filled(pool, f"w3{TT - 1}")
            nc.gpsimd.memset(at(M_XG, (1, 2048)), 0.0).then_inc(xg_clear, 1)
            for t in range(TT):
                R = ROWS[t]
                pool.wait_ge(x2_ready, t + 1)
                pool.dma_start(x2_d[t * 128:t * 128 + R, :], at(M_X2 + (t % 2) * 1024, (1, D), pn=R)).then_inc(x2_out[t % 2], 16)
            pool.wait_ge(slot_ready, 1)
            pool.wait_ge(tab_set, 16)
            for k in range(2):
                for t in range(TT):
                    R = ROWS[t]
                    pool.indirect_dma_start(
                        out=tab_d[:, :], out_offset=bass.IndirectOffsetOnAxis(at(R_SL + k * TT + t, (1, 1), pn=R).bitcast(U32), 0),
                        in_=at(R_PI + k * TT + t, (1, 1), pn=R).bitcast(U32), in_offset=None).then_inc(scat, 16)
            pool.wait_ge(scat, 160)
            pool.dma_start(at(M_IDX, (1, BLK)).bitcast(U32), tab_d[:, :].rearrange("(p b) o -> p (b o)", b=BLK))\
                .then_inc(ld["tb"], 16)
            pool.wait_ge(idx_ready, 2)
            pool.wait_ge(x2_out[0], 48)
            pool.wait_ge(x2_out[1], 32)
            pool.wait_ge(xg_clear, 1)

            def gather(r, k):
                i = 4 * r + k
                wait_pos(pool, xt_ps, r, k, -1)
                pool.indirect_dma_start(
                    out=at(M_XG + (k % 2) * 1024, (1, D)), out_offset=None, in_=x2_d[:, :],
                    in_offset=bass.IndirectOffsetOnAxis(at(M_IDX + 128 + i, (1, 1)).bitcast(U32), 0),
                    bounds_check=T - 1, oob_is_err=False).then_inc(xg_ready[k % 2], 16)

            def scatter(r, k):
                i = 4 * r + k
                wait_pos(pool, y_copied, r, k, 1)
                pool.indirect_dma_start(
                    out=y_d[:, :], out_offset=bass.IndirectOffsetOnAxis(at(M_IDX + i, (1, 1)).bitcast(U32), 0),
                    in_=at(M_YO + (k % 2) * 1024, (1, D)), in_offset=None,
                    bounds_check=PAIRS - 1, oob_is_err=False).then_inc(y_sent[k % 2], 16)

            def blocks(i0, i1):
                gather(i0 // 4, 0)
                gather(i0 // 4, 1)
                for i in range(i0, i1):
                    if i + 2 < i1:
                        gather((i + 2) // 4, (i + 2) % 4)
                    if i > i0:
                        scatter((i - 1) // 4, (i - 1) % 4)
                scatter(i1 // 4 - 1, 3)
                for s in range(2):
                    pool.wait_ge(y_sent[s], 16 * (i1 // 2))

            blocks(0, NE)
            with pool.If(overflow(pool) > 0):
                blocks(NE, BLK)
            for t in range(TT):
                R = ROWS[t]
                for k in range(2):
                    pool.dma_start(at(A_WG + t * 2048 + k * D, (1, D), pn=R),
                                   y_d[k * T + t * 128:k * T + t * 128 + R, :]).then_inc(y_ld[t], 16)
            for t in range(TT):
                R = ROWS[t]
                pool.wait_ge(y_done, 2 * t + 2)
                store(out_y[t * 128:t * 128 + R, :], at(O_H + t * D, (1, D), pn=R))
            pool.wait_ge(out_st, 16 * stores[0])


def columns_block(w, cols):
    w = w[:, cols]
    return w.reshape(-1, P, w.shape[1]).transpose(1, 0, 2).reshape(P, -1)


def kernel(**inputs):
    import numpy as np
    import concourse.bacc as bacc
    from concourse.bass_utils import run_bass_kernel_spmd

    a = {k: np.asarray(v) for k, v in inputs.items()}
    f32 = np.float32
    cat, tile = np.concatenate, np.tile

    def dup(v):
        return cat([v.T, v.T])

    heads = np.arange(512).reshape(8, 64)
    qcols = cat([heads[[m, m + 4]].reshape(-1) for m in range(4)])
    small = cat([
        dup(a["lam_re"][0]), dup(a["lam_im"][0]), tile(a["log_dt"][0], (P, 1)),
        a["norm1_g"][0].reshape(KT, P).T, a["mem_norm_g"][0].reshape(KT, P).T, a["b_glu"][0].reshape(4, P).T,
        tile(a["d_skip"][0].reshape(G, CH).T, (8, 1)), tile(a["sinks"][0], (P, 1)),
        tile(np.repeat(a["sinks"][0].reshape(2, 4).T, NQ, axis=0), (4, 1))], axis=1)
    bm_re, bm_im = (a[n][0].transpose(1, 0, 2).reshape(ST, -1) for n in ("bm_re", "bm_im"))
    cm_re, cm_im = (a[n][0].transpose(2, 0, 1).reshape(ST, -1) for n in ("cm_re", "cm_im"))
    ssm = cat([cat([m, m]) for m in (bm_re, bm_im, cm_re, cm_im)], axis=1)
    s_re, s_im = (a[n][0].transpose(2, 0, 1).reshape(ST, -1) for n in ("state_ssm_re", "state_ssm_im"))
    h0 = np.stack([cat([s_re, s_im]), cat([s_im, s_re])], axis=1)
    x = cat([a["x_prompt"][0], a["x_sample"].reshape(-1, D)])
    xT = x.reshape(T, KT, P).transpose(2, 1, 0).reshape(P, -1)
    memT = a["mem_prompt"][0].reshape(MEM, KT, P).transpose(2, 1, 0).reshape(P, -1)

    w_in, w_kv = a["w_in"][0], a["w_mem_kv"][0]
    at = np.cumsum([0, 512, 512, 256, 512])
    ar = np.arange
    blocks = [columns_block(w_in, ar(256 * i, 256 * i + 256)) for i in range(2)]
    blocks += [columns_block(w_in, ar(at[2], at[3]))]
    blocks += [columns_block(w_in, at[1] + qcols[256 * i:256 * i + 256]) for i in range(2)]
    gates = at[4]
    blocks += [columns_block(w_in, ar(gates + 256 * i, gates + 256 * i + 256)) for i in range(4)]
    blocks += [columns_block(w_in, ar(at[3] + 256 * i, at[3] + 256 * i + 256)) for i in range(2)]
    blocks += [columns_block(w_kv, ar(256 * i, 256 * i + 256)) for i in range(4)]
    blocks += [columns_block(a["w_glu"][0], ar(512))]
    branch = [a["w_br_ssm"][0], a["w_br_swa"][0][qcols], a["w_br_mem"][0]]
    for d in range(KT):
        c = ar(128 * d, 128 * d + 128)
        blocks += [columns_block(w_in, cat([gates + D + c, gates + 2 * D + c]))]
        blocks += [cat([columns_block(w, c) for w in branch] + [np.zeros((P, 512), f32)], axis=1)]
    blocks += [columns_block(a["w_out"][0], ar(256 * i, 256 * i + 256)) for i in range(4)]
    wstream = np.stack(blocks)
    gu = cat([a["w_e_gate"][0], a["w_e_up"][0]], axis=2).reshape(NE, KT, P, 2 * DE).transpose(0, 2, 1, 3).reshape(NE, P, -1)
    dn = a["w_e_down"][0].reshape(NE, 2, P, D).transpose(0, 2, 1, 3).reshape(NE, P, -1)
    wexp = cat([gu, dn], axis=2)

    n = ar(P)
    far = 16 + (np.log(np.maximum(n, 1).astype(f32) / f32(16)) / f32(np.log(8.0)) * f32(16)).astype(np.int32)
    bucket = np.where(n < 16, n, np.minimum(far, 31))
    table = cat([a["rel_table"], np.full((1, 8), -1e30, f32)])

    def biases(rows, keys):
        dist = rows[:, None] + P - keys[None, :]
        return table[np.where((dist >= 0) & (dist < P), bucket[np.clip(dist, 0, P - 1)], 32)]

    bias = biases(ar(P), ar(256)).transpose(0, 2, 1).reshape(P, -1)
    sb_ = biases(ar(NQ), ar(136)).transpose(0, 2, 1).reshape(NQ, 2, 4, 136)
    sbias = tile(sb_.transpose(2, 0, 1, 3).reshape(32, -1), (4, 1))

    ck, cv = (a[m][0].reshape(NB, P, P) for m in ("cache_swa_k", "cache_swa_v"))
    skT = ck.transpose(2, 0, 1)
    sv = cv.transpose(1, 0, 2).reshape(P, -1)
    mkT = a["cache_mem_k"][0].transpose(0, 3, 2, 1).reshape(NB, P, -1)
    mv = a["cache_mem_v"][0].reshape(NB, 2, P, 512).transpose(0, 2, 1, 3).reshape(NB, P, -1)
    pid = cat([k * T + t * 128 + ar(P)[:, None] for k in range(2) for t in range(TT)], axis=1)
    const = cat([np.eye(P), np.triu(np.ones((P, P)), 1), tile(ar(32), (P, 1)), pid, np.full((P, BLK), NOROW)], axis=1)
    rows = cat([a["norm2_g"][0], a["final_norm_g"]])[None]
    wr = cat([a["w_rg"][0], a["w_rexp"][0]], axis=1)
    wr = cat([columns_block(wr, ar(36)), tile(cat([a["b_rg"][0], a["b_rexp"][0]]), (P, 1))], axis=1)

    ins = dict(small=small, ssm=ssm, h0=h0, xT=xT, x=x, memT=memT, wstream=wstream, wexp=wexp, bias=bias, sbias=sbias,
               skT=skT, sv=sv, mkT=mkT, mv=mv, cache_k=ck, cache_v=cv, const=const.astype(f32), rows=rows, wr=wr)
    outs = dict(out_y=(T, D), out_kvp=(P, 256), out_mem=(MEM, 1024), out_sk=(NB, P, P), out_sv=(NB, P, P),
                out_ssm=(P, 9 * G))
    nc = bacc.Bacc("TRN2", target_bir_lowering=False, num_devices=1)
    arrays, args = {}, {}
    for k, v in ins.items():
        arrays["in_" + k] = np.ascontiguousarray(v)
        args[k] = nc.dram_tensor("in_" + k, v.shape, F32, kind="ExternalInput").ap()
    for k, shape in outs.items():
        args[k] = nc.dram_tensor(k, shape, F32, kind="ExternalOutput").ap()
    build(nc, **args)
    r = run_bass_kernel_spmd(nc, [arrays], core_ids=[0]).results[0]
    y, kvp, mem, ssm_o = r["out_y"], r["out_kvp"], r["out_mem"], r["out_ssm"].reshape(2, ST, 9, G)
    st = ssm_o.transpose(0, 2, 3, 1)
    return (y[:NP_].reshape(1, NP_, D), y[NP_:].reshape(NB, NQ, D),
            kvp[:, :P].reshape(1, 1, P, 2, 64), kvp[:, P:].reshape(1, 1, P, 2, 64),
            st[0, 0][None, None], st[1, 0][None, None],
            mem[:, :512].reshape(1, 1, MEM, MH, 128), mem[:, 512:].reshape(1, 1, MEM, MH, 128),
            r["out_sk"].reshape(1, NB, P, 2, 64), r["out_sv"].reshape(1, NB, P, 2, 64),
            st[0, 1:][None], st[1, 1:][None])
```

```python
from contextlib import ExitStack

import concourse.bass as bass
from concourse import mybir

F32 = mybir.dt.float32
F32R = mybir.dt.float32r
U32 = mybir.dt.uint32
I32 = mybir.dt.int32
ALU = mybir.AluOpType
ACT = mybir.ActivationFunctionType
AX = mybir.AxisListType.X

P = 128
D = 1024
KT = D // P
NP_, NB, NQ = 512, 8, 8
T = NP_ + NB * NQ
TT = 5
ROWS = [128, 128, 128, 128, 64]
TH = T // 2
G, CH, ST = 32, 16, 64
L = 8
NC = T // L
PC = NP_ // L
MEM, MH = 256, 4
MEM_SCALE = float(128) ** -0.5
SWA_SCALE = 0.125
NE, DE = 32, 256
PAIRS = 2 * T
RB = 64
OVER = 20
BLK = NE + OVER
NOROW = 4096
WB = 2048
NBLOCKS = 34
RING = 4
EPS = 1e-6
TWO_PI_A, TWO_PI_B, TWO_PI_C = 6.28125, 0.0019354820251464844, -1.7484555314695172e-07
MAGIC = 12582912.0

O_W = 0
O_X = 8192
O_TH = 12800
O_Z = 17408
O_O = 19712
O_H = O_Z
O_Q = 24320
O_UG = 26624
O_KT = 28928
O_KV = 29504
O_RS = 30784
O_ID = 31360
O_ONE = 31488
O_SM = 31616
O_PW = 32640
O_A = 34368
WORDS = 53136
REGIONS = [(0, O_TH), (O_TH, O_A), (O_A, WORDS)]

S_LR, S_LI, S_LD, S_G1, S_GM, S_BG, S_DS, S_SK, S_SS = 0, 32, 64, 96, 104, 112, 116, 148, 156
N_SMALL = 158
S_T = 160
S_A8 = 640
S_SC = 768
S_ST = 896

A_VT, A_Y, A_UC, A_TAIL = O_A, O_A + 4096, O_A + 8704, O_A + 12800
A_US = A_TAIL
A_KS = A_TAIL + 2560
A_S = A_TAIL
SLOTS = PC + NB + 1 + NB
A_ZERO = A_TAIL + 5184
A_UP = A_TAIL
A_MK, A_MV = O_A, O_A + 2048
A_MKV, A_KMT, A_SB, A_SKT = O_A + 4096, O_A + 6144, O_A + 7168, O_A + 7440
A_SC, A_PT, A_BI, A_SV, A_SVN, A_QZ = O_A + 8528, O_A + 10576, O_A + 12624, O_A + 14672, O_A + 15696, O_A + 16720
A_THG = O_A + 8704
O_QZS = A_QZ
O_QM = O_O + 2304
A_WG = O_A

M_X2 = O_X
M_X2T = O_X + 2048
M_G2, M_GF, M_WR, M_BR = O_TH, O_TH + 1024, O_TH + 2048, O_TH + 2336
M_R = O_TH + 2372
M_XG, M_XGT = 22528, 24576
M_THE, M_HID, M_HT, M_YO = 26624, 27136, 27648, 28160
M_XGL = [M_G2, O_PW]
M_HTL = 12288
E_GU, E_GH, E_DL = O_A, O_A + 8192, O_A + 16384
E_D, E_DH, E_GL = 0, 4096, 8192
assert E_DL + 2048 <= WORDS and M_HTL + 512 <= O_TH
M_IDX = 30208
M_JUNK = O_PW
A_GL = A_TAIL
C_TRI, C_IOTA, C_PF, C_NOROW, N_CONST = 128, 256, 288, 298, 298 + BLK
_at = [M_R]


def _take(n):
    _at[0] += n
    return _at[0] - n


R_TRI, R_IOTA, R_PF, R_NOROW = _take(128), _take(32), _take(10), _take(BLK)
R_LG, R_GP, R_GM, R_IX = _take(36 * TT), _take(8 * TT), _take(8 * TT), _take(8 * TT)
R_GX, R_GE, R_OG, R_EP, R_EM, R_ED = _take(TT), _take(4 * TT), _take(4 * TT), _take(8 * TT), _take(8 * TT), _take(TT)
R_EK, R_MK, R_M, R_TM = _take(2 * TT), _take(64 * TT), _take(32 * TT), _take(32 * OVER)
R_RK, R_NB, R_RA, R_OB, R_FL, R_OV = _take(192), _take(96), _take(10), _take(10), _take(10), _take(10)
R_SL, R_PI, R_W0, R_W1, R_SS = _take(10), _take(10), _take(TT), _take(TT), _take(16)
R_MC = R_RK
assert _at[0] <= O_Z


def plan_jobs():
    jobs = ["ssq"] + [f"u{t}" for t in range(TT)] + [f"kv{t}" for t in range(TT)] + ["kT"]
    jobs += [f"q{m}" for m in range(4)] + [f"K{i}" for i in range(8)]
    jobs += [f"VT{i}" for i in range(4)] + [f"U{i}" for i in range(4)] + [f"B{i}" for i in range(4)]
    jobs += [f"g0{d}" for d in range(8)] + [f"qm{m}" for m in range(4)] + [f"Y{i}" for i in range(4)]
    jobs += [f"g{j}" for j in range(EARLY)]
    jobs += [f"Z{i}" for i in range(4)] + ["ssqm"] + [f"mm{i}" for i in range(4)] + ["kmT"]
    jobs += [f"G{m}" for m in range(4)]
    n = len(UNITS)
    jobs += ["S0"]
    for i in range(n + 1):
        jobs += [f"S{i + 1}"] if i + 1 < n else []
        jobs += [f"O{i - 1}"] if i >= 1 else []
        jobs += pieces_at(i)
        jobs += [f"T{i}"] if i < n else []
    jobs += pieces_at(n + 1)
    jobs += [f"w{b}{t}" for b in range(4) for t in range(TT)]
    jobs += ["x2T0"] + [j for t in range(TT) for j in ([f"x2T{t + 1}"] if t + 1 < TT else []) + [f"lg{t}"]] + ["rk"]
    return {j: i for i, j in enumerate(jobs)}


EARLY = 4
PIECES = [f"c{d}" for d in range(8)] + [f"g{j}{h}" for j in range(EARLY, EARLY + 3) for h in "ab"]
PIECES += [f"p{j}" for j in range(EARLY)]
for _j in range(EARLY, 16):
    PIECES += [f"p{_j}"] + ([f"g{_j + 3}a", f"g{_j + 3}b"] if _j + 3 < 16 else [])
FILL = [2, 2, 1, 1, 1, 1, 2, 1, 1, 2, 2, 2, 2, 2, 2, 0]


def pieces_at(step):
    first = sum(FILL[:step])
    return PIECES[first:first + FILL[step]] if step < len(FILL) else PIECES[first:]


def piece_block(piece):
    kind, n = piece[0], int(piece[1:].rstrip("ab"))
    return kind, n // (2 if kind == "g" else 4)


BRANCH_BLOCKS = list(dict.fromkeys(piece_block(q) for q in PIECES))

UNITS = [("w", qt, kv) for qt in range(4) for kv in range(2)]
UNITS += [("ws", 0, 0)] + [("m", qt, 0) for qt in range(4)] + [("ms", 0, 0), ("ms", 1, 0)]
J = plan_jobs()


def build(nc, small, ssm, h0, xT, x, memT, wstream, wexp, bias, sbias, skT, sv, mkT, mv, cache_k, cache_v,
          const, rows, wr, out_y, out_kvp, out_mem, out_sk, out_sv, out_ssm):
    u_d = nc.dram_tensor("u_rows", [T, 512], F32)
    k_d = nc.dram_tensor("k_pad", [G, CH, 240], F32)
    kvs_d = nc.dram_tensor("kv_sample", [64, 256], F32)
    x2_d = nc.dram_tensor("xn2_rows", [T, D], F32)
    y_d = nc.dram_tensor("expert_rows", [PAIRS, D], F32)
    tab_d = nc.dram_tensor("pair_table", [RB * BLK, 1], U32)

    def regions(name, dtype):
        tensors = []
        with ExitStack() as stack:
            for i, (start, end) in enumerate(REGIONS):
                tensors.append(stack.enter_context(nc.sbuf_tensor(f"{name}{i}", [P, end - start], dtype)))
        return tensors

    sb, sr = regions("sb", F32), regions("sr", F32R)

    with ExitStack() as ctx:
        def sem(name):
            return ctx.enter_context(nc.semaphore(name))

        ps = [ctx.enter_context(nc.psum_tensor(f"ps{i}", [P, 1024], F32)) for i in range(4)]

        def view(tensors, off, dims, p0=0, pn=P):
            i = next(i for i, (_, end) in enumerate(REGIONS) if off < end) if isinstance(off, int) else 2
            start, end = REGIONS[i]
            if isinstance(off, int):
                assert off + sum(s * (n - 1) for s, n in dims if s > 0) < end
            return bass.AP(tensors[i], (off - start) + p0 * (end - start), [[end - start, pn]] + [[s, n] for s, n in dims])

        def at(off, *dims, p0=0, pn=P):
            return view(sb, off, dims, p0, pn)

        def r32(off, n):
            return view(sr, off, [(1, n)])

        def r32t(off, n):
            return view(sr, off, [(RB, n), (1, RB)])

        def pat(i, off, *dims, p0=0, pn=P):
            return bass.AP(ps[i], p0 * 1024 + off, [[1024, pn]] + [[s, n] for s, n in dims])

        ident = at(O_ID, (1, 128))

        ps_ready = sem("ps_ready")
        ps_free = [sem(f"ps_free{i}") for i in range(4)]
        vec_step, act_step, pool_step = sem("vec_step"), sem("act_step"), sem("pool_step")
        w_ready = [sem(f"w_ready{i}") for i in range(RING)]
        w_used = sem("w_used")
        ld = {n: sem("ld_" + n) for n in ("small", "ssm", "xT0", "xT1", "const", "h0", "memT", "bias", "samp", "svn", "uc", "T",
                                          "x", "rows", "wr", "tab", "tb")}
        x_sq, ones_set, xn_ready = sem("x_sq"), sem("ones_set"), sem("xn_ready")
        u_sb, kv_sb, kT_sb, q_sb = sem("u_sb"), sem("kv_sb"), sem("kT_sb"), sem("q_sb")
        u_out, kvs_out, kz_out = sem("u_out"), sem("kvs_out"), sem("kz_out")
        exp_ssm, trig, ang_ready, par_ready = sem("exp_ssm"), sem("trig"), sem("ang_ready"), sem("par_ready")
        zero_set, y_built, vt_built = sem("zero_set"), sem("y_built"), sem("vt_built")
        ks_sb, vt_sb, ug_sb, b_sb = sem("ks_sb"), sem("vt_sb"), sem("ug_sb"), sem("b_sb")
        scan, scanned = sem("scan"), sem("scanned")
        yc_sb, gelu_in, gelu_th, zc_ready, z_sb = sem("yc_sb"), sem("gelu_in"), sem("gelu_th"), sem("zc_ready"), sem("z_sb")
        qm_sb, memn, memsq, mkv_sb, kmT_sb, thg_sb, zz_ready = (sem(n) for n in (
            "qm_sb", "memn", "memsq", "mkv_sb", "kmT_sb", "thg_sb", "zz_ready"))
        qz_ready, qzs_ready = sem("qz_ready"), sem("qzs_ready")
        stat_ready, exp_ready, p_ready, pt_ready, o_sb = (sem(n) for n in (
            "stat_ready", "exp_ready", "p_ready", "pt_ready", "o_sb"))
        ldmk, ldmv = [sem("ldmk0"), sem("ldmk1")], [sem("ldmv0"), sem("ldmv1")]
        gate_sb, gate_used, h_ready = sem("gate_sb"), sem("gate_used"), sem("h_ready")
        ss2, x2_ready, x2T_sb, lg_sb, gate_d, gate_e, m_onehot, rk_sb, slot_ready, tab_set, idx_ready = (
            sem(n) for n in ("ss2", "x2_ready", "x2T_sb", "lg_sb", "gate_d", "gate_e", "m_onehot", "rk_sb",
                             "slot_ready", "tab_set", "idx_ready"))
        xg_clear = sem("xg_clear")
        scat = sem("scat")
        mk_used, mv_used, t_ready, svn_ready, up_sb, ms_ready, root_ready = sem("mk_used"), sem("mv_used"), sem("t_ready"), sem("svn_ready"), sem("up_sb"), sem("ms_ready"), sem("root_ready")
        k_out = [sem(f"k_out{i}") for i in range(4)]
        x2_out = [sem(f"x2_out{i}") for i in range(2)]
        y_ld = [sem(f"y_ld{i}") for i in range(TT)]
        wg_ready = [sem(f"wg_ready{i}") for i in range(4)]
        wd_ready = [sem(f"wd_ready{i}") for i in range(2)]
        gu_hi, gu_lo, d_hi, d_lo = sem("gu_hi"), sem("gu_lo"), sem("d_hi"), sem("d_lo")
        xg_ready = [sem(f"xg_ready{i}") for i in range(2)]
        y_sent = [sem(f"y_sent{i}") for i in range(2)]
        xt_ps, xT_hi, xT_lo, gu_ps, th_ready, hid_ready, hT_ps, hT_hi, hT_lo, y_ps, y_copied = (
            sem(n) for n in ("xt_ps", "xT_hi", "xT_lo", "gu_ps", "th_ready", "hid_ready", "hT_ps", "hT_hi", "hT_lo",
                             "y_ps", "y_copied"))
        ssf, y_sum, y_done = sem("ssf"), sem("y_sum"), sem("y_done")
        out_st = sem("out_st")
        block = ctx.enter_context(nc.Block())

        def pair(job):
            return J[job] % 4

        def filled(eng, job):
            eng.wait_ge(ps_ready, J[job] + 1)

        def free_count(job):
            return J[job] // 4 + 1

        def wait_pos(eng, sem_, r, k, d):
            if not isinstance(r, int) or 4 * r + k + d > 0:
                eng.wait_ge(sem_, r * 4 + (k + d))

        def wait_half(eng, sem_, r, k, d):
            if not isinstance(r, int) or 8 * r + 2 * k + d > 0:
                eng.wait_ge(sem_, r * 8 + (2 * k + d))

        def gate_slot(j):
            return O_UG + j * T if j < EARLY else O_PW + (j % 3) * T

        def overflow(eng):
            eng.wait_ge(idx_ready, 1)
            return eng.value_load(at(M_IDX + 256 + OVER, (1, 1), pn=1).bitcast(I32), min_val=0, max_val=OVER)

        class Chain:

            def __init__(self, eng, step):
                self.eng, self.step, self.count, self.last = eng, step, {}, None

            def do(self, ins, to=None, value=None):
                to = self.step if to is None else to
                ins.then_inc(to, 1)
                self.count[id(to)] = self.count.get(id(to), 0) + 1
                self.last = (to, self.count[id(to)] if value is None else value)

            def free(self, ins, job):
                self.do(ins, ps_free[pair(job)], free_count(job))

            def settle(self):
                self.eng.wait_ge(*self.last)

        @block.sync
        def _(sp):
            sp.wait_ge(ld["xT1"], 16)
            for s in range(RING):
                sp.dma_start(at(O_W + s * WB, (1, WB)), wstream[s]).then_inc(w_ready[s], 16)
            with sp.Fori(1, NBLOCKS // RING) as r:
                for s in range(RING):
                    sp.wait_ge(w_used, r * RING + (s + 1 - RING))
                    sp.dma_start(at(O_W + s * WB, (1, WB)), wstream[r * RING + s]).then_inc(w_ready[s], 16)
            for b in range(NBLOCKS // RING * RING, NBLOCKS):
                sp.wait_ge(w_used, b + 1 - RING)
                sp.dma_start(at(O_W + (b % RING) * WB, (1, WB)), wstream[b]).then_inc(w_ready[b % RING], 16)

            def gate_up(e, k, c):
                sp.dma_start(at(E_GU + (k % 2) * 4096 + c * 2048, (1, 2048)), wexp[e, :, c * 2048:c * 2048 + 2048])\
                    .then_inc(wg_ready[k % 2 * 2 + c], 16)

            def down(e, k):
                sp.dma_start(at(E_D + (k % 2) * 2048, (1, 2048)), wexp[e, :, 4096:6144]).then_inc(wd_ready[k % 2], 16)

            def load(e, r, k):
                for c in range(2):
                    wait_half(sp, gu_lo, r, k, c - 3)
                    gate_up(e, k, c)
                wait_pos(sp, d_lo, r, k, -1)
                down(e, k)

            filled(sp, f"O{len(UNITS) - 1}")
            sp.wait_ge(out_st, 16 * 7)
            sp.wait_ge(o_sb, len(UNITS))
            for k in range(2):
                gate_up(k, k, 0)
                gate_up(k, k, 1)
            sp.wait_ge(w_used, NBLOCKS)
            for k in range(2):
                down(k, k)
            for k in range(2, 4):
                load(k, 0, k)
            with sp.Fori(1, NE // 4) as r:
                for k in range(4):
                    load(r * 4 + k, r, k)
            with sp.If(overflow(sp) > 0):
                for j in range(OVER):
                    e = sp.value_load(at(M_IDX + 256 + j, (1, 1), pn=1).bitcast(I32), min_val=0, max_val=NE - 1)
                    load(e, (NE + j) // 4, (NE + j) % 4)

        @block.tensor
        def _(pe):
            blocks_taken = [0]

            def take(job):
                if J[job] >= 4:
                    pe.wait_ge(ps_free[pair(job)], J[job] // 4)

            def weights():
                b = blocks_taken[0]
                blocks_taken[0] += 1
                pe.wait_ge(w_ready[b % RING], 16 * (b // RING + 1))
                return O_W + (b % RING) * WB

            owed = []

            def signed(ins):
                if owed:
                    ins.then_inc(*owed.pop(0))
                return ins

            def mm(*a, **kw):
                return signed(nc.tensor.matmul(*a, **kw))

            def turn_tile(*a):
                return signed(nc.tensor.transpose(*a))

            def columns(job, w, wstep, src, kts):
                take(job)
                p = pair(job)
                for half in range(2):
                    for kt in range(kts):
                        last = mm(pat(p, half * 512, (1, TH)), at(w + kt * wstep, (1, 128)),
                                  at(src + kt * T + half * TH, (1, TH)), start=(kt == 0), stop=(kt == kts - 1))
                return last

            def rows_of(job, off, w, wn, n, src, t, kts=KT, wstep=None, srcw=T):
                wstep = wn if wstep is None else wstep
                R = ROWS[t]
                for kt in range(kts):
                    if job == "u0" and off == 0:
                        pe.wait_ge(xn_ready, kt + 1)
                    last = mm(pat(pair(job), off, (1, n), pn=R), at(src + kt * srcw + t * 128, (1, R)),
                              at(w + kt * wstep, (1, n)), start=(kt == 0), stop=(kt == kts - 1))
                return last

            pe.wait_ge(ones_set, 1)
            take("ssq")
            for kt in range(KT):
                if kt % 4 == 0:
                    pe.wait_ge(x_sq, kt // 4 + 1)
                for half in range(2):
                    last = mm(pat(pair("ssq"), half * 512, (1, TH)), at(O_ONE, (1, 128)),
                              at(A_Y + kt * T + half * TH, (1, TH)), start=(kt == 0), stop=(kt == KT - 1))
            last.then_inc(ps_ready, 1)
            wu = [weights(), weights()]
            for t in range(TT):
                take(f"u{t}")
                for i in range(2):
                    last = rows_of(f"u{t}", i * 256, wu[i], 256, 256, O_X, t)
                last.then_inc(ps_ready, 1)
            owed.append((w_used, 2))
            w = weights()
            for t in range(TT):
                take(f"kv{t}")
                rows_of(f"kv{t}", 0, w, 256, 256, O_X, t).then_inc(ps_ready, 1)
            owed.append((w_used, 1))
            pe.wait_ge(ld["const"], 16)
            pe.wait_ge(kv_sb, TT)
            take("kT")
            for t in range(TT):
                last = turn_tile(pat(pair("kT"), t * 128, (1, ROWS[t])),
                                           at(O_KV + t * 256, (1, 128), pn=ROWS[t]), at(O_ID, (1, ROWS[t]), pn=ROWS[t]))
            last.then_inc(ps_ready, 1)
            for m in range(4):
                if m % 2 == 0:
                    w = weights()
                columns(f"q{m}", w + (m % 2) * 128, 256, O_X, KT).then_inc(ps_ready, 1)
                if m % 2:
                    owed.append((w_used, 1))
            pe.wait_ge(y_built, 1)
            for i in range(8):
                take(f"K{i}")
                for n in range(4):
                    g = 4 * i + n
                    last = mm(pat(pair(f"K{i}"), n * 128, (1, 128), pn=CH), at(O_TH + 2048 + g * CH, (1, CH)),
                              at(A_Y + g * 144, (1, 128)), start=True, stop=True)
                last.then_inc(ps_ready, 1)
            pe.wait_ge(vt_built, 1)
            for i in range(4):
                take(f"VT{i}")
                for n in range(8):
                    last = turn_tile(pat(pair(f"VT{i}"), n * 128, (1, 128)),
                                               at(O_O + (8 * i + n) * 128, (1, 128)), ident)
                last.then_inc(ps_ready, 1)
            for i in range(4):
                pe.wait_ge(up_sb, i + 1)
                take(f"U{i}")
                for n in range(8):
                    g = 8 * i + n
                    last = turn_tile(pat(pair(f"U{i}"), (n // 4) * 512 + (n % 4) * NC, (1, NC)),
                                               at(A_UP + (i % 2) * 1024 + n * 128, (1, 128), pn=NC), at(O_ID, (1, NC), pn=NC))
                last.then_inc(ps_ready, 1)
            for i in range(4):
                pe.wait_ge(vt_sb, i + 1)
                pe.wait_ge(ug_sb, i + 1)
                take(f"B{i}")
                for n in range(8):
                    g = 8 * i + n
                    last = mm(pat(pair(f"B{i}"), (n // 4) * 512 + (n % 4) * NC, (1, NC)), at(A_VT + g * 128, (1, 128)),
                              at(O_UG + g * NC, (1, NC)), start=True, stop=True)
                last.then_inc(ps_ready, 1)
            for d in range(8):
                if d % 2 == 0:
                    w = weights()
                columns(f"g0{d}", w + (d % 2) * 128, 256, O_X, KT).then_inc(ps_ready, 1)
                if d % 2:
                    owed.append((w_used, 1))
            for m in range(4):
                if m % 2 == 0:
                    w = weights()
                columns(f"qm{m}", w + (m % 2) * 128, 256, O_X, KT).then_inc(ps_ready, 1)
                if m % 2:
                    owed.append((w_used, 1))
            pe.wait_ge(ld["T"], 16 * L)
            pe.wait_ge(scanned, 1)
            for i in range(4):
                take(f"Y{i}")
                for n in range(8):
                    g = 8 * i + n
                    dst = pat(pair(f"Y{i}"), n * 128, (1, 128), pn=NC)
                    mm(dst, at(O_UG + g * NC, (1, NC)), at(A_VT + g * 128, (1, 128)), start=True, stop=False)
                    last = mm(dst, at(A_S + g, (G, NC)), at(A_Y + g * 144 + CH, (1, 128)), start=False, stop=True)
                last.then_inc(ps_ready, 1)
            for j in range(EARLY):
                if j % 2 == 0:
                    w = weights()
                columns(f"g{j}", w + (j % 2) * 128, 256, O_X, KT).then_inc(ps_ready, 1)
                if j % 2:
                    owed.append((w_used, 1))
            for i in range(4):
                pe.wait_ge(zc_ready, i + 1)
                take(f"Z{i}")
                for j in range(L):
                    last = turn_tile(pat(pair(f"Z{i}"), (j // 4) * 512 + (j % 4) * NC, (1, NC)),
                                               at(A_UC + i * 1024 + j * 128, (1, 128), pn=NC), at(O_ID, (1, NC), pn=NC))
                last.then_inc(ps_ready, 1)
            pe.wait_ge(memsq, 1)
            take("ssqm")
            for kt in range(KT):
                last = mm(pat(pair("ssqm"), 0, (1, MEM)), at(O_ONE, (1, 128)), at(A_MV + kt * MEM, (1, MEM)),
                          start=(kt == 0), stop=(kt == KT - 1))
            last.then_inc(ps_ready, 1)
            pe.wait_ge(memn, 1)
            for i in range(4):
                w = weights()
                take(f"mm{i}")
                for t in range(2):
                    last = rows_of(f"mm{i}", t * 512, w, 256, 256, A_MK, t, srcw=MEM)
                last.then_inc(ps_ready, 1)
                owed.append((w_used, 1))
            pe.wait_ge(mkv_sb, 2)
            take("kmT")
            for h in range(MH):
                for t in range(2):
                    last = turn_tile(pat(pair("kmT"), h * 256 + t * 128, (1, 128)),
                                               at(A_MKV + t * 1024 + h * 128, (1, 128)), ident)
            last.then_inc(ps_ready, 1)
            pe.wait_ge(z_sb, 4)
            w = weights()
            for m in range(4):
                columns(f"G{m}", w + m * 128, 512, O_Z, 4).then_inc(ps_ready, 1)
            owed.append((w_used, 1))

            def scores(n):
                kind, a, b = UNITS[n]
                take(f"S{n}")
                p = pair(f"S{n}")
                if kind == "w":
                    k0, kn = (a - 1, 256) if a else (0, 128)
                    for m in range(4):
                        last = mm(pat(p, m * 256, (1, kn)), at(O_Q + m * T + a * 128, (1, 128), p0=64 * b, pn=64),
                                  at(O_KT + k0 * 128, (1, kn), p0=64 * b, pn=64), start=True, stop=True)
                elif kind == "m":
                    for h in range(MH):
                        last = mm(pat(p, h * 256, (1, MEM)), at(O_QM + h * T + a * 128, (1, 128)),
                                  at(A_KMT + h * MEM, (1, MEM)), start=True, stop=True)
                elif kind == "ws":
                    pe.wait_ge(ld["samp"], 48)
                    pe.wait_ge(qzs_ready, 1)
                    for kv in range(2):
                        for hf in range(2):
                            for b4 in range(4):
                                last = mm(pat(p, (kv * 2 + hf) * 256, (1, 136)),
                                          at(O_QZS + hf * 512 + b4 * 128, (1, 128), p0=64 * kv, pn=64),
                                          at(A_SKT + (4 * hf + b4) * 136, (1, 136), p0=64 * kv, pn=64),
                                          start=(b4 == 0), stop=(b4 == 3))
                else:
                    pe.wait_ge(qz_ready, a + 1)
                    for b4 in range(4):
                        bb = 4 * a + b4
                        pe.wait_ge(ldmk[bb % 2], 16 * (bb // 2 + 1))
                        for h in range(MH):
                            last = mm(pat(p, 0, (1, MEM)), at(A_QZ + (b4 * 4 + h) * 128, (1, 128)),
                                      at(A_MK + (bb % 2) * 1024 + h * MEM, (1, MEM)),
                                      start=(b4 == 0 and h == 0), stop=(b4 == 3 and h == 3))
                        if b4 < 3:
                            last.then_inc(mk_used, 1)
                last.then_inc(ps_ready, 1)
                if kind == "ms":
                    owed.append((mk_used, 1))

            def turn(n):
                kind, a, b = UNITS[n]
                pe.wait_ge(p_ready, n + 1)
                take(f"T{n}")
                p = pair(f"T{n}")
                sc = A_SC + (n % 2) * 1024
                if kind in "wm":
                    for kb in range(1 if kind == "w" and a == 0 else 2):
                        for m in range(4):
                            last = turn_tile(pat(p, kb * 512 + m * 128, (1, 128)),
                                                       at(sc + m * 256 + kb * 128, (1, 128)), ident)
                elif kind == "ws":
                    for t4 in range(4):
                        turn_tile(pat(p, t4 * 128, (1, 128)), at(sc + t4 * 256, (1, 128)), ident)
                        last = turn_tile(pat(p, 512 + t4 * 128, (1, 128), pn=8),
                                                   at(sc + t4 * 256 + 128, (1, 8)), ident)
                else:
                    for kb in range(2):
                        last = turn_tile(pat(p, kb * 128, (1, 128)), at(sc + kb * 128, (1, 128)), ident)
                last.then_inc(ps_ready, 1)

            def outputs(n):
                kind, a, b = UNITS[n]
                pe.wait_ge(pt_ready, n + 1)
                take(f"O{n}")
                p = pair(f"O{n}")
                pt = A_PT + (n % 2) * 1024
                if kind == "w":
                    kbs = 2 if a else 1
                    for kb in range(kbs):
                        last = mm(pat(p, 0, (1, 512), pn=64),
                                  at(O_KV + (a - (kbs - 1) + kb) * 256 + 128 + 64 * b, (1, 64)),
                                  at(pt + kb * 512, (1, 512)), start=(kb == 0), stop=(kb == kbs - 1))
                elif kind == "m":
                    for h in range(MH):
                        for kb in range(2):
                            last = mm(pat(p, h * 128, (1, 128)), at(A_MKV + kb * 1024 + 512 + h * 128, (1, 128)),
                                      at(pt + kb * 512 + h * 128, (1, 128)), start=(kb == 0), stop=(kb == 1))
                elif kind == "ws":
                    pe.wait_ge(ld["svn"], 16)
                    pe.wait_ge(svn_ready, 16)
                    for kv in range(2):
                        for bb in range(NB):
                            dst = pat(p, kv * 256 + bb * 32, (1, 32), pn=64)
                            col = (kv * 2 + bb // 4) * 128 + (bb % 4) * 32
                            mm(dst, at(A_SV + bb * 128 + kv * 64, (1, 64)), at(pt + col, (1, 32)), start=True, stop=False)
                            last = mm(dst, at(A_SVN + bb * 128 + kv * 64, (1, 64), pn=8),
                                      at(pt + 512 + col, (1, 32), pn=8), start=False, stop=True)
                else:
                    for b4 in range(4):
                        bb = 4 * a + b4
                        pe.wait_ge(ldmv[bb % 2], 16 * (bb // 2 + 1))
                        for h in range(MH):
                            for kb in range(2):
                                last = mm(pat(p, (b4 * 4 + h) * 8, (1, 8)),
                                          at(A_MV + (bb % 2) * 1024 + kb * 512 + h * 128, (1, 128)),
                                          at(pt + kb * 128 + (b4 * 4 + h) * 8, (1, 8)), start=(kb == 0), stop=(kb == 1))
                        if b4 < 3:
                            last.then_inc(mv_used, 1)
                last.then_inc(ps_ready, 1)
                if kind == "ms":
                    owed.append((mv_used, 1))

            pe.wait_ge(kT_sb, 1)
            pe.wait_ge(q_sb, 4)
            pe.wait_ge(qm_sb, 4)
            pe.wait_ge(kmT_sb, 1)
            pe.wait_ge(mkv_sb, 4)
            n_units = len(UNITS)
            held, pieces_left = {}, list(PIECES)

            def piece(name):
                kind, n, blk = name[0], int(name[1:].rstrip("ab")), piece_block(name)
                if blk not in held:
                    held[blk] = weights()
                w = held[blk]
                if kind == "g":
                    half = "ab".index(name[-1])
                    take(name)
                    for kt in range(KT):
                        last = mm(pat(pair(name), 0, (1, TH)), at(w + (n % 2) * 128 + kt * 256, (1, 128)),
                                  at(O_X + kt * T + half * TH, (1, TH)), start=(kt == 0), stop=(kt == KT - 1))
                else:
                    src = {"c": O_Z, "p": O_O + n // 8 * 2304}[kind]
                    if name == "c0":
                        pe.wait_ge(zz_ready, 1)
                    if name == "p0":
                        pe.wait_ge(o_sb, 9)
                    if name == "p8":
                        pe.wait_ge(o_sb, n_units)
                    last = columns(name, w + (n % 4) * 512, 128, src, 4)
                last.then_inc(ps_ready, 1)
                pieces_left.pop(0)
                done = 0
                for b in list(held):
                    if any(piece_block(q) == b for q in pieces_left):
                        break
                    del held[b]
                    done += 1
                if done:
                    owed.append((w_used, done))

            scores(0)
            for n in range(n_units + 1):
                if n + 1 < n_units:
                    scores(n + 1)
                if n >= 1:
                    outputs(n - 1)
                for q in pieces_at(n):
                    piece(q)
                if n < n_units:
                    turn(n)
            for q in pieces_at(n_units + 1):
                piece(q)
            pe.wait_ge(gate_used, 16)
            for b in range(4):
                w = weights()
                for t in range(TT):
                    take(f"w{b}{t}")
                    rows_of(f"w{b}{t}", 0, w, 256, 256, O_Q, t).then_inc(ps_ready, 1)
                owed.append((w_used, 1))
            def turn_norm(t):
                R = ROWS[t]
                pe.wait_ge(x2_ready, t + 1)
                take(f"x2T{t}")
                for kt in range(KT):
                    last = turn_tile(pat(pair(f"x2T{t}"), kt * 128, (1, R)),
                                     at(M_X2 + (t % 2) * 1024 + kt * 128, (1, 128), pn=R), at(O_ID, (1, R), pn=R))
                last.then_inc(ps_ready, 1)

            pe.wait_ge(ld["wr"], 16)
            turn_norm(0)
            for t in range(TT):
                R = ROWS[t]
                if t + 1 < TT:
                    turn_norm(t + 1)
                pe.wait_ge(x2T_sb, t + 1)
                take(f"lg{t}")
                for kt in range(KT):
                    last = mm(pat(pair(f"lg{t}"), 0, (1, 36), pn=R), at(M_X2T + (t % 2) * 1024 + kt * 128, (1, R)),
                              at(M_WR + kt * 36, (1, 36)), start=(kt == 0), stop=(kt == KT - 1))
                last.then_inc(ps_ready, 1)
            pe.wait_ge(m_onehot, 1)
            take("rk")
            p = pair("rk")
            for t in range(TT + 1):
                R = ROWS[t] if t < TT else 128
                dst = pat(p, t * 32, (1, 32), pn=R)
                if t:
                    last = mm(dst, at(O_ONE, (1, R)), at(R_MC + (t - 1) * 32, (1, 32)), start=True, stop=(t == TT))
                if t < TT:
                    last = mm(dst, at(R_TRI, (1, R), pn=R), at(R_M + t * 32, (1, 32), pn=R), start=(t == 0), stop=True)
            last.then_inc(ps_ready, 1)

            def turn_rows(r, k):
                pe.wait_ge(xg_ready[k % 2], 32 * r + 16 * (k // 2 + 1))
                wait_pos(pe, xT_lo, r, k, 0)
                for kt in range(KT):
                    last = turn_tile(pat(0, kt * 128, (1, 128)), at(M_XG + (k % 2) * 1024 + kt * 128, (1, 128)), ident)
                last.then_inc(xt_ps, 1)

            def gate_up(r, k, low):
                xh, xl, dst = M_XGT + (k % 2) * 1024, M_XGL[k % 2], pat(1, (k % 2) * 512, (1, 512), pn=RB)
                if not low:
                    wait_pos(pe, xT_lo, r, k, 1)
                    wait_pos(pe, hid_ready, r, k, -1)
                for kt in range(KT):
                    if kt % 4 == 0:
                        wait_half(pe, gu_lo if low else gu_hi, r, k, 1 + kt // 4)
                    for src, w in ((xh, E_GL),) if low else ((xh, E_GH + (k % 2) * 4096), (xl, E_GH + (k % 2) * 4096)):
                        last = mm(dst, r32(src + kt * RB, RB), r32(w + kt * 512, 512),
                                  start=(not low and kt == 0 and src == xh), stop=(low and kt == KT - 1))
                if low:
                    last.then_inc(gu_ps, 1)

            def turn_hidden(r, k):
                wait_pos(pe, hid_ready, r, k, 1)
                wait_pos(pe, hT_lo, r, k, 0)
                for c in range(2):
                    last = turn_tile(pat(2, c * 128, (1, 128)), at(M_HID + (k % 2) * 256 + c * 128, (1, 128)), ident)
                last.then_inc(hT_ps, 1)

            def down(r, k):
                wait_pos(pe, hT_lo, r, k, 1)
                wait_pos(pe, d_hi, r, k, 1)
                wait_pos(pe, y_copied, r, k, 0)
                hh, hl, wh = M_HT + (k % 2) * 256, M_HTL + (k % 2) * 256, E_DH + (k % 2) * 2048
                for n, (src, w) in enumerate(((hh, wh), (hl, wh), (hh, E_DL))):
                    if n == 2:
                        wait_pos(pe, d_lo, r, k, 1)
                    for half in range(2):
                        for c in range(2):
                            last = mm(pat(3, half * 512, (1, 512), pn=RB), r32(src + c * RB, RB),
                                      r32(w + c * 1024 + half * 512, 512), start=(n == 0 and c == 0), stop=(n == 2 and c == 1))
                last.then_inc(y_ps, 1)

            def body(r, k, first=False, last=False):
                pr, pk = (r, k - 1) if k else (r - 1, 3)
                nr, nk = (r, k + 1) if k < 3 else (r + 1, 0)
                gate_up(r, k, False)
                if not first:
                    turn_hidden(pr, pk)
                if not last:
                    turn_rows(nr, nk)
                gate_up(r, k, True)
                if not first:
                    down(pr, pk)

            for i in range(4):
                last_job = max(j for j in J.values() if j % 4 == i)
                pe.wait_ge(ps_free[i], last_job // 4 + 1)

            def blocks(r0, r1):
                turn_rows(r0, 0)
                for k in range(4):
                    body(r0, k, first=(k == 0))
                if r1 - r0 > 2:
                    with pe.Fori(r0 + 1, r1 - 1) as r:
                        for k in range(4):
                            body(r, k)
                for k in range(4):
                    body(r1 - 1, k, last=(k == 3))
                turn_hidden(r1 - 1, 3)
                down(r1 - 1, 3)

            blocks(0, NE // 4)
            with pe.If(overflow(pe) > 0):
                blocks(NE // 4, BLK // 4)

        @block.scalar
        def _(act):
            c = Chain(act, act_step)
            fn = nc.scalar.activation

            for i in range(2):
                act.dma_start(at(O_X + i * 4 * T, (1, 4 * T)), xT[:, i * 4 * T:(i + 1) * 4 * T]).then_inc(ld[f"xT{i}"], 16)
            act.dma_start(at(O_SM, (1, N_SMALL)), small).then_inc(ld["small"], 16)
            act.dma_start(at(O_TH, (1, 2048)), ssm).then_inc(ld["ssm"], 16)
            act.dma_start(at(O_ID, (1, 128)), const[:, 0:128]).then_inc(ld["const"], 16)
            act.wait_ge(ld["small"], 16)
            fn(at(O_SM + S_T, (1, 32)), at(O_SM + S_LD, (1, 32)), ACT.Exp).then_inc(exp_ssm, 1)
            for i in range(2):
                act.wait_ge(ld[f"xT{i}"], 16)
                fn(at(A_Y + i * 4 * T, (1, 4 * T)), at(O_X + i * 4 * T, (1, 4 * T)), ACT.Square).then_inc(x_sq, 1)
            act.wait_ge(ang_ready, 1)
            fn(at(O_SM + S_T + 32, (1, 32)), at(O_SM + S_T + 64, (1, 32)), ACT.Exp).then_inc(exp_ssm, 1)
            fn(at(O_SM + S_T + 96, (1, 64)), at(O_SM + S_T + 160, (1, 64)), ACT.Sin).then_inc(trig, 1)

            roots = [0]

            def root(ap):
                roots[0] += 1
                act.wait_ge(ms_ready, roots[0])
                fn(ap, ap, ACT.Sqrt).then_inc(root_ready, 1)

            root(at(O_RS, (1, T)))

            def copy_out(job, dst, src, to, **kw):
                filled(act, job)
                c.free(fn(dst, src, ACT.Copy, **kw), job)
                act.wait_ge(*c.last)
                act.sem_inc(to, 1)

            for t in range(TT):
                R = ROWS[t]
                copy_out(f"u{t}", at(A_US + t * 512, (1, 512), pn=R), pat(pair(f"u{t}"), 0, (1, 512), pn=R), u_sb)
            for t in range(TT):
                R = ROWS[t]
                copy_out(f"kv{t}", at(O_KV + t * 256, (1, 256), pn=R), pat(pair(f"kv{t}"), 0, (1, 256), pn=R), kv_sb)
            copy_out("kT", at(O_KT, (1, T)), pat(pair("kT"), 0, (1, T)), kT_sb)
            for m in range(4):
                copy_out(f"q{m}", at(O_Q + m * T, (TH, 2), (1, TH)), pat(pair(f"q{m}"), 0, (512, 2), (1, TH)), q_sb)
            for i in range(4):
                copy_out(f"VT{i}", at(A_VT + i * 1024, (1, 1024)), pat(pair(f"VT{i}"), 0, (1, 1024)), vt_sb)
            for i in range(4):
                copy_out(f"U{i}", at(O_UG + i * 8 * NC, (4 * NC, 2), (1, 4 * NC)),
                         pat(pair(f"U{i}"), 0, (512, 2), (1, 4 * NC)), ug_sb)
            for d in range(8):
                filled(act, f"g0{d}")
                c.free(fn(at(O_TH + d * T, (TH, 2), (1, TH)), pat(pair(f"g0{d}"), 0, (512, 2), (1, TH)), ACT.Tanh, scale=0.5),
                       f"g0{d}")
            for m in range(4):
                copy_out(f"qm{m}", at(O_QM + m * T, (TH, 2), (1, TH)), pat(pair(f"qm{m}"), 0, (512, 2), (1, TH)), qm_sb)
            for i in range(4):
                p = pair(f"Y{i}")
                copy_out(f"Y{i}", at(A_UC + i * 1024, (CH, 8), (128, L), (1, CH), pn=NC),
                         pat(p, 0, (128, 8), (CH, L), (1, CH), pn=NC), yc_sb)
            def early_gate(j):
                job = f"g{j}"
                filled(act, job)
                c.free(fn(at(O_UG + j * T, (TH, 2), (1, TH)), pat(pair(job), 0, (512, 2), (1, TH)), ACT.Tanh, scale=0.5), job)

            for i in range(4):
                if i == 3:
                    early_gate(0)
                act.wait_ge(gelu_in, i + 1)
                fn(at(A_GL + (i % 2) * 1024, (1, 1024), pn=NC), at(A_GL + (i % 2) * 1024, (1, 1024), pn=NC), ACT.Tanh,
                   scale=0.7978845608028654).then_inc(gelu_th, 1)
            for j in range(1, EARLY):
                early_gate(j)
            act.wait_ge(*c.last)
            act.sem_inc(gate_sb, EARLY)
            for i in range(4):
                filled(act, f"Z{i}")
                for half in range(2):
                    ins = fn(at(O_Z + i * T + half * 4, (1, 4), (L, NC)), pat(pair(f"Z{i}"), half * 512, (NC, 4), (1, NC)),
                             ACT.Copy, scale=0.5)
                    if half:
                        c.free(ins, f"Z{i}")
                    else:
                        c.do(ins)
                act.wait_ge(*c.last)
                act.sem_inc(z_sb, 1)
            act.wait_ge(ld["memT"], 16)
            fn(at(A_MV, (1, KT * MEM)), at(A_MK, (1, KT * MEM)), ACT.Square).then_inc(memsq, 1)
            root(at(O_RS, (1, MEM)))
            for i in range(4):
                copy_out(f"mm{i}", at(A_MKV + i * 256, (1024, 2), (1, 256)), pat(pair(f"mm{i}"), 0, (512, 2), (1, 256)), mkv_sb)
            copy_out("kmT", at(A_KMT, (1, 1024)), pat(pair("kmT"), 0, (1, 1024)), kmT_sb)
            act.wait_ge(par_ready, 1)
            for m in range(4):
                filled(act, f"G{m}")
                c.free(fn(at(A_THG + m * T, (TH, 2), (1, TH)), pat(pair(f"G{m}"), 0, (512, 2), (1, TH)), ACT.Tanh, scale=0.5,
                          bias=at(O_SM + S_BG + m, (1, 1))), f"G{m}")
            act.wait_ge(*c.last)
            act.sem_inc(thg_sb, 1)

            def stat(n, k):
                return O_SM + S_ST + (n % 2) * 24 + 4 * k

            def exponentials(n):
                kind, a, b = UNITS[n]
                act.wait_ge(stat_ready, n + 1)
                sc = A_SC + (n % 2) * 1024
                if n >= 2:
                    filled(act, f"T{n - 2}")
                if kind in ("w", "ws"):
                    keys = 136 if kind == "ws" else (256 if a else 128)
                    for m in range(4):
                        fn(at(sc + m * 256, (1, keys)), at(sc + m * 256, (1, keys)), ACT.Exp,
                           bias=at(stat(n, 1) + m, (1, 1)), accum_out=at(stat(n, 3) + m, (1, 1)))
                    fn(at(stat(n, 4), (1, 4)), at(stat(n, 2), (1, 4)), ACT.Exp).then_inc(exp_ready, 1)
                else:
                    for m in range(4 if kind == "m" else 1):
                        ins = fn(at(sc + m * 256, (1, 256)), pat(pair(f"S{n}"), m * 256, (1, 256)), ACT.Exp, scale=MEM_SCALE,
                                 bias=at(stat(n, 1) + m, (1, 1)), accum_out=at(stat(n, 3) + m, (1, 1)))
                        if m + 1 < (4 if kind == "m" else 1):
                            c.do(ins)
                    c.free(ins, f"S{n}")

            def turned(n):
                kind, a, b = UNITS[n]
                filled(act, f"T{n}")
                if n >= 2:
                    filled(act, f"O{n - 2}")
                p, pt = pair(f"T{n}"), A_PT + (n % 2) * 1024
                if kind == "ws":
                    c.do(fn(at(pt, (1, 512)), pat(p, 0, (1, 512)), ACT.Copy))
                    ins = fn(at(pt + 512, (1, 512), pn=8), pat(p, 512, (1, 512), pn=8), ACT.Copy)
                else:
                    w = 256 if kind == "ms" else (512 if kind == "w" and a == 0 else 1024)
                    ins = fn(at(pt, (1, w)), pat(p, 0, (1, w)), ACT.Copy)
                c.free(ins, f"T{n}")
                act.wait_ge(*c.last)
                act.sem_inc(pt_ready, 1)

            def output(n):
                kind, a, b = UNITS[n]
                filled(act, f"O{n}")
                p = pair(f"O{n}")
                if kind == "w":
                    ins = fn(at(O_O + a * 128, (T, 4), (1, 128), p0=64 * b, pn=64), pat(p, 0, (128, 4), (1, 128), pn=64), ACT.Copy)
                elif kind == "m":
                    ins = fn(at(O_O + 2304 + a * 128, (T, 4), (1, 128)), pat(p, 0, (128, 4), (1, 128)), ACT.Copy)
                elif kind == "ws":
                    for kv in range(2):
                        ins = fn(at(O_O + 512, (NQ, NB), (T, 4), (1, NQ), p0=64 * kv, pn=64),
                                 pat(p, kv * 256, (32, NB), (8, 4), (1, NQ), pn=64), ACT.Copy)
                        if kv == 0:
                            c.do(ins)
                else:
                    ins = fn(at(O_O + 2304 + 512 + a * 32, (NQ, 4), (T, 4), (1, NQ)), pat(p, 0, (32, 4), (8, 4), (1, NQ)), ACT.Copy)
                c.free(ins, f"O{n}")
                act.wait_ge(*c.last)
                act.sem_inc(o_sb, 1)

            def gate_half(name):
                j, half = int(name[1:-1]), "ab".index(name[-1])
                filled(act, name)
                if j >= EARLY + 3:
                    act.wait_ge(gate_used, j - 2)
                c.free(fn(at(gate_slot(j) + half * TH, (1, TH)), pat(pair(name), 0, (1, TH)), ACT.Tanh, scale=0.5), name)
                if half:
                    act.wait_ge(*c.last)
                    act.sem_inc(gate_sb, 1)

            n_units = len(UNITS)
            exponentials(0)
            for n in range(n_units + 2):
                if n + 1 < n_units:
                    exponentials(n + 1)
                if 1 <= n <= n_units:
                    output(n - 1)
                for q in pieces_at(n):
                    if q[0] == "g":
                        gate_half(q)
                if n < n_units:
                    turned(n)
            def copy_x2T(t):
                R = ROWS[t]
                if t >= 2:
                    filled(act, f"lg{t - 2}")
                copy_out(f"x2T{t}", at(M_X2T + (t % 2) * 1024, (128, KT), (1, R)),
                         pat(pair(f"x2T{t}"), 0, (128, KT), (1, R)), x2T_sb)

            for t in range(TT):
                R = ROWS[t]
                act.wait_ge(h_ready, 15 + t + 1)
                fn(at(M_JUNK, (1, D), pn=R), at(O_H + t * D, (1, D), pn=R), ACT.Square,
                   accum_out=at(R_SS + t, (1, 1), pn=R)).then_inc(ss2, 1)
                root(at(R_SS + t, (1, 1), pn=R))
                if t >= 1:
                    copy_x2T(t - 1)
            copy_x2T(TT - 1)
            act.wait_ge(gate_d, 1)
            fn(at(R_GE, (1, 20)), at(R_GE, (1, 20)), ACT.Exp).then_inc(gate_e, 1)
            fn(at(R_ED, (1, 5)), at(R_ED, (1, 5)), ACT.Exp).then_inc(gate_e, 1)

            def high_gate_up(r, k, h):
                act.wait_ge(wg_ready[k % 2 * 2 + h], 32 * r + 16 * (k // 2 + 1))
                wait_pos(act, gu_ps, r, k, -1)
                o = (k % 2) * 4096 + h * 2048
                fn(r32(E_GH + o, 2048), at(E_GU + o, (1, 2048)), ACT.Copy).then_inc(gu_hi, 1)

            def high_down(r, k):
                act.wait_ge(wd_ready[k % 2], 32 * r + 16 * (k // 2 + 1))
                wait_pos(act, y_ps, r, k, -1)
                fn(r32(E_DH + (k % 2) * 2048, 2048), at(E_D + (k % 2) * 2048, (1, 2048)), ACT.Copy).then_inc(d_hi, 1)

            def rows_turned(r, k):
                wait_pos(act, xt_ps, r, k, 1)
                wait_pos(act, gu_ps, r, k, -1)
                fn(r32t(M_XGT + (k % 2) * 1024, KT), pat(0, 0, (128, KT), (1, RB)), ACT.Copy).then_inc(xT_hi, 1)

            def hidden_turned(r, k):
                wait_pos(act, hT_ps, r, k, 1)
                wait_pos(act, y_ps, r, k, -1)
                fn(r32t(M_HT + (k % 2) * 256, 2), pat(2, 0, (128, 2), (1, RB)), ACT.Copy).then_inc(hT_hi, 1)

            def gate(r, k):
                wait_pos(act, gu_ps, r, k, 1)
                wait_pos(act, hid_ready, r, k, -1)
                fn(at(M_THE + (k % 2) * 256, (1, 256), pn=RB), pat(1, (k % 2) * 512, (1, 256), pn=RB), ACT.Tanh, scale=0.5)\
                    .then_inc(th_ready, 1)

            def body(r, k, first=False, last=False):
                pr, pk = (r, k - 1) if k else (r - 1, 3)
                nr, nk = (r, k + 1) if k < 3 else (r + 1, 0)
                high_down(r, k)
                if not first:
                    hidden_turned(pr, pk)
                if not last:
                    high_gate_up(nr, nk, 0)
                    rows_turned(nr, nk)
                    high_gate_up(nr, nk, 1)
                gate(r, k)

            def blocks(r0, r1):
                for h in range(2):
                    high_gate_up(r0, 0, h)
                rows_turned(r0, 0)
                for k in range(4):
                    body(r0, k, first=(k == 0))
                if r1 - r0 > 2:
                    with act.Fori(r0 + 1, r1 - 1) as r:
                        for k in range(4):
                            body(r, k)
                for k in range(4):
                    body(r1 - 1, k, last=(k == 3))
                hidden_turned(r1 - 1, 3)

            blocks(0, NE // 4)
            with act.If(overflow(act) > 0):
                blocks(NE // 4, BLK // 4)
            def square(t):
                R = ROWS[t]
                act.wait_ge(y_sum, t + 1)
                if t:
                    act.wait_ge(ssf, t)
                fn(at(M_JUNK, (1, D), pn=R), at(O_H + t * D, (1, D), pn=R), ACT.Square,
                   accum_out=at(R_SS + 8 + t, (1, 1), pn=R)).then_inc(ssf, 1)

            square(0)
            for t in range(TT):
                if t + 1 < TT:
                    square(t + 1)
                root(at(R_SS + 8 + t, (1, 1), pn=ROWS[t]))

        @block.vector
        def _(dve):
            c = Chain(dve, vec_step)
            v = nc.vector

            def sm(k, n=32, p0=0, pn=P):
                return at(O_SM + S_T + 32 * k, (1, n), p0=p0, pn=pn)

            def op(ins, settle=True):
                c.do(ins)
                if settle:
                    c.settle()

            roots = [0]

            def inverse(ap):
                c.settle()
                dve.sem_inc(ms_ready, 1)
                roots[0] += 1
                dve.wait_ge(root_ready, roots[0])
                op(v.reciprocal(ap, ap))

            v.memset(at(O_ONE, (1, 128)), 1.0).then_inc(ones_set, 1)
            v.memset(at(A_ZERO, (1, 112)), 0.0).then_inc(zero_set, 1)
            dve.wait_ge(ld["small"], 16)
            op(v.tensor_scalar(at(O_SM + S_BG, (1, 4)), at(O_SM + S_BG, (1, 4)), 0.5, None, ALU.mult))
            dve.wait_ge(exp_ssm, 1)
            op(v.tensor_tensor(sm(2), at(O_SM + S_LR, (1, 32)), sm(0), ALU.mult), False)
            op(v.tensor_tensor(sm(7), at(O_SM + S_LI, (1, 32)), sm(0), ALU.mult))
            op(v.tensor_scalar(sm(8), sm(7), 1.0 / 6.283185307179586, MAGIC, ALU.mult, ALU.add))
            op(v.tensor_scalar(sm(8), sm(8), MAGIC, None, ALU.subtract))
            for part in (TWO_PI_A, TWO_PI_B, TWO_PI_C):
                op(v.scalar_tensor_tensor(sm(7), sm(8), -part, sm(7), ALU.mult, ALU.add))
            op(v.tensor_scalar(sm(5), sm(7), 3.1415925, -3.1415925, ALU.min, ALU.max))
            op(v.scalar_tensor_tensor(sm(6), sm(5), -1.0, sm(5), ALU.mult, ALU.max))
            c.do(v.tensor_scalar(sm(6), sm(6), -1.0, 1.5707963267948966, ALU.mult, ALU.add), ang_ready)
            filled(dve, "ssq")
            p = pair("ssq")
            c.free(v.tensor_scalar(at(O_RS, (TH, 2), (1, TH)), pat(p, 0, (512, 2), (1, TH)), 1.0 / D, EPS, ALU.mult, ALU.add),
                   "ssq")
            inverse(at(O_RS, (1, T)))
            for kt in range(KT):
                ins = v.scalar_tensor_tensor(at(O_X + kt * T, (1, T)), at(O_X + kt * T, (1, T)),
                                             at(O_SM + S_G1 + kt, (1, 1)), at(O_RS, (1, T)), ALU.mult, ALU.mult)
                c.do(ins, xn_ready)

            dve.wait_ge(exp_ssm, 2)
            dve.wait_ge(trig, 1)
            pr, pi = O_PW, O_PW + 288

            def pw(base, j, n=1, **kw):
                return at(base + j * 32, (1, 32 * n), **kw)

            op(v.memset(pw(pr, 0), 1.0), False)
            op(v.memset(pw(pi, 0), 0.0), False)
            op(v.tensor_tensor(pw(pr, 1), sm(1), sm(4), ALU.mult), False)
            op(v.tensor_tensor(pw(pi, 1), sm(1), sm(3), ALU.mult))
            for j in range(2, 9):
                h = {2: 1, 3: 2, 4: 2, 5: 4, 6: 4, 7: 4, 8: 4}[j]
                op(v.tensor_tensor(sm(7), pw(pr, h), pw(pr, j - h), ALU.mult), False)
                op(v.tensor_tensor(sm(8), pw(pi, h), pw(pi, j - h), ALU.mult), False)
                op(v.tensor_tensor(sm(9), pw(pr, h), pw(pi, j - h), ALU.mult), False)
                op(v.tensor_tensor(sm(10), pw(pi, h), pw(pr, j - h), ALU.mult))
                op(v.tensor_tensor(pw(pr, j), sm(7), sm(8), ALU.subtract), False)
                op(v.tensor_tensor(pw(pi, j), sm(9), sm(10), ALU.add))
            op(v.tensor_copy(at(O_SM + S_A8, (32, 2), (1, 32)), at(pr + 8 * 32, (0, 2), (1, 32))), False)
            op(v.tensor_scalar(at(O_SM + S_A8 + 64, (1, 32)), pw(pi, 8), -1.0, None, ALU.mult), False)
            op(v.tensor_copy(at(O_SM + S_A8 + 96, (1, 32)), pw(pi, 8)))
            lr, li = at(O_SM + S_LR, (1, 32)), at(O_SM + S_LI, (1, 32))
            op(v.tensor_tensor(sm(7), lr, lr, ALU.mult), False)
            op(v.tensor_tensor(sm(8), li, li, ALU.mult), False)
            op(v.tensor_scalar(sm(9), pw(pr, 1), 1.0, None, ALU.subtract))
            op(v.tensor_tensor(sm(7), sm(7), sm(8), ALU.add), False)
            op(v.tensor_tensor(sm(10), sm(9), lr, ALU.mult), False)
            op(v.tensor_tensor(sm(11), pw(pi, 1), li, ALU.mult), False)
            op(v.tensor_tensor(sm(12), pw(pi, 1), lr, ALU.mult), False)
            op(v.tensor_tensor(sm(13), sm(9), li, ALU.mult))
            op(v.reciprocal(sm(7), sm(7)), False)
            op(v.tensor_tensor(sm(10), sm(10), sm(11), ALU.add), False)
            op(v.tensor_tensor(sm(12), sm(12), sm(13), ALU.subtract))
            op(v.tensor_tensor(sm(11), sm(10), sm(7), ALU.mult), False)
            op(v.tensor_tensor(sm(12), sm(12), sm(7), ALU.mult))
            P1, P2, Q1, Q2 = (O_PW + 576 + 288 * k for k in range(4))
            for dst, re, rs, im, is_ in ((P1, pr, 1.0, pi, -1.0), (P2, pi, -1.0, pr, -1.0), (Q1, pr, 1.0, pi, 1.0),
                                         (Q2, pi, -1.0, pr, 1.0)):
                op(v.tensor_scalar(pw(dst, 0, 9, pn=64), pw(re, 0, 9, pn=64), rs, None, ALU.mult), False)
                op(v.tensor_scalar(pw(dst, 0, 9, p0=64, pn=64), pw(im, 0, 9, p0=64, pn=64), is_, None, ALU.mult), False)
            c.settle()
            dve.wait_ge(ld["ssm"], 16)
            b1, b2, c1, c2 = (O_TH + 512 * k for k in range(4))
            br_, bi_ = O_TH + 3072, O_TH + 3584
            bst = O_TH + 2048

            def g16(off, n=G):
                return at(off, (CH, n), (1, CH))

            def fb(k):
                return at(O_SM + S_T + 32 * k, (1, G), (0, CH))

            tmp = O_Z
            op(v.tensor_tensor(g16(br_), g16(b1), fb(11), ALU.mult), False)
            op(v.tensor_tensor(g16(tmp), g16(b2), fb(12), ALU.mult), False)
            op(v.tensor_tensor(g16(bi_), g16(b2), fb(11), ALU.mult), False)
            op(v.tensor_tensor(g16(tmp + 512), g16(b1), fb(12), ALU.mult))
            op(v.tensor_tensor(at(br_, (1, 512)), at(br_, (1, 512)), at(tmp, (1, 512)), ALU.subtract), False)
            op(v.tensor_tensor(at(bi_, (1, 512)), at(bi_, (1, 512)), at(tmp + 512, (1, 512)), ALU.add))
            op(v.tensor_copy(at(bst, (1, 512), pn=64), at(br_, (1, 512), pn=64)), False)
            op(v.tensor_copy(at(bst, (1, 512), p0=64, pn=64), at(bi_, (1, 512), p0=64, pn=64)))

            for hf in range(2):
                dims = ((144, 16), (CH, 9), (1, CH))
                g0 = 16 * hf
                dst = at(A_Y + g0 * 144, *dims)
                op(v.tensor_tensor(dst, at(c1 + g0 * CH, (CH, 16), (0, 9), (1, CH)), at(P1 + g0, (1, 16), (32, 9), (0, CH)),
                                   ALU.mult), False)
                op(v.tensor_tensor(at(tmp, *dims), at(c2 + g0 * CH, (CH, 16), (0, 9), (1, CH)),
                                   at(P2 + g0, (1, 16), (32, 9), (0, CH)), ALU.mult))
                ins = v.tensor_tensor(at(A_Y + g0 * 144, (1, 2304)), at(A_Y + g0 * 144, (1, 2304)), at(tmp, (1, 2304)), ALU.add)
                if hf:
                    c.do(ins, y_built)
                else:
                    c.do(ins)
                c.settle()
            for hf in range(2):
                dims = ((128, 16), (CH, L), (1, CH))
                g0 = 16 * hf
                op(v.tensor_tensor(at(O_O + g0 * 128, *dims), at(br_ + g0 * CH, (CH, 16), (0, L), (1, CH)),
                                   at(Q1 + 7 * 32 + g0, (1, 16), (-32, L), (0, CH)), ALU.mult), False)
                op(v.tensor_tensor(at(tmp, *dims), at(bi_ + g0 * CH, (CH, 16), (0, L), (1, CH)),
                                   at(Q2 + 7 * 32 + g0, (1, 16), (-32, L), (0, CH)), ALU.mult))
                ins = v.tensor_tensor(at(O_O + g0 * 128, (1, 2048)), at(O_O + g0 * 128, (1, 2048)), at(tmp, (1, 2048)), ALU.add)
                if hf:
                    c.do(ins, vt_built)
                else:
                    c.do(ins)
                c.settle()
            dve.wait_ge(ld["const"], 16)
            op(v.tensor_tensor(at(tmp, (CH, G), (1, CH), pn=CH), at(O_ID, (0, G), (1, CH), pn=CH),
                               at(O_SM + S_DS, (1, G), (0, CH), pn=CH), ALU.mult))
            for i in range(8):
                filled(dve, f"K{i}")
                if i >= 4:
                    dve.wait_ge(k_out[i % 4], 16)
                p, ks = pair(f"K{i}"), A_KS + (i % 4) * 512
                op(v.tensor_copy(at(ks, (1, 512), pn=CH), pat(p, 0, (1, 512), pn=CH)))
                c.free(v.tensor_tensor(at(ks, (128, 4), (1, CH), pn=CH), pat(p, 0, (128, 4), (1, CH), pn=CH),
                                       at(tmp + i * 64, (CH, 4), (1, CH), pn=CH), ALU.add), f"K{i}")
                c.settle()
                dve.sem_inc(ks_sb, 1)

            dve.wait_ge(u_out, 16 * TT)
            dve.wait_ge(ld["uc"], 16)
            for i in range(4):
                if i >= 2:
                    filled(dve, f"U{i - 2}")
                c.do(v.tensor_copy(at(A_UP + (i % 2) * 1024, (128, 8), (CH, L), (1, CH), pn=NC),
                                   at(A_UC + i * 128, (CH, 8), (512, L), (1, CH), pn=NC)), up_sb)

            def slot(n, comp=0, cnt=1, p0=0, pn=P):
                return at(A_S + comp * SLOTS * G + n * G, (1, cnt * G), p0=p0, pn=pn)

            dve.wait_ge(u_out, 16 * TT)
            for n in range(4):
                dve.wait_ge(k_out[n], 32)
            dve.wait_ge(kz_out, 16)
            filled(dve, "U3")
            op(v.memset(slot(0), 0.0), False)
            op(v.memset(slot(0, 1), 0.0))
            dve.sem_inc(par_ready, 1)
            for i in range(4):
                filled(dve, f"B{i}")
                p = pair(f"B{i}")
                for n in range(2):
                    g0 = 8 * i + 4 * n
                    op(v.tensor_copy(at(A_S + G + g0, (G, PC - 1), (1, 4)), pat(p, n * 512, (1, PC - 1), (NC, 4))), False)
                    ins = v.tensor_copy(at(A_S + 72 * G + g0, (G, 1 + NB), (1, 4)), pat(p, n * 512 + PC - 1, (1, 1 + NB), (NC, 4)))
                    if n == 0:
                        c.do(ins)
                    else:
                        c.free(ins, f"B{i}")
            c.settle()
            for a, cnt in ((1, PC - 1), (72, 1 + NB)):
                op(v.tensor_scalar(slot(a, 1, cnt, 0, 64), slot(a, 0, cnt, 64, 64), -1.0, None, ALU.mult), False)
                op(v.tensor_copy(slot(a, 1, cnt, 64, 64), slot(a, 0, cnt, 0, 64)), False)
            dve.wait_ge(ld["h0"], 16)
            op(v.tensor_scalar(slot(64, 1, NB, 0, 64), slot(64, 1, NB, 0, 64), -1.0, None, ALU.mult))
            t1 = O_SM + S_SC
            CS = SLOTS * G

            def advance(src, dst, k):
                v.tensor_tensor(at(t1, (64, 2), (32, 2), (1, G)), at(O_SM + S_A8, (64, 2), (32, 2), (1, G)),
                                at(A_S + src, (0, 2), (CS, 2), (1, G)), ALU.mult).then_inc(scan, 1)
                dve.wait_ge(scan, k * 4 + 1)
                v.tensor_tensor(at(A_S + dst, (CS, 2), (1, G)), at(A_S + dst, (CS, 2), (1, G)), at(t1, (32, 2), (1, G)),
                                ALU.add).then_inc(scan, 1)
                dve.wait_ge(scan, k * 4 + 2)
                for comp, term in ((0, 3), (1, 2)):
                    part = at(A_S + comp * CS + dst, (1, G))
                    v.tensor_tensor(part, part, at(t1 + 32 * term, (1, G)), ALU.add).then_inc(scan, 1)
                dve.wait_ge(scan, k * 4 + 4)

            with dve.Fori(0, (PC - 2) // 2) as r:
                for k in range(2):
                    advance((r * 2 + (k + 1)) * G, (r * 2 + (k + 2)) * G, r * 2 + k)
            advance((PC - 1) * G, 72 * G, PC - 2)
            for n in range(NB):
                src, dst = (64 + n) * G, (73 + n) * G
                w = tmp + 64 * n
                op(v.tensor_tensor(at(w, (1, G)), at(O_SM + S_A8, (1, G)), at(A_S + src, (1, G)), ALU.mult), False)
                op(v.tensor_tensor(at(w + 32, (1, G)), at(O_SM + S_A8 + 96, (1, G)), at(A_S + CS + src, (1, G)), ALU.mult), False)
            c.settle()
            for n in range(2):
                op(v.tensor_tensor(at(A_S + 73 * G, (G, NB), (1, G)), at(A_S + 73 * G, (G, NB), (1, G)),
                                   at(tmp + 32 * n, (64, NB), (1, G)), ALU.add))
            dve.sem_inc(scanned, 1)

            def gelu_begin(i):
                yc, gl = at(A_UC + i * 1024, (1, 1024), pn=NC), at(A_GL + (i % 2) * 1024, (1, 1024), pn=NC)
                dve.wait_ge(yc_sb, i + 1)
                op(v.scalar_tensor_tensor(gl, yc, 0.044715, yc, ALU.mult, ALU.mult))
                c.do(v.scalar_tensor_tensor(gl, gl, 1.0, yc, ALU.add, ALU.mult), gelu_in)

            def gelu_end(i):
                yc, gl = at(A_UC + i * 1024, (1, 1024), pn=NC), at(A_GL + (i % 2) * 1024, (1, 1024), pn=NC)
                dve.wait_ge(gelu_th, i + 1)
                c.do(v.scalar_tensor_tensor(yc, gl, 1.0, yc, ALU.add, ALU.mult), zc_ready)
                c.settle()

            filled(dve, "Y3")
            dve.wait_ge(out_st, 16 * 2)
            gelu_begin(0)
            for i in range(4):
                if i < 3:
                    gelu_begin(i + 1)
                gelu_end(i)
            filled(dve, "ssqm")
            c.free(v.tensor_scalar(at(O_RS, (1, MEM)), pat(pair("ssqm"), 0, (1, MEM)), 1.0 / D, EPS, ALU.mult, ALU.add), "ssqm")
            inverse(at(O_RS, (1, MEM)))
            for kt in range(KT):
                ins = v.scalar_tensor_tensor(at(A_MK + kt * MEM, (1, MEM)), at(A_MK + kt * MEM, (1, MEM)),
                                             at(O_SM + S_GM + kt, (1, 1)), at(O_RS, (1, MEM)), ALU.mult, ALU.mult)
                c.do(ins, memn if kt == KT - 1 else None)
            dve.wait_ge(thg_sb, 1)
            ins = v.scalar_tensor_tensor(at(O_Z, (1, 4 * T)), at(A_THG, (1, 4 * T)), 1.0, at(O_Z, (1, 4 * T)), ALU.add, ALU.mult)
            c.do(ins, zz_ready)
            c.settle()

            def stat(n, k, m=4):
                return at(O_SM + S_ST + (n % 2) * 24 + 4 * k, (1, m))

            def maxima(n):
                kind, a, b = UNITS[n]
                filled(dve, f"S{n}")
                if n >= 2:
                    filled(dve, f"T{n - 2}")
                p, sc = pair(f"S{n}"), A_SC + (n % 2) * 1024
                if kind in ("w", "ws"):
                    if kind == "w":
                        keys, k0 = (256, 0) if a else (128, 128)
                        sc_v, ps_v = at(sc, (256, 4), (1, keys)), pat(p, 0, (256, 4), (1, keys))
                        bias_v = at(A_BI + b * 1024 + k0, (256, 4), (1, keys))
                        sink = at(O_SM + S_SK + 4 * b, (1, 4))
                        if n == 0:
                            dve.wait_ge(ld["bias"], 16)
                        c.free(v.scalar_tensor_tensor(sc_v, ps_v, SWA_SCALE, bias_v, ALU.mult, ALU.add), f"S{n}")
                    else:
                        keys = 136
                        sc_v = at(sc, (256, 4), (1, keys))
                        sink = at(O_SM + S_SS, (1, 2), (0, 2))
                        for kv in range(2):
                            ins = v.scalar_tensor_tensor(at(sc + kv * 512, (256, 2), (1, keys)),
                                                         pat(p, kv * 512, (256, 2), (1, keys)), SWA_SCALE,
                                                         at(A_SB + kv * 136, (0, 2), (1, keys)), ALU.mult, ALU.add)
                            if kv:
                                c.free(ins, f"S{n}")
                            else:
                                c.do(ins)
                    c.settle()
                    op(v.tensor_reduce(stat(n, 0), sc_v, AX, ALU.max))
                    op(v.tensor_tensor(stat(n, 0), stat(n, 0), sink, ALU.max))
                    op(v.tensor_scalar(stat(n, 1), stat(n, 0), -1.0, None, ALU.mult), False)
                    c.do(v.tensor_tensor(stat(n, 2), sink, stat(n, 0), ALU.subtract), stat_ready)
                else:
                    m = 4 if kind == "m" else 1
                    op(v.tensor_reduce(stat(n, 0, m), pat(p, 0, (256, m), (1, 256)), AX, ALU.max))
                    c.do(v.tensor_scalar(stat(n, 1, m), stat(n, 0, m), -MEM_SCALE, None, ALU.mult), stat_ready)

            def divide(n):
                kind, a, b = UNITS[n]
                if kind in ("w", "ws"):
                    dve.wait_ge(exp_ready, n + 1)
                else:
                    dve.wait_ge(ps_free[pair(f"S{n}")], free_count(f"S{n}"))
                sc = A_SC + (n % 2) * 1024
                m = 1 if kind == "ms" else 4
                if kind in ("w", "ws"):
                    keys = 136 if kind == "ws" else (256 if a else 128)
                    op(v.tensor_tensor(stat(n, 3), stat(n, 3), stat(n, 4), ALU.add))
                    op(v.reciprocal(stat(n, 5), stat(n, 3)))
                else:
                    keys = 256
                    op(v.reciprocal(stat(n, 5, m), stat(n, 3, m)))
                c.do(v.tensor_tensor(at(sc, (256, m), (1, keys)), at(sc, (256, m), (1, keys)),
                                     at(O_SM + S_ST + (n % 2) * 24 + 20, (1, m), (0, keys)), ALU.mult), p_ready)

            dve.wait_ge(z_sb, 4)
            op(v.memset(at(O_QZS, (1, 1024)), 0.0), False)
            dve.wait_ge(q_sb, 4)
            c.settle()
            for hf in range(2):
                c.do(v.tensor_copy(at(O_QZS + hf * 512, (128 + 32, 4), (8, 4), (1, NQ)),
                                   at(O_Q + 512 + hf * 32, (NQ, 4), (T, 4), (1, NQ))), qzs_ready if hf else None)

            def place(half):
                c.do(v.tensor_copy(at(A_QZ, (4 * 136, 4), (136, 4), (1, NQ)), at(O_QM + 512 + half * 32, (NQ, 4), (T, 4), (1, NQ))),
                     qz_ready)

            def piece(name):
                kind, n = name[0], int(name[1:])
                filled(dve, name)
                d = n % 8
                m0 = at(O_TH + d * T, (1, T))
                gate = O_TH + d * T if kind == "c" else gate_slot(n)
                if kind == "p":
                    dve.wait_ge(gate_sb, n + 1)
                g2 = at(gate, (TH, 2), (1, TH))
                c.free(v.scalar_tensor_tensor(g2, g2, 1.0, pat(pair(name), 0, (512, 2), (1, TH)), ALU.add, ALU.mult), name)
                if kind == "p":
                    c.settle()
                    if n < 8:
                        c.do(v.scalar_tensor_tensor(m0, m0, 0.5, at(gate, (1, T)), ALU.mult, ALU.add), gate_used)
                    else:
                        c.do(v.tensor_tensor(at(O_Q + d * T, (1, T)), m0, at(gate, (1, T)), ALU.add), gate_used)

            n_units = len(UNITS)
            maxima(0)
            for n in range(n_units + 2):
                if n + 1 < n_units:
                    maxima(n + 1)
                if n < n_units:
                    divide(n)
                if n < n_units and UNITS[n][0] == "ws":
                    op(v.memset(at(A_QZ, (1, 2048)), 0.0), False)
                    dve.wait_ge(qm_sb, 4)
                    c.settle()
                    place(0)
                if n + 1 < n_units and UNITS[n + 1] == ("ms", 0, 0):
                    filled(dve, f"S{n + 1}")
                    place(1)
                for q in pieces_at(n):
                    if q[0] != "g":
                        piece(q)
            c.settle()
            dve.wait_ge(ld["x"], 16 * TT)
            for b in range(4):
                for t in range(TT):
                    R, job = ROWS[t], f"w{b}{t}"
                    filled(dve, job)
                    h = at(O_H + t * D + b * 256, (1, 256), pn=R)
                    c.free(v.scalar_tensor_tensor(h, pat(pair(job), 0, (1, 256), pn=R), 0.5, h, ALU.mult, ALU.add), job)
                    c.settle()
                    dve.sem_inc(h_ready, 1)
            dve.wait_ge(ld["rows"], 32)
            op(v.memset(at(R_LG, (1, 36 * TT)), 0.0), False)
            op(v.memset(at(R_GP, (1, 8 * TT)), -3.0e38), False)

            def logits(t):
                R = ROWS[t]
                filled(dve, f"lg{t}")
                c.free(v.tensor_tensor(at(R_LG + 36 * t, (1, 36), pn=R), pat(pair(f"lg{t}"), 0, (1, 36), pn=R),
                                       at(M_BR, (1, 36), pn=R), ALU.add), f"lg{t}")

            dve.wait_ge(ld["wr"], 16)
            for t in range(TT):
                R = ROWS[t]
                ss = at(R_SS + t, (1, 1), pn=R)
                dve.wait_ge(ss2, t + 1)
                op(v.tensor_scalar(ss, ss, 1.0 / D, EPS, ALU.mult, ALU.add))
                inverse(ss)
                if t >= 2:
                    dve.wait_ge(x2_out[t % 2], 16 * (t // 2))
                    filled(dve, f"x2T{t - 2}")
                c.do(v.scalar_tensor_tensor(at(M_X2 + (t % 2) * 1024, (1, D), pn=R), at(O_H + t * D, (1, D), pn=R), ss,
                                            at(M_G2, (1, D), pn=R), ALU.mult, ALU.mult), x2_ready)
                if t >= 2:
                    logits(t - 2)
            logits(TT - 2)
            logits(TT - 1)
            c.settle()
            n5 = TT
            op(v.tensor_copy(at(R_GP, (8, n5), (1, 4)), at(R_LG, (36, n5), (1, 4))))
            for t in range(n5):
                op(v.max(at(R_GM + 8 * t, (1, 8)), at(R_GP + 8 * t, (1, 8))), False)
            c.settle()
            for t in range(n5):
                op(v.max_index(at(R_IX + 8 * t, (1, 8)).bitcast(U32), at(R_GM + 8 * t, (1, 8)), at(R_GP + 8 * t, (1, 8))), False)
            c.settle()
            op(v.tensor_copy(at(R_GX, (1, n5)), at(R_IX, (8, n5)).bitcast(U32)), False)
            op(v.tensor_tensor(at(R_GE, (4, n5), (1, 4)), at(R_LG, (36, n5), (1, 4)), at(R_GM, (8, n5), (0, 4)), ALU.subtract))
            op(v.tensor_tensor(at(R_OG, (4, n5), (1, 4)), at(R_IOTA, (0, n5), (1, 4)), at(R_GX, (1, n5), (0, 4)), ALU.is_equal))
            op(v.tensor_tensor(at(R_TM, (32, n5), (8, 4), (1, 8)), at(R_LG + 4, (36, n5), (8, 4), (1, 8)),
                               at(R_OG, (4, n5), (1, 4), (0, 8)), ALU.mult))
            op(v.tensor_reduce(at(R_EP, (8, n5), (1, 8)), at(R_TM, (32, n5), (1, 8), (8, 4)), AX, ALU.add))
            for t in range(n5):
                op(v.max(at(R_EM + 8 * t, (1, 8)), at(R_EP + 8 * t, (1, 8))), False)
            c.settle()
            for t in range(n5):
                op(v.max_index(at(R_IX + 8 * t, (1, 8)).bitcast(U32), at(R_EM + 8 * t, (1, 8)), at(R_EP + 8 * t, (1, 8))), False)
            c.do(v.tensor_tensor(at(R_ED, (1, n5)), at(R_EM + 1, (8, n5)), at(R_EM, (8, n5)), ALU.subtract), gate_d)
            c.settle()
            op(v.tensor_copy(at(R_EK, (n5, 2), (1, n5)), at(R_IX, (1, 2), (8, n5)).bitcast(U32)))
            op(v.scalar_tensor_tensor(at(R_EK, (n5, 2), (1, n5)), at(R_GX, (0, 2), (1, n5)), 8.0, at(R_EK, (n5, 2), (1, n5)),
                                      ALU.mult, ALU.add))
            op(v.tensor_tensor(at(R_MK, (32, 2 * n5), (1, 32)), at(R_IOTA, (0, 2 * n5), (1, 32)),
                               at(R_EK, (1, 2 * n5), (0, 32)), ALU.is_equal))
            op(v.tensor_tensor(at(R_M, (1, 32 * n5)), at(R_MK, (1, 32 * n5)), at(R_MK + 32 * n5, (1, 32 * n5)), ALU.add))
            op(v.memset(at(R_M + 32 * 4, (1, 32), p0=64, pn=64), 0.0))
            op(v.tensor_copy(at(R_MC, (1, 32)), at(R_M, (1, 32))))
            for t in range(1, n5):
                ins = v.tensor_tensor(at(R_MC + 32 * t, (1, 32)), at(R_MC + 32 * (t - 1), (1, 32)), at(R_M + 32 * t, (1, 32)), ALU.add)
                c.do(ins, m_onehot if t == n5 - 1 else None)
                c.settle()
            dve.wait_ge(gate_e, 2)
            op(v.tensor_reduce(at(R_W0, (1, n5)), at(R_GE, (4, n5), (1, 4)), AX, ALU.add), False)
            op(v.tensor_scalar(at(R_W1, (1, n5)), at(R_ED, (1, n5)), 1.0, None, ALU.add))
            op(v.tensor_tensor(at(R_W0, (1, n5)), at(R_W0, (1, n5)), at(R_W1, (1, n5)), ALU.mult))
            op(v.reciprocal(at(R_W0, (1, n5)), at(R_W0, (1, n5))))
            op(v.tensor_scalar(at(R_W0, (1, n5)), at(R_W0, (1, n5)), 0.5, None, ALU.mult))
            op(v.tensor_tensor(at(R_W1, (1, n5)), at(R_W0, (1, n5)), at(R_ED, (1, n5)), ALU.mult), False)
            filled(dve, "rk")
            for t in range(TT + 1):
                R = ROWS[t] if t < TT else 128
                ins = v.tensor_copy(at(R_RK + 32 * t, (1, 32), pn=R), pat(pair("rk"), 32 * t, (1, 32), pn=R))
                if t < TT:
                    c.do(ins)
                else:
                    c.free(ins, "rk")
            op(v.memset(at(R_RK + 32 * 4, (1, 32), p0=64, pn=64), 0.0))
            cnt, nb, inc, ovo = R_RK + 160, R_NB, R_NB + 32, R_NB + 64
            def whole(dst, src, n, less):
                op(v.tensor_scalar(at(dst, (1, n)), at(src, (1, n)), 1.0 / RB, -(less + RB / 2 - 0.5) / RB, ALU.mult, ALU.add))
                op(v.tensor_scalar(at(dst, (1, n)), at(dst, (1, n)), MAGIC, None, ALU.add))
                op(v.tensor_scalar(at(dst, (1, n)), at(dst, (1, n)), MAGIC, None, ALU.subtract))

            whole(nb, cnt, 32, 1)
            op(v.tensor_scalar(at(nb, (1, 32)), at(nb, (1, 32)), 0.0, None, ALU.max))
            op(v.tensor_tensor_scan(at(inc, (1, 32)), at(O_ONE, (1, 32)), at(nb, (1, 32)), 0.0, ALU.mult, ALU.add))
            op(v.tensor_tensor(at(ovo, (1, 32)), at(inc, (1, 32)), at(nb, (1, 32)), ALU.subtract))
            op(v.tensor_tensor(at(R_TM, (160, 2), (1, 160)), at(R_MK, (160, 2), (1, 160)), at(R_RK, (0, 2), (1, 160)), ALU.mult))
            op(v.tensor_reduce(at(R_RA, (1, 10)), at(R_TM, (32, 10), (1, 32)), AX, ALU.add))
            op(v.tensor_tensor(at(R_TM, (32, 10), (1, 32)), at(R_MK, (32, 10), (1, 32)), at(ovo, (0, 10), (1, 32)), ALU.mult))
            op(v.tensor_reduce(at(R_OB, (1, 10)), at(R_TM, (32, 10), (1, 32)), AX, ALU.add), False)
            ra, ob, fl, ov, ek = (at(o, (1, 10)) for o in (R_RA, R_OB, R_FL, R_OV, R_EK))
            whole(R_FL, R_RA, 10, 0)
            op(v.tensor_scalar(ov, fl, 1.0, None, ALU.is_ge), False)
            op(v.tensor_tensor(ob, ob, fl, ALU.add))
            op(v.tensor_scalar(ob, ob, float(NE - 1), None, ALU.add))
            op(v.tensor_tensor(ob, ob, ek, ALU.subtract))
            op(v.tensor_tensor(ob, ob, ov, ALU.mult))
            op(v.tensor_tensor(ob, ob, ek, ALU.add))
            op(v.scalar_tensor_tensor(ra, fl, -float(RB), ra, ALU.mult, ALU.add))
            op(v.scalar_tensor_tensor(ra, ra, float(BLK), ob, ALU.mult, ALU.add))
            op(v.tensor_copy(at(R_SL, (1, 10)).bitcast(U32), ra), False)
            c.do(v.tensor_copy(at(R_PI, (1, 10)).bitcast(U32), at(R_PF, (1, 10))), slot_ready)
            op(v.tensor_tensor(at(R_TM, (32, OVER), (1, 32)), at(inc, (0, OVER), (1, 32)), at(R_IOTA, (1, OVER), (0, 32)), ALU.is_le))
            op(v.tensor_reduce(at(R_TM, (1, OVER)), at(R_TM, (32, OVER), (1, 32)), AX, ALU.add))
            op(v.tensor_scalar(at(R_TM, (1, OVER)), at(R_TM, (1, OVER)), float(NE - 1), None, ALU.min))
            op(v.tensor_copy(at(M_IDX + 256, (1, OVER)).bitcast(I32), at(R_TM, (1, OVER))), False)
            c.do(v.tensor_copy(at(M_IDX + 256 + OVER, (1, 1)).bitcast(I32), at(inc + 31, (1, 1))), idx_ready)
            dve.wait_ge(ld["tb"], 16)
            tb, tf, tg = M_IDX, M_IDX + 64, M_IDX + 128
            def ids(o):
                return at(o, (1, BLK), pn=RB)

            op(v.tensor_copy(ids(tf), ids(tb).bitcast(U32)))
            op(v.tensor_scalar(ids(tg), ids(tf), float(T), -float(T), ALU.is_ge, ALU.mult))
            op(v.tensor_tensor(ids(tf), ids(tf), ids(tg), ALU.add))
            c.do(v.tensor_copy(ids(tg).bitcast(U32), ids(tf)), idx_ready)

            def hidden(r, k):
                wait_pos(dve, th_ready, r, k, 1)
                g, u = pat(1, (k % 2) * 512, (1, 256), pn=RB), pat(1, (k % 2) * 512 + 256, (1, 256), pn=RB)
                th, hid = at(M_THE + (k % 2) * 256, (1, 256), pn=RB), at(M_HID + (k % 2) * 256, (1, 256), pn=RB)
                v.scalar_tensor_tensor(th, th, 1.0, g, ALU.add, ALU.mult).then_inc(t_ready, 1)
                wait_pos(dve, t_ready, r, k, 1)
                wait_pos(dve, hT_ps, r, k, -1)
                v.tensor_tensor(hid, th, u, ALU.mult).then_inc(hid_ready, 1)

            def low_gate_up(r, k, h):
                wait_half(dve, gu_hi, r, k, 1 + h)
                if h == 0:
                    wait_pos(dve, gu_ps, r, k, 0)
                o = (k % 2) * 4096 + h * 2048
                v.tensor_tensor(r32(E_GL + h * 2048, 2048), at(E_GU + o, (1, 2048)), r32(E_GH + o, 2048).bitcast(F32),
                                ALU.subtract).then_inc(gu_lo, 1)

            def rows_turned(r, k):
                wait_pos(dve, xT_hi, r, k, 1)
                v.tensor_tensor(r32t(M_XGL[k % 2], KT), pat(0, 0, (128, KT), (1, RB)), r32t(M_XGT + (k % 2) * 1024, KT).bitcast(F32),
                                ALU.subtract).then_inc(xT_lo, 1)

            def hidden_turned(r, k):
                wait_pos(dve, hT_hi, r, k, 1)
                v.tensor_tensor(r32t(M_HTL + (k % 2) * 256, 2), pat(2, 0, (128, 2), (1, RB)), r32t(M_HT + (k % 2) * 256, 2).bitcast(F32),
                                ALU.subtract).then_inc(hT_lo, 1)

            def result(r, k):
                wait_pos(dve, y_ps, r, k, 1)
                prev = 32 * r + 16 * (k // 2)
                if not (isinstance(prev, int) and prev <= 0):
                    dve.wait_ge(y_sent[k % 2], prev)
                v.tensor_copy(at(M_YO + (k % 2) * 1024, (1, 1024), pn=RB), pat(3, 0, (1, 1024), pn=RB)).then_inc(y_copied, 1)

            def body(r, k, done=4, last=False):
                p1, p2 = [(r, k - n) if k >= n else (r - 1, k - n + 4) for n in (1, 2)]
                nr, nk = (r, k + 1) if k < 3 else (r + 1, 0)
                if done >= 2:
                    result(*p2)
                low_gate_up(r, k, 0)
                if done >= 1:
                    hidden_turned(*p1)
                low_gate_up(r, k, 1)
                if not last:
                    rows_turned(nr, nk)
                hidden(r, k)

            def blocks(r0, r1):
                rows_turned(r0, 0)
                for k in range(4):
                    body(r0, k, done=k)
                if r1 - r0 > 2:
                    with dve.Fori(r0 + 1, r1 - 1) as r:
                        for k in range(4):
                            body(r, k)
                for k in range(4):
                    body(r1 - 1, k, last=(k == 3))
                result(r1 - 1, 2)
                hidden_turned(r1 - 1, 3)
                result(r1 - 1, 3)

            dve.wait_ge(x2_out[0], 48)
            dve.wait_ge(x2_out[1], 32)
            blocks(0, NE // 4)
            with dve.If(overflow(dve) > 0):
                blocks(NE // 4, BLK // 4)

            def combine(t):
                R = ROWS[t]
                h = at(O_H + t * D, (1, D), pn=R)
                dve.wait_ge(y_ld[t], 32)
                op(v.scalar_tensor_tensor(h, at(A_WG + t * 2048, (1, D), pn=R), at(R_W0 + t, (1, 1), pn=R), h, ALU.mult, ALU.add))
                c.do(v.scalar_tensor_tensor(h, at(A_WG + t * 2048 + D, (1, D), pn=R), at(R_W1 + t, (1, 1), pn=R), h,
                                            ALU.mult, ALU.add), y_sum)

            def finish(t):
                R = ROWS[t]
                h = at(O_H + t * D, (1, D), pn=R)
                ss = at(R_SS + 8 + t, (1, 1), pn=R)
                dve.wait_ge(ssf, t + 1)
                op(v.tensor_scalar(ss, ss, 1.0 / D, EPS, ALU.mult, ALU.add))
                inverse(ss)
                c.do(v.scalar_tensor_tensor(h, h, ss, at(M_GF, (1, D), pn=R), ALU.mult, ALU.mult), y_done)

            combine(0)
            for t in range(TT):
                if t + 1 < TT:
                    combine(t + 1)
                finish(t)

        @block.gpsimd
        def _(pool):
            stores = [0]

            def store(dst, src):
                pool.dma_start(dst, src).then_inc(out_st, 16)
                stores[0] += 1

            pool.wait_ge(zero_set, 1)
            pool.dma_start(k_d[:, :, 0:112].rearrange("(a g) h c -> (g h) a c", g=8),
                           at(A_ZERO, (0, 4), (1, 112))).then_inc(kz_out, 16)
            for t in range(TT):
                R = ROWS[t]
                pool.wait_ge(u_sb, t + 1)
                pool.dma_start(u_d[t * 128:t * 128 + R, :], at(A_US + t * 512, (1, 512), pn=R)).then_inc(u_out, 16)
            pool.wait_ge(u_out, 16 * TT)
            pool.dma_start(at(A_UC, (1, 4096), pn=NC), u_d[:, :].rearrange("(c j) f -> c (j f)", j=L)).then_inc(ld["uc"], 16)
            pool.wait_ge(kv_sb, TT)
            pool.dma_start(kvs_d[:, :], at(O_KV + 4 * 256, (1, 256), pn=64)).then_inc(kvs_out, 16)
            for i in range(8):
                pool.wait_ge(ks_sb, i + 1)
                pool.dma_start(k_d[4 * i:4 * i + 4, :, 112:240].rearrange("g h c -> h g c"),
                               at(A_KS + (i % 4) * 512, (128, 4), (1, 128), pn=CH)).then_inc(k_out[i % 4], 16)
            for n in range(4):
                pool.wait_ge(k_out[n], 32)
            pool.dma_start(at(A_S + 64 * G, (SLOTS * G, 2), (1, NB * G)), h0).then_inc(ld["h0"], 16)
            filled(pool, "B3")
            for s in range(L):
                pool.dma_start(at(A_VT, (128, G), (1, 128), p0=CH * s, pn=CH),
                               k_d[:, :, 112 - CH * s:240 - CH * s].rearrange("g h c -> h g c")).then_inc(ld["T"], 16)
            store(out_kvp, at(O_KV + 3 * 256, (1, 256)))
            pool.wait_ge(scanned, 1)
            store(out_ssm, at(A_S + 72 * G, (1, 9 * G)))
            filled(pool, "Y3")
            pool.dma_start(at(A_MK, (1, KT * MEM)), memT).then_inc(ld["memT"], 16)
            pool.wait_ge(kvs_out, 16)
            pool.dma_start(at(A_SKT, (136, NB), (1, 128)), skT[:, :, :]).then_inc(ld["samp"], 16)
            pool.dma_start(at(A_SB, (1, 272)), sbias).then_inc(ld["samp"], 16)
            pool.wait_ge(kT_sb, 1)
            pool.dma_start(at(A_SKT + 128, (136, NB), (1, NQ)), at(O_KT + 512, (NQ, NB), (1, NQ))).then_inc(ld["samp"], 16)
            pool.wait_ge(zc_ready, 4)
            filled(pool, "Z3")
            pool.dma_start(at(A_BI, (1, 2048)), bias).then_inc(ld["bias"], 16)
            pool.dma_start(at(A_SV, (1, 1024)), sv).then_inc(ld["svn"], 16)
            pool.wait_ge(ld["svn"], 16)
            pool.dma_start(at(A_SVN, (128, NB), (1, 128), pn=NQ),
                           kvs_d[:, 128:256].rearrange("(b q) f -> q b f", q=NQ)).then_inc(svn_ready, 16)
            store(out_sk[:, 0:120, :], cache_k[:, 8:128, :])
            store(out_sv[:, 0:120, :], cache_v[:, 8:128, :])
            store(out_sk[:, 120:128, :], kvs_d[:, 0:128].rearrange("(b q) f -> b q f", q=NQ))
            store(out_sv[:, 120:128, :], kvs_d[:, 128:256].rearrange("(b q) f -> b q f", q=NQ))
            pool.wait_ge(mkv_sb, 4)
            store(out_mem.rearrange("(t p) f -> p t f", p=128), at(A_MKV, (1024, 2), (1, 1024)))
            def load_k(b):
                if b >= 2:
                    pool.wait_ge(mk_used, b - 1)
                pool.dma_start(at(A_MK + (b % 2) * 1024, (1, 1024)), mkT[b]).then_inc(ldmk[b % 2], 16)

            def load_v(b):
                if b >= 2:
                    pool.wait_ge(mv_used, b - 1)
                pool.dma_start(at(A_MV + (b % 2) * 1024, (1, 1024)), mv[b]).then_inc(ldmv[b % 2], 16)

            for b in range(2):
                load_k(b)
                load_v(b)
            for b in range(2, NB):
                load_k(b)
            for b in range(2, NB):
                load_v(b)
            for t in range(TT):
                R = ROWS[t]
                filled(pool, ("c7", "c7", "p7", "p7", "p15")[t])
                pool.dma_start(at(O_H + t * D, (1, D), pn=R), x[t * 128:t * 128 + R, :]).then_inc(ld["x"], 16)
            pool.wait_ge(gate_used, 16)
            pool.dma_start(at(M_G2, (1, 2048)), bass.AP(rows.tensor, rows.offset, [[0, P], [1, 2048]])).then_inc(ld["rows"], 16)
            pool.dma_start(at(M_WR, (1, 324)), wr).then_inc(ld["wr"], 16)
            pool.dma_start(at(R_TRI, (1, N_CONST - 128)), const[:, 128:N_CONST]).then_inc(ld["rows"], 16)
            pool.wait_ge(ld["rows"], 32)
            c = Chain(pool, pool_step)
            c.do(nc.gpsimd.tensor_copy(at(M_IDX, (1, BLK), pn=RB).bitcast(U32), at(R_NOROW, (1, BLK), pn=RB)))
            c.settle()
            pool.dma_start(tab_d[:, :].rearrange("(p b) o -> p (b o)", b=BLK), at(M_IDX, (1, BLK), pn=RB).bitcast(U32))\
                .then_inc(tab_set, 16)
            filled(pool, f"w3{TT - 1}")
            nc.gpsimd.memset(at(M_XG, (1, 2048)), 0.0).then_inc(xg_clear, 1)
            pool.wait_ge(xg_clear, 1)
            nc.gpsimd.memset(at(M_HID, (1, 512), p0=RB, pn=P - RB), 0.0).then_inc(xg_clear, 1)
            for t in range(TT):
                R = ROWS[t]
                pool.wait_ge(x2_ready, t + 1)
                pool.dma_start(x2_d[t * 128:t * 128 + R, :], at(M_X2 + (t % 2) * 1024, (1, D), pn=R)).then_inc(x2_out[t % 2], 16)
            pool.wait_ge(slot_ready, 1)
            pool.wait_ge(tab_set, 16)
            for k in range(2):
                for t in range(TT):
                    R = ROWS[t]
                    pool.indirect_dma_start(
                        out=tab_d[:, :], out_offset=bass.IndirectOffsetOnAxis(at(R_SL + k * TT + t, (1, 1), pn=R).bitcast(U32), 0),
                        in_=at(R_PI + k * TT + t, (1, 1), pn=R).bitcast(U32), in_offset=None).then_inc(scat, 16)
            pool.wait_ge(scat, 160)
            pool.dma_start(at(M_IDX, (1, BLK), pn=RB).bitcast(U32), tab_d[:, :].rearrange("(p b) o -> p (b o)", b=BLK))\
                .then_inc(ld["tb"], 16)
            pool.wait_ge(idx_ready, 2)
            pool.wait_ge(x2_out[0], 48)
            pool.wait_ge(x2_out[1], 32)
            pool.wait_ge(xg_clear, 2)

            def gather(r, k):
                i = 4 * r + k
                wait_pos(pool, xt_ps, r, k, -1)
                pool.indirect_dma_start(
                    out=at(M_XG + (k % 2) * 1024, (1, D), pn=RB), out_offset=None, in_=x2_d[:, :],
                    in_offset=bass.IndirectOffsetOnAxis(at(M_IDX + 128 + i, (1, 1), pn=RB).bitcast(U32), 0),
                    bounds_check=T - 1, oob_is_err=False).then_inc(xg_ready[k % 2], 16)

            def low_down(r, k):
                wait_pos(pool, d_hi, r, k, 1)
                wait_pos(pool, y_ps, r, k, 0)
                o = (k % 2) * 2048
                nc.gpsimd.tensor_tensor(r32(E_DL, 2048), at(E_D + o, (1, 2048)), r32(E_DH + o, 2048).bitcast(F32),
                                        ALU.subtract).then_inc(d_lo, 1)

            def scatter(r, k):
                i = 4 * r + k
                wait_pos(pool, y_copied, r, k, 1)
                pool.indirect_dma_start(
                    out=y_d[:, :], out_offset=bass.IndirectOffsetOnAxis(at(M_IDX + i, (1, 1), pn=RB).bitcast(U32), 0),
                    in_=at(M_YO + (k % 2) * 1024, (1, D), pn=RB), in_offset=None,
                    bounds_check=PAIRS - 1, oob_is_err=False).then_inc(y_sent[k % 2], 16)

            def blocks(i0, i1):
                gather(i0 // 4, 0)
                gather(i0 // 4, 1)
                for i in range(i0, i1):
                    if i + 2 < i1:
                        gather((i + 2) // 4, (i + 2) % 4)
                    low_down(i // 4, i % 4)
                    if i > i0:
                        scatter((i - 1) // 4, (i - 1) % 4)
                scatter(i1 // 4 - 1, 3)
                for s in range(2):
                    pool.wait_ge(y_sent[s], 16 * (i1 // 2))

            blocks(0, NE)
            with pool.If(overflow(pool) > 0):
                blocks(NE, BLK)
            for t in range(TT):
                R = ROWS[t]
                for k in range(2):
                    pool.dma_start(at(A_WG + t * 2048 + k * D, (1, D), pn=R),
                                   y_d[k * T + t * 128:k * T + t * 128 + R, :]).then_inc(y_ld[t], 16)
            for t in range(TT):
                R = ROWS[t]
                pool.wait_ge(y_done, t + 1)
                store(out_y[t * 128:t * 128 + R, :], at(O_H + t * D, (1, D), pn=R))
            pool.wait_ge(out_st, 16 * stores[0])


def columns_block(w, cols):
    w = w[:, cols]
    return w.reshape(-1, P, w.shape[1]).transpose(1, 0, 2).reshape(P, -1)


def kernel(**inputs):
    import numpy as np
    import concourse.bacc as bacc
    from concourse.bass_utils import run_bass_kernel_spmd

    a = {k: np.asarray(v) for k, v in inputs.items()}
    f32 = np.float32
    cat, tile = np.concatenate, np.tile

    def dup(v):
        return cat([v.T, v.T])

    heads = np.arange(512).reshape(8, 64)
    qcols = cat([heads[[m, m + 4]].reshape(-1) for m in range(4)])
    small = cat([
        dup(a["lam_re"][0]), dup(a["lam_im"][0]), tile(a["log_dt"][0], (P, 1)),
        a["norm1_g"][0].reshape(KT, P).T, a["mem_norm_g"][0].reshape(KT, P).T, a["b_glu"][0].reshape(4, P).T,
        tile(a["d_skip"][0].reshape(G, CH).T, (8, 1)), tile(a["sinks"][0], (P, 1)),
        tile(np.repeat(a["sinks"][0].reshape(2, 4).T, NQ, axis=0), (4, 1))], axis=1)
    bm_re, bm_im = (a[n][0].transpose(1, 0, 2).reshape(ST, -1) for n in ("bm_re", "bm_im"))
    cm_re, cm_im = (a[n][0].transpose(2, 0, 1).reshape(ST, -1) for n in ("cm_re", "cm_im"))
    ssm = cat([cat([m, m]) for m in (bm_re, bm_im, cm_re, cm_im)], axis=1)
    s_re, s_im = (a[n][0].transpose(2, 0, 1).reshape(ST, -1) for n in ("state_ssm_re", "state_ssm_im"))
    h0 = np.stack([cat([s_re, s_im]), cat([s_im, s_re])], axis=1)
    x = cat([a["x_prompt"][0], a["x_sample"].reshape(-1, D)])
    xT = x.reshape(T, KT, P).transpose(2, 1, 0).reshape(P, -1)
    memT = a["mem_prompt"][0].reshape(MEM, KT, P).transpose(2, 1, 0).reshape(P, -1)

    w_in, w_kv = a["w_in"][0], a["w_mem_kv"][0]
    at = np.cumsum([0, 512, 512, 256, 512])
    ar = np.arange
    blocks = [columns_block(w_in, ar(256 * i, 256 * i + 256)) for i in range(2)]
    blocks += [columns_block(w_in, ar(at[2], at[3]))]
    blocks += [columns_block(w_in, at[1] + qcols[256 * i:256 * i + 256]) for i in range(2)]
    gates = at[4]
    blocks += [columns_block(w_in, ar(gates + 256 * i, gates + 256 * i + 256)) for i in range(4)]
    blocks += [columns_block(w_in, ar(at[3] + 256 * i, at[3] + 256 * i + 256)) for i in range(2)]
    gate_blocks = [columns_block(w_in, ar(gates + D + 256 * i, gates + D + 256 * i + 256)) for i in range(8)]
    blocks += gate_blocks[:EARLY // 2]
    blocks += [columns_block(w_kv, ar(256 * i, 256 * i + 256)) for i in range(4)]
    blocks += [columns_block(a["w_glu"][0], ar(512))]

    def products(w, i):
        return cat([columns_block(w, ar(128 * d, 128 * d + 128)) for d in range(4 * i, 4 * i + 4)], axis=1)

    branch = [a["w_br_swa"][0][qcols], a["w_br_mem"][0]]
    for kind, i in BRANCH_BLOCKS:
        blocks += [gate_blocks[i] if kind == "g" else products(a["w_br_ssm"][0], i) if kind == "c"
                   else products(branch[i // 2], i % 2)]
    blocks += [columns_block(a["w_out"][0], ar(256 * i, 256 * i + 256)) for i in range(4)]
    wstream = np.stack(blocks)
    gu = cat([a["w_e_gate"][0], a["w_e_up"][0]], axis=2).reshape(NE, KT, P, 2 * DE).transpose(0, 2, 1, 3).reshape(NE, P, -1)
    dn = a["w_e_down"][0].reshape(NE, 2, P, D).transpose(0, 2, 1, 3).reshape(NE, P, -1)
    wexp = cat([gu, dn], axis=2)

    n = ar(P)
    far = 16 + (np.log(np.maximum(n, 1).astype(f32) / f32(16)) / f32(np.log(8.0)) * f32(16)).astype(np.int32)
    bucket = np.where(n < 16, n, np.minimum(far, 31))
    table = cat([a["rel_table"], np.full((1, 8), -1e30, f32)])

    def biases(rows, keys):
        dist = rows[:, None] + P - keys[None, :]
        return table[np.where((dist >= 0) & (dist < P), bucket[np.clip(dist, 0, P - 1)], 32)]

    bias = biases(ar(P), ar(256)).transpose(0, 2, 1).reshape(P, -1)
    sb_ = biases(ar(NQ), ar(136)).transpose(0, 2, 1).reshape(NQ, 2, 4, 136)
    sbias = tile(sb_.transpose(2, 0, 1, 3).reshape(32, -1), (4, 1))

    ck, cv = (a[m][0].reshape(NB, P, P) for m in ("cache_swa_k", "cache_swa_v"))
    skT = ck.transpose(2, 0, 1)
    sv = cv.transpose(1, 0, 2).reshape(P, -1)
    mkT = a["cache_mem_k"][0].transpose(0, 3, 2, 1).reshape(NB, P, -1)
    mv = a["cache_mem_v"][0].reshape(NB, 2, P, 512).transpose(0, 2, 1, 3).reshape(NB, P, -1)
    pid = cat([k * T + t * 128 + ar(P)[:, None] for k in range(2) for t in range(TT)], axis=1)
    const = cat([np.eye(P), np.triu(np.ones((P, P)), 1), tile(ar(32), (P, 1)), pid, np.full((P, BLK), NOROW)], axis=1)
    rows = cat([a["norm2_g"][0], a["final_norm_g"]])[None]
    wr = cat([a["w_rg"][0], a["w_rexp"][0]], axis=1)
    wr = cat([columns_block(wr, ar(36)), tile(cat([a["b_rg"][0], a["b_rexp"][0]]), (P, 1))], axis=1)

    ins = dict(small=small, ssm=ssm, h0=h0, xT=xT, x=x, memT=memT, wstream=wstream, wexp=wexp, bias=bias, sbias=sbias,
               skT=skT, sv=sv, mkT=mkT, mv=mv, cache_k=ck, cache_v=cv, const=const.astype(f32), rows=rows, wr=wr)
    outs = dict(out_y=(T, D), out_kvp=(P, 256), out_mem=(MEM, 1024), out_sk=(NB, P, P), out_sv=(NB, P, P),
                out_ssm=(P, 9 * G))
    nc = bacc.Bacc("TRN2", target_bir_lowering=False, num_devices=1)
    arrays, args = {}, {}
    for k, v in ins.items():
        arrays["in_" + k] = np.ascontiguousarray(v)
        args[k] = nc.dram_tensor("in_" + k, v.shape, F32, kind="ExternalInput").ap()
    for k, shape in outs.items():
        args[k] = nc.dram_tensor(k, shape, F32, kind="ExternalOutput").ap()
    build(nc, **args)
    r = run_bass_kernel_spmd(nc, [arrays], core_ids=[0]).results[0]
    y, kvp, mem, ssm_o = r["out_y"], r["out_kvp"], r["out_mem"], r["out_ssm"].reshape(2, ST, 9, G)
    st = ssm_o.transpose(0, 2, 3, 1)
    return (y[:NP_].reshape(1, NP_, D), y[NP_:].reshape(NB, NQ, D),
            kvp[:, :P].reshape(1, 1, P, 2, 64), kvp[:, P:].reshape(1, 1, P, 2, 64),
            st[0, 0][None, None], st[1, 0][None, None],
            mem[:, :512].reshape(1, 1, MEM, MH, 128), mem[:, 512:].reshape(1, 1, MEM, MH, 128),
            r["out_sk"].reshape(1, NB, P, 2, 64), r["out_sv"].reshape(1, NB, P, 2, 64),
            st[0, 1:][None], st[1, 1:][None])
```
